# Optimizing a Trainium2 kernel written in Bass

```python
import math
import jax
import jax.numpy as jnp
from jax import lax
import numpy as np

D_MODEL = 1024
BATCH = 1
SEQ = 512
DEPTH = 1
DEC_BATCH = 8
DEC_SEQ = 4
PAST_LEN = 1024
PAGE_SIZE = 128

DA_HEADS = 8
DA_HEAD_DIM = 64
DA_V_DIM = 2 * DA_HEAD_DIM
DA_WIDTH = DA_HEADS * DA_V_DIM
RET_HEADS = 4
RET_K_DIM = 128
RET_V_DIM = 256
RET_QK_WIDTH = RET_HEADS * RET_K_DIM
RET_WIDTH = RET_HEADS * RET_V_DIM
D_FF = 2816
Q_BLOCK = 128
RET_CHUNK = 128
LN_EPS = 1e-5
ALPHA = (2.0 * DEPTH) ** 0.25
BETA = (8.0 * DEPTH) ** -0.25
IN_SPLITS = (DA_WIDTH, DA_WIDTH, DA_WIDTH, RET_QK_WIDTH, RET_QK_WIDTH, RET_WIDTH, RET_WIDTH, D_MODEL, D_MODEL)
IN_WIDTH = sum(IN_SPLITS)
IN_OFFSETS = [int(o) for o in np.cumsum(IN_SPLITS)[:-1]]

kernel_name = "hybrid_diffattn_retention_macaron_step"

def lambda_init(layer):
    return 0.8 - 0.6 * math.exp(-0.3 * layer)

def alibi_slopes():
    return jnp.asarray((2.0 ** (-8.0 * np.arange(1, DA_HEADS + 1) / DA_HEADS)).astype(np.float32))

def retention_log_decay():
    return jnp.asarray(np.log(1.0 - 2.0 ** (-5.0 - np.arange(RET_HEADS))).astype(np.float32))

def layer_norm(x, g, b):
    x32 = x.astype(jnp.float32)
    mu = x32.mean(-1, keepdims=True)
    var = jnp.square(x32 - mu).mean(-1, keepdims=True)
    return ((x32 - mu) * lax.rsqrt(var + LN_EPS) * g + b).astype(x.dtype)

def rms_norm(x):
    x32 = x.astype(jnp.float32)
    return x32 * lax.rsqrt(jnp.mean(jnp.square(x32), axis=-1, keepdims=True) + LN_EPS)

def swiglu(x, w_gu, w_down):
    a, u = jnp.split(x @ w_gu, 2, axis=-1)
    return (jax.nn.silu(a) * u) @ w_down

def ffn_sublayer(x, w_gu, w_down, g, b):
    return layer_norm(ALPHA * x + 0.5 * swiglu(x, w_gu, w_down), g, b)

def split_inputs(x, w_in):
    B, T = x.shape[:2]
    qa, ka, va, qr, kr, vr, gr, ga, gb = jnp.split(x @ w_in, IN_OFFSETS, axis=-1)
    qa = qa.reshape(B, T, DA_HEADS, 2, DA_HEAD_DIM)
    ka = ka.reshape(B, T, DA_HEADS, 2 * DA_HEAD_DIM)
    va = va.reshape(B, T, DA_HEADS, DA_V_DIM)
    qr = qr.reshape(B, T, RET_HEADS, RET_K_DIM)
    kr = kr.reshape(B, T, RET_HEADS, RET_K_DIM) * (RET_K_DIM ** -0.5)
    vr = vr.reshape(B, T, RET_HEADS, RET_V_DIM)
    return qa, ka, va, qr, kr, vr, gr, ga, gb

def diff_lambda(lp, lam_init):
    lp = lp.astype(jnp.float32)
    return jnp.exp(jnp.sum(lp[0] * lp[1])) - jnp.exp(jnp.sum(lp[2] * lp[3])) + lam_init

def diff_attention(q, k, v, q_pos, k_pos, lam):
    B, Tk = k.shape[:2]
    k = k.reshape(B, Tk, DA_HEADS, 2, DA_HEAD_DIM)
    s = jnp.einsum('bqhmd,bkhmd->bhmqk', q, k, preferred_element_type=jnp.float32) * (DA_HEAD_DIM ** -0.5)
    dist = jnp.abs(q_pos[:, None] - k_pos[None, :]).astype(jnp.float32)
    bias = -alibi_slopes()[:, None, None] * dist
    causal = k_pos[None, :] <= q_pos[:, None]
    s = jnp.where(causal, s + bias[:, None], -jnp.inf)
    p = jax.nn.softmax(s, axis=-1)
    a = p[:, :, 0] - lam * p[:, :, 1]
    return jnp.einsum('bhqk,bkhd->bqhd', a, v)

def diff_attention_prompt(q, k, v, lam):
    B, S = q.shape[:2]
    nqb = S // Q_BLOCK
    qb = q.reshape(B, nqb, Q_BLOCK, DA_HEADS, 2, DA_HEAD_DIM).swapaxes(0, 1)
    pos = jnp.arange(S)
    qpos = pos.reshape(nqb, Q_BLOCK)
    out = lax.map(lambda a: diff_attention(a[0], k, v, a[1], pos, lam), (qb, qpos))
    return out.swapaxes(0, 1).reshape(B, S, DA_HEADS, DA_V_DIM)

def diff_post(o, subln_g, lam_init):
    B, T = o.shape[:2]
    return (rms_norm(o) * subln_g * (1.0 - lam_init)).reshape(B, T, DA_WIDTH)

def retention_chunk(state, q, k, v):
    log_g = retention_log_decay()
    q, k, v, state = (t.astype(jnp.float32) for t in (q, k, v, state))
    C = q.shape[1]
    idx = jnp.arange(C, dtype=jnp.float32)
    diff = idx[:, None] - idx[None, :]
    decay = jnp.where(diff >= 0, jnp.exp(jnp.maximum(diff, 0.0)[None] * log_g[:, None, None]), 0.0)
    scores = jnp.einsum('bihd,bjhd->bhij', q, k) * decay
    cross_decay = jnp.exp((idx + 1.0)[:, None] * log_g[None, :])[None, :, :, None]
    o = jnp.einsum('bhij,bjhe->bihe', scores, v) + jnp.einsum('bihd,bhde->bihe', q, state) * cross_decay
    k_w = k * jnp.exp((C - 1.0 - idx)[:, None] * log_g[None, :])[None, :, :, None]
    new_state = jnp.exp(C * log_g)[None, :, None, None] * state + jnp.einsum('bjhd,bjhe->bhde', k_w, v)
    return new_state, o

def retention_prompt(q, k, v):
    B, S = q.shape[:2]
    nc = S // RET_CHUNK
    to_chunks = lambda t: t.astype(jnp.float32).reshape(B, nc, RET_CHUNK, *t.shape[2:]).swapaxes(0, 1)
    s0 = jnp.zeros((B, RET_HEADS, RET_K_DIM, RET_V_DIM), jnp.float32)
    s_fin, o = lax.scan(lambda st, c: retention_chunk(st, *c), s0, (to_chunks(q), to_chunks(k), to_chunks(v)))
    return o.swapaxes(0, 1).reshape(B, S, RET_HEADS, RET_V_DIM), s_fin

def ret_post(o, gr):
    B, T = o.shape[:2]
    return rms_norm(o).reshape(B, T, RET_WIDTH) * jax.nn.silu(gr.astype(jnp.float32))

def merge_sublayer(x, oa, ob, ga, gb, w_pa, w_pb, w_o, g, b):
    m = jax.nn.sigmoid(ga) * (oa @ w_pa) + jax.nn.sigmoid(gb) * (ob @ w_pb)
    return layer_norm(ALPHA * x + m @ w_o, g, b)

def setup_inputs(seed: int = 0) -> dict:
    key = jax.random.key(seed)
    ks = jax.random.split(key, 20)
    n_pages = PAST_LEN // PAGE_SIZE
    n_phys = (DEC_BATCH * n_pages * 5) // 4
    nrm = lambda k, shape, scale: jax.random.normal(k, shape, jnp.float32) * scale
    col_scale = np.ones((IN_WIDTH,), np.float32)
    col_scale[IN_OFFSETS[1]:IN_OFFSETS[2]] = BETA
    col_scale[IN_OFFSETS[4]:IN_OFFSETS[5]] = BETA
    page_table = jax.random.permutation(ks[5], n_phys)[: DEC_BATCH * n_pages].reshape(DEC_BATCH, n_pages).astype(jnp.int32)
    return {
        "x_prompt": nrm(ks[0], (BATCH, SEQ, D_MODEL), 1.0),
        "x_sample": nrm(ks[1], (DEC_BATCH, DEC_SEQ, D_MODEL), 1.0),
        "cache_k": nrm(ks[2], (DEPTH, n_phys, PAGE_SIZE, DA_HEADS, 2 * DA_HEAD_DIM), 1.0),
        "cache_v": nrm(ks[3], (DEPTH, n_phys, PAGE_SIZE, DA_HEADS, DA_V_DIM), BETA),
        "state_ret": nrm(ks[4], (DEPTH, DEC_BATCH, RET_HEADS, RET_K_DIM, RET_V_DIM), 1.0),
        "page_table": page_table,
        "ln_g": 1.0 + nrm(ks[6], (DEPTH, 3, D_MODEL), 0.02),
        "ln_b": nrm(ks[7], (DEPTH, 3, D_MODEL), 0.02),
        "ffn1_w_gu": nrm(ks[8], (DEPTH, D_MODEL, 2 * D_FF), BETA * D_MODEL ** -0.5),
        "ffn1_w_down": nrm(ks[9], (DEPTH, D_FF, D_MODEL), BETA * D_FF ** -0.5),
        "w_in": nrm(ks[10], (DEPTH, D_MODEL, IN_WIDTH), D_MODEL ** -0.5) * jnp.asarray(col_scale),
        "da_lambda": nrm(ks[11], (DEPTH, 4, DA_HEAD_DIM), 0.1),
        "da_subln_g": 1.0 + nrm(ks[12], (DEPTH, DA_V_DIM), 0.02),
        "w_branch_a": nrm(ks[13], (DEPTH, DA_WIDTH, D_MODEL), DA_WIDTH ** -0.5),
        "w_branch_b": nrm(ks[14], (DEPTH, RET_WIDTH, D_MODEL), RET_WIDTH ** -0.5),
        "w_out": nrm(ks[15], (DEPTH, D_MODEL, D_MODEL), BETA * D_MODEL ** -0.5),
        "ffn2_w_gu": nrm(ks[16], (DEPTH, D_MODEL, 2 * D_FF), BETA * D_MODEL ** -0.5),
        "ffn2_w_down": nrm(ks[17], (DEPTH, D_FF, D_MODEL), BETA * D_FF ** -0.5),
    }

def reference(x_prompt, x_sample, cache_k, cache_v, state_ret, page_table, ln_g, ln_b, ffn1_w_gu, ffn1_w_down,
              w_in, da_lambda, da_subln_g, w_branch_a, w_branch_b, w_out, ffn2_w_gu, ffn2_w_down):
    xp, xs = x_prompt, x_sample
    n_dec, t_dec = xs.shape[:2]
    q_pos_s = PAST_LEN + jnp.arange(t_dec)
    k_pos_s = jnp.arange(PAST_LEN + t_dec)
    kp_l, vp_l, sp_l, ks_l, vs_l, ss_l = [], [], [], [], [], []
    for l in range(DEPTH):
        lam_init = lambda_init(l)
        lam = diff_lambda(da_lambda[l], lam_init)
        xp = ffn_sublayer(xp, ffn1_w_gu[l], ffn1_w_down[l], ln_g[l, 0], ln_b[l, 0])
        qa, ka, va, qr, kr, vr, gr, ga, gb = split_inputs(xp, w_in[l])
        oa = diff_post(diff_attention_prompt(qa, ka, va, lam), da_subln_g[l], lam_init)
        o_r, s_fin = retention_prompt(qr, kr, vr)
        ob = ret_post(o_r, gr)
        xp = merge_sublayer(xp, oa, ob, ga, gb, w_branch_a[l], w_branch_b[l], w_out[l], ln_g[l, 1], ln_b[l, 1])
        xp = ffn_sublayer(xp, ffn2_w_gu[l], ffn2_w_down[l], ln_g[l, 2], ln_b[l, 2])
        kp_l.append(ka)
        vp_l.append(va)
        sp_l.append(s_fin)
        xs = ffn_sublayer(xs, ffn1_w_gu[l], ffn1_w_down[l], ln_g[l, 0], ln_b[l, 0])
        qa, ka, va, qr, kr, vr, gr, ga, gb = split_inputs(xs, w_in[l])
        k_past = cache_k[l][page_table].reshape(n_dec, PAST_LEN, DA_HEADS, 2 * DA_HEAD_DIM)
        v_past = cache_v[l][page_table].reshape(n_dec, PAST_LEN, DA_HEADS, DA_V_DIM)
        k_all = jnp.concatenate([k_past, ka.astype(k_past.dtype)], axis=1)
        v_all = jnp.concatenate([v_past, va.astype(v_past.dtype)], axis=1)
        oa = diff_post(diff_attention(qa, k_all, v_all, q_pos_s, k_pos_s, lam), da_subln_g[l], lam_init)
        s_new, o_r = retention_chunk(state_ret[l], qr, kr, vr)
        ob = ret_post(o_r, gr)
        xs = merge_sublayer(xs, oa, ob, ga, gb, w_branch_a[l], w_branch_b[l], w_out[l], ln_g[l, 1], ln_b[l, 1])
        xs = ffn_sublayer(xs, ffn2_w_gu[l], ffn2_w_down[l], ln_g[l, 2], ln_b[l, 2])
        ks_l.append(ka)
        vs_l.append(va)
        ss_l.append(s_new)
    k_prompt = jnp.stack(kp_l)
    v_prompt = jnp.stack(vp_l)
    ret_state_prompt = jnp.stack(sp_l)
    k_sample = jnp.stack(ks_l)
    v_sample = jnp.stack(vs_l)
    ret_state_sample = jnp.stack(ss_l)
    return (xp, xs, k_prompt, v_prompt, ret_state_prompt, k_sample, v_sample, ret_state_sample)


_drawn_inputs = setup_inputs


def setup_inputs(seed=0):
    import zlib

    import numpy as np

    out = dict(_drawn_inputs(seed))
    spreads = {}
    factors = {}
    for name, (base, spread) in spreads.items():
        noise = np.random.default_rng([zlib.crc32(name.encode()), seed]).standard_normal(out[name].shape)
        drawn = base * np.exp(spread * noise) if base else spread * noise
        out[name] = jnp.asarray(drawn.astype(out[name].dtype))
    for name, factor in factors.items():
        out[name] = (out[name] * factor).astype(out[name].dtype)
    return out
```

```python
from contextlib import ExitStack

import numpy as np

import concourse.bass as bass
from concourse import mybir

F32 = mybir.dt.float32
F32R = mybir.dt.float32r
I32 = mybir.dt.int32
ALU = mybir.AluOpType
ACT = mybir.ActivationFunctionType
AX_X = mybir.AxisListType.X
RMAX = bass.bass_isa.ReduceOp.max

P = 128
D = 1024
KD = D // P
SEQ = 512
NB = SEQ // P
DEC, TDEC = 8, 4
NS = DEC * TDEC
T = SEQ + NS
HALF = T // 2
FF = 2816
KF = FF // P
PAST, PAGE = 1024, 128
PAGES = PAST // PAGE
HA, DH, DV = 8, 64, 128
HR, RK, RV = 4, 128, 256
ALPHA = 2.0 ** 0.25
EPS = 1e-5
LAM_INIT = 0.2
MASKED = -1e30
W_IN_COLS = dict(qa=0, ka=1024, va=2048, qr=3072, kr=3584, vr=4096, gr=5120, ga=6144, gb=7168)
TOKENS = [(P * j, P) for j in range(NB)] + [(SEQ, NS)]

FFN_UP, FFN_DOWN = KF, 12
C_FFN1_UP = 0
C_FFN1_DOWN = C_FFN1_UP + FFN_UP
C_KA = C_FFN1_DOWN + FFN_DOWN
C_VA = C_KA + 4
C_QA = C_VA + 4
C_BRANCH_A = C_QA + 4
C_QR = C_BRANCH_A + 8
C_KR = C_QR + 2
C_VR = C_KR + 2
C_GR = C_VR + 4
C_BRANCH_B = C_GR + 4
C_OUT = C_BRANCH_B + 8
C_FFN2_UP = C_OUT + 4
C_FFN2_DOWN = C_FFN2_UP + FFN_UP
C_END = C_FFN2_DOWN + FFN_DOWN


def constants():
    p = np.arange(P)
    slopes = 2.0 ** -(1.0 + np.arange(HA))
    gamma = 1.0 - 2.0 ** (-5.0 - np.arange(HR))
    t = {}
    t["ident"] = np.eye(P)
    t["ones"] = np.ones((P, P))
    u = np.arange(SEQ)[None, :] - (SEQ - P) - p[:, None]
    t["dist"] = np.where(u <= 0, u, MASKED)
    t["slope8"] = np.broadcast_to(8.0 * slopes, (P, HA))
    t["map_rows"] = np.stack([p < DH, p >= DH], 1)
    g, h, m, q = np.meshgrid(np.arange(PAGES), np.arange(HA), np.arange(2), np.arange(TDEC), indexing="ij")
    t["bias_past"] = (slopes[h] * (PAGE * g + p[:, None, None, None, None] - PAST - q)).reshape(P, -1)
    b, h, m, q = np.meshgrid(np.arange(DEC), np.arange(HA), np.arange(2), np.arange(TDEC), indexing="ij")
    d = p[:, None, None, None, None] - TDEC * b
    t["bias_new"] = np.where((d >= 0) & (d <= q), slopes[h] * (d - q), MASKED).reshape(P, -1)
    i = np.arange(P)
    dd = i[None, None, :] - p[:, None, None]
    t["decay"] = np.where(dd >= 0, gamma[None, :, None] ** np.maximum(dd, 0), 0.0).reshape(P, -1)
    t["cross"] = np.broadcast_to(gamma[:, None] ** (i[None, :] + 1.0), (P, HR, P)).reshape(P, -1)
    t["kdec"] = gamma[None, :] ** (P - 1.0 - p[:, None])
    js = np.arange(NS)
    same = (p[:, None, None] // TDEC == js[None, None, :] // TDEC) & (js[None, None, :] >= p[:, None, None])
    ds = np.maximum(js[None, None, :] - p[:, None, None], 0)
    t["decay_s"] = np.where(same, gamma[None, :, None] ** ds, 0.0).reshape(P, -1)
    own = p[:, None, None] // TDEC == np.arange(DEC)[None, :, None]
    t["kdec_s"] = np.where(own, gamma[None, None, :] ** (TDEC - 1.0 - (p[:, None, None] % TDEC)), 0.0).reshape(P, -1)
    at, parts = {}, []
    n = 0
    for name, a in t.items():
        a = np.asarray(a, np.float32).reshape(P, -1)
        at[name] = (n, a.shape[1])
        n += a.shape[1]
        parts.append(a)
    return at, np.ascontiguousarray(np.concatenate(parts, 1), np.float32)


def build(nc, x_prompt, x_sample, cache_k, cache_v, state_ret, page_table, ln_g, ln_b, ffn1_w_gu,
          ffn1_w_down, w_in, da_lambda, da_subln_g, w_branch_a, w_branch_b, w_out, ffn2_w_gu,
          ffn2_w_down, const, y_prompt, y_sample, k_prompt, v_prompt, ret_state_prompt, k_sample,
          v_sample, ret_state_sample):
    const_at, _ = constants()
    gamma = [1.0 - 2.0 ** (-5.0 - h) for h in range(HR)]

    with ExitStack() as ctx:
        base = 16512

        def at(name, offset, shape, dt=F32):
            return nc.alloc_sbuf_tensor_at(name, [P, *shape], dt, offset=base + offset)

        def sem(name):
            return ctx.enter_context(nc.semaphore(name))

        ps = ctx.enter_context(nc.psum_tensor("ps", [P, 8, 512], F32))

        w_raw = at("w_raw", 0, [2, KD, 256])
        w_hi_t = at("w_hi_t", 16384, [2, KD, 256], F32R)
        w_lo_t = at("w_lo_t", 32768, [2, KD, 256], F32R)
        xT = at("xT", 49152, [KD, T])
        xh = at("xh", 66560, [KD, T], F32R)
        xl = at("xl", 83968, [KD, T], F32R)
        A = 101376
        hh = at("hh", A, [KF, T], F32R)
        hl = at("hl", A + 47872, [KF, T], F32R)
        xn = at("xn", A, [5, D])
        qaT = at("qaT", A, [HA, T])
        kaT = at("kaT", A + 17408, [HA, T])
        v_nat = at("v_nat", A + 34816, [NB, D])
        v_nat_s = at("v_nat_s", A + 51200, [D])
        k_nat = at("k_nat", A + 55296, [NB, D])
        k_nat_s = at("k_nat_s", A + 71680, [D])
        o_nat = at("o_nat", A + 55296, [NB, D])
        s_sb = at("s_sb", A + 71680, [2, 2, 512])
        p_sb = at("p_sb", A + 79872, [2, 2, 512])
        turned = at("turned", A + 79872, [2, T])
        a_sb = at("a_sb", A + 88064, [2, 512])
        aT = at("aT", A + 92160, [2, 512])
        oaT = at("oaT", A, [KD, T])
        oah = at("oah", A + 17408, [KD, T], F32R)
        oal = at("oal", A + 34816, [KD, T], F32R)
        k_page = at("k_page", 66560, [4, D])
        v_page = at("v_page", 83968, [4, D])
        kT = at("kT", A + 88064, [2, D])
        ds_sb = at("ds_sb", A + 71680, [512])
        dec_o = at("dec_o", A + 73728, [2, 256])
        dec_l = at("dec_l", A + 75776, [2, 256])
        dp_sb = at("dp_sb", A + 77824, [512])
        sq = at("sq", A + 79872, [2, D])
        mT = at("mT", A, [KD, T])
        mh = at("mh", A + 52224, [KD, T], F32R)
        ml = at("ml", A + 69632, [KD, T], F32R)
        R = A + 17408
        qrT = at("qrT", R, [HR, T])
        krT = at("krT", R + 8704, [HR, T])
        vr_nat = at("vr_nat", R + 17408, [NB, D])
        vr_nat_s = at("vr_nat_s", R + 33792, [D])
        kr_nat = at("kr_nat", R + 37888, [NB, HR * RK])
        kr_nat_s = at("kr_nat_s", R + 46080, [HR * RK])
        rturned = at("rturned", R + 48128, [2, T])
        state = at("state", R + 52480, [2, D])
        or_s = at("or_s", R + 58368, [D])
        or_nat = at("or_nat", R + 62464, [NB, D])
        rsq = at("rsq", R, [2, D])
        st_in = at("st_in", R + 17408, [2, D])
        st_out = at("st_out", R + 25600, [2, D])
        kw_s = at("kw_s", R + 37888, [2, HR * RK])
        onT = at("onT", A + 52224, [KD, T])
        obh = at("obh", A + 17408, [KD, T], F32R)
        obl = at("obl", A + 34816, [KD, T], F32R)
        C = A + 96256
        ident = at("ident", C, [P])
        ones = at("ones", C + 512, [P])
        M = C + 1024
        gated = at("gated", M, [2, T])
        prod = at("prod", M + 4352, [2, T])
        ln_gain = at("ln_gain", M, [D])
        ln_bias = at("ln_bias", M + 4096, [D])
        bias8 = at("bias8", M, [2, 512])
        q_stage = at("q_stage", M + 4096, [2, 2, P])
        q_bd = at("q_bd", M + 6144, [DEC, HA, 8])
        bias_past = at("bias_past", M, [512])
        decay = at("decay", M, [HR, P])
        cross = at("cross", M + 2048, [HR, P])
        scT = at("scT", M + 4096, [2, HR * P])
        decay_s = at("decay_s", M + 8192, [HR, NS])
        s_new = at("s_new", C + 9728, [DEC, HA * 8])
        dist = at("dist", C + 11776, [512])
        dmax = at("dmax", C + 11776, [64])
        dmax_all = at("dmax_all", C + 12032, [64])
        dpsum = at("dpsum", C + 12288, [64])
        lam_in = at("lam_in", C + 9728, [4, DH])
        qm = at("qm", C + 9728, [DEC, HR, NS])
        qx = at("qx", C + 9728, [2, HR, P])      
        small = at("small", C + 13824, [240])
        pages = at("pages", C + 14784, [DEC * PAGES], I32)
        col = {}
        used = [0]

        def tiny(name, n):
            a = used[0]
            used[0] += n
            assert used[0] <= 240
            col[name] = small[:, a:a + n]
            return col[name]

        bn = tiny("bn", 60)
        mv = tiny("mv", 10)
        sd = tiny("sd", 5)
        rstd = tiny("rstd", 5)
        slope8 = tiny("slope8", HA)
        lamv = tiny("lamv", 2)
        map_rows = tiny("map_rows", 2)
        lam_t = tiny("lam_t", 4)
        subln = tiny("subln", 1)
        subln8 = tiny("subln8", 1)
        nmax = tiny("nmax", 4)
        rsum = tiny("rsum", 4)
        rr = tiny("rr", 4)
        ss = bn[:, 0:32]
        ssd = tiny("ssd", 32)
        srs = tiny("srs", 32)
        kdec = tiny("kdec", HR)
        kdec_s = tiny("kdec_s", DEC * HR)

        raw_landed = [sem(f"raw_landed{j}") for j in range(2)]
        hi_split = sem("hi_split")
        lo_split = sem("lo_split")
        gemm_done = sem("gemm_done")
        const_landed = sem("const_landed")
        out_stored = sem("out_stored")

        def load_chunk(sp, c, half, j, w, col, row=0, nk=KD):
            sp.wait_ge(lo_split, c + 1)
            src = w[0, row:row + nk * P, :].rearrange("(k p) n -> p k n", p=P)[:, :, bass.ds(col, 256)]
            sp.dma_start(w_raw[:, j, 0:nk], src).then_inc(raw_landed[j], 16)

        def split_hi(act, c, half, j, nk=KD):
            act.wait_ge(raw_landed[j], 16 * half + 16)
            act.wait_ge(gemm_done, 2 * c + 2)
            nc.scalar.copy(w_hi_t[:, j, 0:nk], w_raw[:, j, 0:nk]).then_inc(hi_split, 1)

        def split_lo(dve, c, j, nk=KD):
            dve.wait_ge(hi_split, c + 1)
            nc.vector.tensor_tensor(w_lo_t[:, j, 0:nk], w_raw[:, j, 0:nk], w_hi_t[:, j, 0:nk].bitcast(F32),
                                    ALU.subtract).then_inc(lo_split, 1)

        def chunk_ready(pe, c):
            pe.wait_ge(lo_split, c + 3)

        def gemm(bank, j, n, nk, mh_, ml_, k0=0, start=True, stop=True):
            for k in range(nk):
                w_cols = slice(n * P, n * P + P)
                for pas, (w, m) in enumerate(((w_hi_t, mh_), (w_hi_t, ml_), (w_lo_t, mh_))):
                    for half in range(2):
                        mm = nc.tensor.matmul(ps[:, bank + half, 0:HALF], w[:, j, k, w_cols],
                                              m[:, k0 + k, half * HALF:half * HALF + HALF],
                                              start=start and k == 0 and pas == 0,
                                              stop=stop and k == nk - 1 and pas == 2)
            mm.then_inc(gemm_done, 1)

        def tile_done(eng, c, n):
            eng.wait_ge(gemm_done, 2 * c + n + 5)

        def banks(b):
            return ps[:, b:b + 2, 0:HALF]

        def halves(tile):
            return tile.rearrange("p (a b) -> p a b", b=HALF)

        class FFN:
            def __init__(self, tag, c_up, w_gu, w_down, last=False):
                self.c, self.gu, self.down, self.last = c_up, w_gu, w_down, last
                self.silu_done = sem(f"{tag}_silu_done")
                self.prod_done = sem(f"{tag}_prod_done")
                self.h_hi = sem(f"{tag}_h_hi")
                self.h_lo = sem(f"{tag}_h_lo")
                self.resid = sem(f"{tag}_resid")

            def loads(self, sp):
                c = self.c
                with sp.Fori(0, KF // 2) as i:
                    for j in range(2):
                        load_chunk(sp, c + 2 * i + j, c // 2 + i, j,
                                   self.gu, 256 * i + FF * j)
                c += FFN_UP
                with sp.Fori(0, 2) as q:
                    for m in range(6):
                        r, s = m // 3, m % 3
                        load_chunk(sp, c + 6 * q + m, c // 2 + 3 * q + m // 2, m % 2,
                                   self.down, 512 * q + 256 * r, 8 * s * P, [8, 8, 6][s])

            def pe_part(self, pe, ready):
                ready(pe)
                c = self.c
                with pe.Fori(0, KF // 2) as i:
                    for j in range(2):
                        chunk_ready(pe, c + 2 * i + j)
                        for n in range(2):
                            pe.wait_ge(self.prod_done if j else self.silu_done, 2 * i + n + 1)
                            gemm(4 * j + 2 * n, j, n, KD, xh, xl)
                c += FFN_UP
                pe.wait_ge(self.h_lo, KF)
                with pe.Fori(0, 2) as q:
                    for r in range(2):
                        for s in range(3):
                            m = 3 * r + s
                            chunk_ready(pe, c + 6 * q + m)
                            for n in range(2):
                                if s == 0:
                                    pe.wait_ge(self.resid, 4 * q + 2 * r + n + 1)
                                gemm(4 * r + 2 * n, m % 2, n, [8, 8, 6][s], hh, hl, 8 * s, s == 0, s == 2)

            def act_part(self, act):
                c = self.c
                act.sem_inc(self.silu_done, 2)
                with act.Fori(0, KF // 2) as i:
                    for n in range(2):
                        tile_done(act, c + 2 * i, n)
                        act.wait_ge(self.prod_done, 2 * i + n + 1)
                        nc.scalar.activation(halves(gated[:, n]), banks(2 * n), ACT.Silu).then_inc(self.silu_done, 1)
                    split_hi(act, c + 2 * i + 2, c // 2 + i + 1, 0)
                    for n in range(2):
                        act.wait_ge(self.prod_done, 2 * i + n + 3)
                        nc.scalar.copy(hh[:, bass.ds(2 * i + n, 1)], prod[:, n:n + 1]).then_inc(self.h_hi, 1)
                    split_hi(act, c + 2 * i + 3, c // 2 + i + 1, 1)
                c += FFN_UP
                for q in range(2):
                    for m in range(6):
                        nxt = 6 * q + m + 2
                        if not (self.last and nxt >= FFN_DOWN):
                            split_hi(act, c + nxt, (c + nxt) // 2, m % 2, 6 if m % 3 == 0 else KD)

            def dve_part(self, dve):
                c = self.c
                dve.sem_inc(self.prod_done, 2)
                with dve.Fori(0, KF // 2) as i:
                    split_lo(dve, c + 2 * i + 2, 0)
                    for n in range(2):
                        tile_done(dve, c + 2 * i + 1, n)
                        dve.wait_ge(self.silu_done, 2 * i + n + 3)
                        nc.vector.tensor_tensor(halves(prod[:, n]), banks(4 + 2 * n), halves(gated[:, n]),
                                                ALU.mult).then_inc(self.prod_done, 1)
                        dve.wait_ge(self.h_hi, 2 * i + n + 1)
                        nc.vector.tensor_tensor(hl[:, bass.ds(2 * i + n, 1)], prod[:, n:n + 1],
                                                hh[:, bass.ds(2 * i + n, 1)].bitcast(F32),
                                                ALU.subtract).then_inc(self.h_lo, 1)
                    split_lo(dve, c + 2 * i + 3, 1)
                c += FFN_UP
                dve.sem_inc(self.resid, 4)
                for q in range(2):
                    for m in range(6):
                        nxt = 6 * q + m + 2
                        r, s = m // 3, m % 3
                        if s == 2:
                            for n in range(2):
                                tile_done(dve, c + 6 * q + m, n)
                                k = 4 * q + 2 * r + n
                                nc.vector.scalar_tensor_tensor(halves(xT[:, k]), banks(4 * r + 2 * n), 0.5 / ALPHA,
                                                               halves(xT[:, k]), ALU.mult, ALU.add
                                                               ).then_inc(self.resid, 1)
                        if not (self.last and nxt >= FFN_DOWN):
                            split_lo(dve, c + nxt, m % 2, 6 if s == 0 else KD)

        class Norm:

            params = sem("ln_params")
            rows = sem("ln_rows")
            bn = sem("ln_bn")
            mean = sem("ln_mean")
            var = sem("ln_var")
            sd = sem("ln_sd")
            rs = sem("ln_rs")
            normed = sem("ln_normed")
            gained = sem("ln_gained")
            biased = sem("ln_biased")
            turned = sem("ln_turned")
            x_hi = sem("ln_x_hi")
            x_lo = sem("ln_x_lo")

            def __init__(self, index, stats_before, backs_before, stats=True, back=True):
                self.index, self.stats, self.back = index, stats, back
                self.s, self.b = 5 * stats_before, 5 * backs_before

            def back_ps(self, t):
                b, n = 4 + 2 * (t % 2), TOKENS[t][1]
                return ps[:, b:b + 2, :].rearrange("p a (k c) -> p (a k) c", c=P)[:, :, 0:n]

            def load_params(self, sp):
                for src, dst in ((ln_g, ln_gain), (ln_b, ln_bias)):
                    sp.dma_start(dst[:], src[0, self.index:self.index + 1, :].broadcast_to([P, D])
                                 ).then_inc(self.params, 16)

            def row_ready(self, pe, t):
                pe.wait_ge(self.biased, self.s + t + 1)

            def pe_part(self, pe):
                def to_rows(t):
                    if t >= 2:
                        pe.wait_ge(self.normed, self.s + t - 1)
                    t0, n = TOKENS[t]
                    for k in range(KD):
                        mm = nc.tensor.transpose(ps[0:n, 2 * (t % 2) + k // 4, (k % 4) * P:(k % 4) * P + P],
                                                 xT[:, k, t0:t0 + n], ident[:])
                    mm.then_inc(self.rows, 1)

                def to_channels(t):
                    if t >= 2:
                        pe.wait_ge(self.x_hi, self.b + t - 1)
                    self.row_ready(pe, t)
                    n = TOKENS[t][1]
                    for k in range(KD):
                        mm = nc.tensor.transpose(ps[:, 4 + 2 * (t % 2) + k // 4, (k % 4) * P:(k % 4) * P + n],
                                                 xn[0:n, t, k * P:k * P + P], ident[0:n, 0:n])
                    mm.then_inc(self.turned, 1)

                if self.stats:
                    to_rows(0)
                    to_rows(1)
                for t in range(5):
                    if self.stats and 2 <= t + 1 < 5:
                        to_rows(t + 1)
                    if self.back:
                        to_channels(t)

            def ready(self, eng):
                eng.wait_ge(self.x_lo, self.b + 5)

            def act_part(self, act):
                def sqrt(t):
                    n = TOKENS[t][1]
                    act.wait_ge(self.var, self.s + t + 1)
                    nc.scalar.activation(sd[0:n, t:t + 1], mv[0:n, 2 * t + 1:2 * t + 2], ACT.Sqrt
                                         ).then_inc(self.sd, 1)

                def evict(t):
                    t0, n = TOKENS[t]
                    act.wait_ge(self.turned, self.b + t + 1)
                    nc.scalar.copy(xT[:, :, t0:t0 + n], self.back_ps(t))
                    nc.scalar.copy(xh[:, :, t0:t0 + n], self.back_ps(t)).then_inc(self.x_hi, 1)

                if self.stats:
                    sqrt(0)
                for t in range(5):
                    if self.stats and t + 1 < 5:
                        sqrt(t + 1)
                    if self.back:
                        evict(t)

            def dve_part(self, dve):
                def stats(t):
                    n = TOKENS[t][1]
                    m = slice(2 * t, 2 * t + 2)
                    v = slice(2 * t + 1, 2 * t + 2)
                    dve.wait_ge(self.rows, self.s + t + 1)
                    for a in range(2):
                        nc.vector.bn_stats(bn[0:n, 12 * t + 6 * a:12 * t + 6 * a + 6],
                                           ps[0:n, 2 * (t % 2) + a, :]).then_inc(self.bn, 1)
                    dve.wait_ge(self.bn, 2 * (self.s + t + 1))
                    nc.vector.bn_aggr(mv[0:n, m], bn[0:n, 12 * t:12 * t + 12]).then_inc(self.mean, 1)
                    dve.wait_ge(self.mean, self.s + t + 1)
                    nc.vector.tensor_scalar(mv[0:n, v], mv[0:n, v], EPS / ALPHA ** 2, None, ALU.add
                                            ).then_inc(self.var, 1)

                def norm(t):
                    n = TOKENS[t][1]
                    dve.wait_ge(self.sd, self.s + t + 1)
                    nc.vector.reciprocal(rstd[0:n, t:t + 1], sd[0:n, t:t + 1]).then_inc(self.rs, 1)
                    dve.wait_ge(self.rs, self.s + t + 1)
                    nc.vector.tensor_scalar(xn[0:n, t], ps[0:n, 2 * (t % 2):2 * (t % 2) + 2, :].rearrange("p a b -> p (a b)"),
                                            mv[0:n, 2 * t:2 * t + 1], rstd[0:n, t:t + 1],
                                            ALU.subtract, ALU.mult).then_inc(self.normed, 1)

                def low(t):
                    t0, n = TOKENS[t]
                    dve.wait_ge(self.x_hi, self.b + t + 1)
                    nc.vector.tensor_tensor(xl[:, :, t0:t0 + n], xT[:, :, t0:t0 + n],
                                            xh[:, :, t0:t0 + n].bitcast(F32), ALU.subtract).then_inc(self.x_lo, 1)

                if self.stats:
                    stats(0)
                for t in range(5):
                    if self.stats:
                        if t + 1 < 5:
                            stats(t + 1)
                        norm(t)
                    if self.back and t >= 1:
                        low(t - 1)
                if self.back:
                    low(4)

            def pool_part(self, pool):
                pool.wait_ge(self.params, 32 * (self.s // 5 + 1))
                for t in range(5):
                    n = TOKENS[t][1]
                    pool.wait_ge(self.normed, self.s + t + 1)
                    nc.gpsimd.tensor_tensor(xn[0:n, t], xn[0:n, t], ln_gain[0:n], ALU.mult).then_inc(self.gained, 1)
                    pool.wait_ge(self.gained, self.s + t + 1)
                    nc.gpsimd.tensor_tensor(xn[0:n, t], xn[0:n, t], ln_bias[0:n], ALU.add).then_inc(self.biased, 1)

        class Project:

            def __init__(self, tag, c, n_chunks, stage=None, nat=None, nat_s=None, keep=None, direct=None, scale=1.0):
                self.c, self.rounds = c, n_chunks // 2
                self.stage, self.nat, self.nat_s, self.keep, self.direct = stage, nat, nat_s, keep, direct
                self.scale = scale
                self.tiles = 2 * n_chunks
                self.taken = sem(f"{tag}_taken")
                if nat is not None:
                    self.rows = sem(f"{tag}_rows")
                    self.stored = sem(f"{tag}_stored")
                if keep is not None:
                    self.kept = sem(f"{tag}_kept")

            def loads(self, sp, col):
                for i in range(self.rounds):
                    for j in range(2):
                        load_chunk(sp, self.c + 2 * i + j, self.c // 2 + i, j,
                                   w_in, col + 512 * i + 256 * j)

            def pe_part(self, pe):
                def turn(i, t):
                    u = 4 * i + t
                    pe.wait_ge(self.taken, u + 3)
                    pe.wait_ge(self.stored, u + 1)
                    b = 4 + 2 * (t % 2)
                    for blk in range(NB):
                        nc.tensor.transpose(ps[:, b, blk * P:blk * P + P], self.stage[:, t % 2, blk * P:blk * P + P],
                                            ident[:])
                    nc.tensor.transpose(ps[0:NS, b + 1, 0:P], self.stage[:, t % 2, SEQ:T], ident[:]
                                        ).then_inc(self.rows, 1)

                with pe.Fori(0, self.rounds) as i:
                    for t in range(4):
                        if t % 2 == 0:
                            chunk_ready(pe, self.c + 2 * i + t // 2)
                        pe.wait_ge(self.taken, 4 * i + t + 1)
                        gemm(2 * (t % 2), t // 2, t % 2, KD, xh, xl)
                        if self.nat is not None and t > 0:
                            turn(i, t - 1)
                    if self.nat is not None:
                        turn(i, 3)

            def act_part(self, act):
                act.sem_inc(self.taken, 2)
                with act.Fori(0, self.rounds) as i:
                    for t in range(4):
                        c = self.c + 2 * i + t // 2
                        tile_done(act, c, t % 2)
                        if self.nat is not None:
                            act.wait_ge(self.rows, 4 * i + t + 1)
                            if self.keep is not None:
                                act.wait_ge(self.kept, 4 * i + t + 1)
                            dst = self.stage[:, t % 2:t % 2 + 1]
                        else:
                            dst = self.direct[:, bass.ds(4 * i + t, 1)]
                        nc.scalar.mul(dst.rearrange("p o (a b) -> p (o a) b", b=HALF), banks(2 * (t % 2)), self.scale
                                      ).then_inc(self.taken, 1)
                        if t % 2 == 1:
                            split_hi(act, c + 2, self.c // 2 + i + 1, t // 2)

            def dve_part(self, dve):
                if self.nat is not None:
                    dve.sem_inc(self.stored, 2)
                with dve.Fori(0, self.rounds) as i:
                    for t in range(4):
                        c = self.c + 2 * i + t // 2
                        if t % 2 == 1:
                            split_lo(dve, c + 2, t // 2)
                        if self.nat is not None:
                            b = 4 + 2 * (t % 2)
                            dve.wait_ge(self.rows, 4 * i + t + 3)
                            nc.vector.tensor_copy(self.nat[:, :, bass.ds(512 * i + P * t, P)],
                                                  ps[:, b, :].rearrange("p (a b) -> p a b", b=P))
                            nc.vector.tensor_copy(self.nat_s[0:NS, bass.ds(512 * i + P * t, P)],
                                                  ps[0:NS, b + 1, 0:P]).then_inc(self.stored, 1)

            def pool_part(self, pool):
                pool.sem_inc(self.kept, 2)
                with pool.Fori(0, self.rounds) as i:
                    for t in range(4):
                        pool.wait_ge(self.taken, 4 * i + t + 3)
                        nc.gpsimd.tensor_copy(self.keep[:, bass.ds(4 * i + t, 1)], self.stage[:, t % 2:t % 2 + 1]
                                              ).then_inc(self.kept, 1)

            def all_stored(self, eng):
                eng.wait_ge(self.stored, self.tiles + 2)

        class Branch:
            def __init__(self, tag, c, col, w, oh, ol, add):
                self.c, self.col, self.w, self.oh, self.ol, self.add = c, col, w, oh, ol, add
                self.sig_done = sem(f"{tag}_sig_done")
                self.prod_done = sem(f"{tag}_prod_done")
                if add:
                    self.merged = sem(f"{tag}_merged")
                    self.m_hi = sem(f"{tag}_m_hi")
                    self.m_lo = sem(f"{tag}_m_lo")

            def loads(self, sp, first, last):
                for i in range(first, last):
                    load_chunk(sp, self.c + 2 * i, self.c // 2 + i, 0,
                               w_in, self.col + 256 * i)
                    load_chunk(sp, self.c + 2 * i + 1, self.c // 2 + i, 1,
                               self.w, 256 * i)

            def pe_part(self, pe):
                with pe.Fori(0, KD // 2) as i:
                    for j in range(2):
                        chunk_ready(pe, self.c + 2 * i + j)
                        for n in range(2):
                            pe.wait_ge(self.prod_done if j else self.sig_done, 2 * i + n + 1)
                            gemm(4 * j + 2 * n, j, n, KD, self.oh if j else xh, self.ol if j else xl)

            def act_part(self, act):
                act.sem_inc(self.sig_done, 2)
                with act.Fori(0, KD // 2) as i:
                    for n in range(2):
                        tile_done(act, self.c + 2 * i, n)
                        act.wait_ge(self.prod_done, 2 * i + n + 1)
                        nc.scalar.activation(halves(gated[:, n]), banks(2 * n), ACT.Sigmoid).then_inc(self.sig_done, 1)
                    split_hi(act, self.c + 2 * i + 2, self.c // 2 + i + 1, 0)
                    if self.add:
                        for n in range(2):
                            act.wait_ge(self.merged, 2 * i + n + 1)
                            nc.scalar.copy(mh[:, bass.ds(2 * i + n, 1)], prod[:, n:n + 1]).then_inc(self.m_hi, 1)
                    split_hi(act, self.c + 2 * i + 3, self.c // 2 + i + 1, 1)

            def dve_part(self, dve):
                dve.sem_inc(self.prod_done, 2)
                with dve.Fori(0, KD // 2) as i:
                    split_lo(dve, self.c + 2 * i + 2, 0)
                    for n in range(2):
                        k = bass.ds(2 * i + n, 1)
                        tile_done(dve, self.c + 2 * i + 1, n)
                        dve.wait_ge(self.sig_done, 2 * i + n + 3)
                        dst = prod[:, n:n + 1] if self.add else mT[:, k]
                        nc.vector.tensor_tensor(dst.rearrange("p o (a b) -> p (o a) b", b=HALF), banks(4 + 2 * n),
                                                halves(gated[:, n]), ALU.mult).then_inc(self.prod_done, 1)
                        if self.add:
                            dve.wait_ge(self.prod_done, 2 * i + n + 3)
                            nc.vector.tensor_tensor(prod[:, n:n + 1], prod[:, n:n + 1], mT[:, k], ALU.add
                                                    ).then_inc(self.merged, 1)
                            dve.wait_ge(self.m_hi, 2 * i + n + 1)
                            nc.vector.tensor_tensor(ml[:, k], prod[:, n:n + 1], mh[:, k].bitcast(F32), ALU.subtract
                                                    ).then_inc(self.m_lo, 1)
                    split_lo(dve, self.c + 2 * i + 3, 1)

        class HeadNorm:

            def __init__(self, tag, blocks, squares, n):
                self.blocks, self.squares, self.n, self.g = blocks, squares, n, D // n
                self.sq_done = sem(f"{tag}_sq_done")
                self.summed = sem(f"{tag}_summed")
                self.guarded = sem(f"{tag}_guarded")
                self.sd = sem(f"{tag}_sd")
                self.rs = sem(f"{tag}_rs")
                self.scaled = sem(f"{tag}_scaled")
                self.turned = sem(f"{tag}_turned")
                self.evicted = sem(f"{tag}_evicted")
                full = sum(n == P for _, _, n in blocks)
                self.parts = [(P, slice(0, full * self.g))]
                if full < len(blocks):
                    self.parts.append((NS, slice(full * self.g, (full + 1) * self.g)))

            def act_squares(self, act):
                for b, (src, _, r) in enumerate(self.blocks):
                    act.wait_ge(self.summed, b + 1)
                    nc.scalar.activation(self.squares[0:r, b % 2], src, ACT.Square).then_inc(self.sq_done, 1)
                for p, (r, c) in enumerate(self.parts):
                    act.wait_ge(self.guarded, p + 1)
                    nc.scalar.activation(ssd[0:r, c], ss[0:r, c], ACT.Sqrt).then_inc(self.sd, 1)

            def dve_scale(self, dve):
                g, n = self.g, self.n
                dve.sem_inc(self.summed, 2)
                for b, (_, _, r) in enumerate(self.blocks):
                    dve.wait_ge(self.sq_done, b + 1)
                    nc.vector.tensor_reduce(ss[0:r, b * g:b * g + g],
                                            self.squares[0:r, b % 2].rearrange("p (h d) -> p h d", d=n), AX_X, ALU.add
                                            ).then_inc(self.summed, 1)
                dve.wait_ge(self.summed, len(self.blocks) + 2)
                for r, c in self.parts:
                    nc.vector.tensor_scalar(ss[0:r, c], ss[0:r, c], 1.0 / n, EPS, ALU.mult, ALU.add
                                            ).then_inc(self.guarded, 1)
                for p, (r, c) in enumerate(self.parts):
                    dve.wait_ge(self.sd, p + 1)
                    nc.vector.reciprocal(srs[0:r, c], ssd[0:r, c]).then_inc(self.rs, 1)
                dve.wait_ge(self.rs, len(self.parts))
                for b, (src, _, r) in enumerate(self.blocks):
                    rows = src.rearrange("p (h d) -> p h d", d=n)
                    nc.vector.tensor_tensor(rows, rows, srs[0:r, b * g:b * g + g].unsqueeze(2).broadcast_to([r, g, n]),
                                            ALU.mult).then_inc(self.scaled, 1)

            def pe_part(self, pe):
                for b, (src, _, r) in enumerate(self.blocks):
                    pe.wait_ge(self.scaled, b + 1)
                    if b >= 2:
                        pe.wait_ge(self.evicted, b - 1)
                    for k in range(KD):
                        mm = nc.tensor.transpose(ps[:, 2 * (b % 2) + k // 4, (k % 4) * P:(k % 4) * P + r],
                                                 src[:, k * P:k * P + P], ident[0:r, 0:r])
                    mm.then_inc(self.turned, 1)

            def act_evict(self, act, dst, scale=1.0):
                for b, (_, t0, r) in enumerate(self.blocks):
                    act.wait_ge(self.turned, b + 1)
                    src = ps[:, 2 * (b % 2):2 * (b % 2) + 2, :].rearrange("p a (k c) -> p (a k) c", c=P)[:, :, 0:r]
                    nc.scalar.mul(dst[:, :, t0:t0 + r], src, scale).then_inc(self.evicted, 1)

        class Split:
            def __init__(self, tag, src, hi, lo):
                self.src, self.hi, self.lo = src, hi, lo
                self.hi_done, self.lo_done = sem(f"{tag}_hi_done"), sem(f"{tag}_lo_done")

            def act_part(self, act):
                for k in range(0, KD, 2):
                    nc.scalar.copy(self.hi[:, k:k + 2], self.src[:, k:k + 2]).then_inc(self.hi_done, 1)

            def dve_part(self, dve):
                for k in range(0, KD, 2):
                    dve.wait_ge(self.hi_done, k // 2 + 1)
                    nc.vector.tensor_tensor(self.lo[:, k:k + 2], self.src[:, k:k + 2],
                                            self.hi[:, k:k + 2].bitcast(F32), ALU.subtract).then_inc(self.lo_done, 1)

            def ready(self, pe):
                pe.wait_ge(self.lo_done, KD // 2)

        class PromptAttention:
            def __init__(self):
                self.q_staged = sem("pa_q_staged")
                self.bias_set = sem("pa_bias_set")
                self.scored = sem("pa_scored")
                self.scaled = sem("pa_scaled")
                self.exped = sem("pa_exped")
                self.recip = sem("pa_recip")
                self.lammed = sem("pa_lammed")
                self.second = sem("pa_second")
                self.combined = sem("pa_combined")
                self.turned = sem("pa_turned")
                self.aT_set = sem("pa_aT_set")
                self.pv = sem("pa_pv")
                self.o_set = sem("pa_o_set")

            def keys(self, i):
                return P * (i + 1)

            def pool_unit(self, pool, i, h, s, u):
                pool.wait_ge(self.scored, u + 1)
                nc.gpsimd.tensor_tensor(q_stage[:, s], qaT[:, h, P * i:P * i + P].broadcast_to([P, 2, P]),
                                        map_rows[:].unsqueeze(2).broadcast_to([P, 2, P]), ALU.mult
                                        ).then_inc(self.q_staged, 1)
                n = self.keys(i)
                pool.wait_ge(self.scaled, u + 1)
                nc.gpsimd.tensor_tensor(bias8[:, s:s + 1, 0:n], dist[:, SEQ - n:SEQ].unsqueeze(1),
                                        slope8[:, h].unsqueeze(2).broadcast_to([P, 1, n]), ALU.mult
                                        ).then_inc(self.bias_set, 1)

            def pool_part(self, pool):
                for i in range(NB):
                    with pool.Fori(0, HA // 2) as hp:
                        for s in range(2):
                            self.pool_unit(pool, i, bass.ds(2 * hp + s, 1), s, HA * i + 2 * hp + s)

            def scores(self, pe, i, h, s, u):
                n = self.keys(i)
                pe.wait_ge(self.q_staged, u + 1)
                pe.wait_ge(self.scaled, u + 1)
                for m in range(2):
                    mm = nc.tensor.matmul(ps[:, 2 * s + m, 0:n], q_stage[:, s, m], kaT[:, h, 0:n], start=True, stop=True)
                mm.then_inc(self.scored, 1)

            def turn(self, pe, i, s, u):
                pe.wait_ge(self.combined, u + 3)
                pe.wait_ge(self.aT_set, u + 1)
                for j in range(i + 1):
                    mm = nc.tensor.transpose(ps[:, 4 + s, P * j:P * j + P], a_sb[:, s, P * j:P * j + P], ident[:])
                mm.then_inc(self.turned, 1)

            def values(self, pe, i, h, s, u):
                pe.wait_ge(self.aT_set, u + 3)
                pe.wait_ge(self.o_set, u + 1)
                for j in range(i + 1):
                    mm = nc.tensor.matmul(ps[:, 6 + s, 0:DV], aT[:, s, P * j:P * j + P],
                                          v_nat[:, j, bass.ds(h * DV, DV)], start=j == 0, stop=j == i)
                mm.then_inc(self.pv, 1)

            def pe_part(self, pe):
                def head(h):
                    return bass.ds(h, 1)
                self.scores(pe, 0, head(0), 0, 0)
                self.scores(pe, 0, head(1), 1, 1)
                for i in range(NB):
                    u0 = HA * i
                    with pe.Fori(0, HA // 2 - 1) as hp:
                        for s in range(2):
                            self.turn(pe, i, s, u0 + 2 * hp + s)
                            self.scores(pe, i, head(2 * hp + s + 2), s, u0 + 2 * hp + s + 2)
                            self.values(pe, i, 2 * hp + s, s, u0 + 2 * hp + s)
                    for s in range(2):
                        self.turn(pe, i, s, u0 + HA - 2 + s)
                        if i + 1 < NB:
                            self.scores(pe, i + 1, head(s), s, u0 + HA + s)
                        self.values(pe, i, HA - 2 + s, s, u0 + HA - 2 + s)

            def scale(self, dve, i, s, u):
                n = self.keys(i)
                dve.wait_ge(self.scored, u + 3)
                dve.wait_ge(self.bias_set, u + 1)
                dve.wait_ge(self.exped, u + 1)
                nc.vector.memset(rsum[:, 2 * s:2 * s + 2], 0.0)
                for m in range(2):
                    ins = nc.vector.tensor_tensor_reduce(s_sb[:, s, m, 0:n], ps[:, 2 * s + m, 0:n], bias8[:, s, 0:n],
                                                         -DH ** -0.5, -MASKED, ALU.add, ALU.min,
                                                         nmax[:, 2 * s + m:2 * s + m + 1])
                ins.then_inc(self.scaled, 1)

            def combine(self, dve, i, s, u):
                n = self.keys(i)
                r = slice(2 * s, 2 * s + 2)
                dve.wait_ge(self.exped, u + 3)
                nc.vector.reciprocal(rr[:, r], rsum[:, r]).then_inc(self.recip, 1)
                dve.wait_ge(self.recip, u + 1)
                nc.vector.tensor_tensor(rr[:, r], rr[:, r], lamv[:], ALU.mult).then_inc(self.lammed, 1)
                dve.wait_ge(self.lammed, u + 1)
                nc.vector.tensor_scalar(p_sb[:, s, 1, 0:n], p_sb[:, s, 1, 0:n], rr[:, 2 * s + 1:2 * s + 2], None,
                                        ALU.mult).then_inc(self.second, 1)
                dve.wait_ge(self.second, u + 1)
                dve.wait_ge(self.turned, u + 1)
                nc.vector.scalar_tensor_tensor(a_sb[:, s, 0:n], p_sb[:, s, 0, 0:n], rr[:, 2 * s:2 * s + 1],
                                               p_sb[:, s, 1, 0:n], ALU.mult, ALU.subtract).then_inc(self.combined, 1)

            def dve_part(self, dve):
                self.scale(dve, 0, 0, 0)
                for i in range(NB):
                    u0 = HA * i
                    with dve.Fori(0, HA // 2 - 1) as hp:
                        for s in range(2):
                            self.scale(dve, i, 1 - s, u0 + 2 * hp + s + 1)
                            self.combine(dve, i, s, u0 + 2 * hp + s)
                    self.scale(dve, i, 1, u0 + HA - 1)
                    self.combine(dve, i, 0, u0 + HA - 2)
                    if i + 1 < NB:
                        self.scale(dve, i + 1, 0, u0 + HA)
                    self.combine(dve, i, 1, u0 + HA - 1)

            def exp(self, act, i, s, u):
                n = self.keys(i)
                act.wait_ge(self.scaled, u + 3)
                act.wait_ge(self.combined, u + 1)
                for m in range(2):
                    k = slice(2 * s + m, 2 * s + m + 1)
                    ins = nc.scalar.activation(p_sb[:, s, m, 0:n], s_sb[:, s, m, 0:n], ACT.Exp, bias=nmax[:, k],
                                               scale=-1.0, accum_out=rsum[:, k])
                ins.then_inc(self.exped, 1)

            def keep_turned(self, act, i, s, u):
                n = self.keys(i)
                act.wait_ge(self.turned, u + 3)
                act.wait_ge(self.pv, u + 1)
                nc.scalar.copy(aT[:, s, 0:n], ps[:, 4 + s, 0:n]).then_inc(self.aT_set, 1)

            def keep_output(self, act, s, u, i, h):
                act.wait_ge(self.pv, u + 3)
                nc.scalar.copy(o_nat[:, i, bass.ds(h * DV, DV)], ps[:, 6 + s, 0:DV]).then_inc(self.o_set, 1)

            def act_part(self, act):
                self.exp(act, 0, 0, 0)
                for i in range(NB):
                    u0 = HA * i
                    self.exp(act, i, 1, u0 + 1)
                    self.keep_turned(act, i, 0, u0)
                    if i:
                        self.keep_output(act, 1, u0 - 1, i - 1, HA - 1)
                    with act.Fori(0, HA // 2 - 1) as hp:
                        for s in range(2):
                            h = 2 * hp + 1 + s
                            self.exp(act, i, s, u0 + h + 1)
                            self.keep_turned(act, i, 1 - s, u0 + h)
                            self.keep_output(act, s, u0 + h - 1, i, h - 1)
                    if i + 1 < NB:
                        self.exp(act, i + 1, 0, u0 + HA)
                    self.keep_turned(act, i, 1, u0 + HA - 1)
                    self.keep_output(act, 0, u0 + HA - 2, i, HA - 2)
                self.keep_output(act, 1, HA * NB - 1, NB - 1, HA - 1)

            def credits_pe(self, pe):
                pe.sem_inc(self.scored, 2)
                pe.sem_inc(self.turned, 2)
                pe.sem_inc(self.pv, 2)

            def credits_dve(self, dve):
                dve.sem_inc(self.scaled, 2)
                dve.sem_inc(self.combined, 2)

            def credits_act(self, act):
                act.sem_inc(self.exped, 2)
                act.sem_inc(self.aT_set, 2)
                act.sem_inc(self.o_set, 2)

        GC = HA * 2 * TDEC

        class DecodeAttention:
            def __init__(self):
                self.k_landed = [sem(f"da_k_landed{r}") for r in range(4)]
                self.v_landed = [sem(f"da_v_landed{r}") for r in range(4)]
                self.k_turned = sem("da_k_turned")
                self.kT_act = sem("da_kT_act")
                self.kT_dve = sem("da_kT_dve")
                self.scored = sem("da_scored")
                self.biased = sem("da_biased")
                self.max_past = sem("da_max_past")
                self.max_both = sem("da_max_both")
                self.max_all = sem("da_max_all")
                self.shifted = sem("da_shifted")
                self.exped = sem("da_exped")
                self.summed = sem("da_summed")
                self.pv = sem("da_pv")
                self.lsum = sem("da_lsum")
                self.kept = sem("da_kept")
                self.q_zero = sem("da_q_zero")
                self.q_set = sem("da_q_set")
                self.new_scored = sem("da_new_scored")
                self.new_biased = sem("da_new_biased")
                self.fin = sem("da_fin")
                self.fin_ss = sem("da_fin_ss")
                self.fin_sd = sem("da_fin_sd")
                self.oa_set = sem("da_oa_set")

            def load_page(self, eng, cache, ring, landed, free, b, g):
                page = eng.value_load(pages[0:1, bass.ds(PAGES * b + g, 1)], min_val=0, max_val=cache.shape[1] - 1)
                eng.wait_ge(free, PAGES * b + g + 1)
                eng.dma_start(ring[:, g % 4], cache[0, bass.ds(page, 1)].rearrange("o p h d -> p (o h d)")
                              ).then_inc(landed[g % 4], 16)

            def load_k(self, sp, b, g):
                self.load_page(sp, cache_k, k_page, self.k_landed, self.k_turned, b, g)

            def load_v(self, pool, b, g):
                self.load_page(pool, cache_v, v_page, self.v_landed, self.pv, b, g)

            def sp_part(self, sp):
                with sp.Fori(0, DEC) as b:
                    for g in range(PAGES):
                        self.load_k(sp, b, g)

            def pool_part(self, pool):
                for b in range(DEC):
                    for g in range(4):
                        self.load_v(pool, b, g)
                    pool.wait_ge(self.max_both, b + 1)
                    nc.gpsimd.partition_all_reduce(dmax_all[:], dmax[:], P, RMAX).then_inc(self.max_all, 1)
                    for g in range(4, PAGES):
                        self.load_v(pool, b, g)

            def pe_scores(self, pe, b):
                def turn(g):
                    s = g % 2
                    n = PAGES * b + g
                    pe.wait_ge(self.k_landed[g % 4], 32 * b + 16 * (g // 4) + 16)
                    pe.wait_ge(self.kT_dve if s else self.kT_act, 4 * b + g // 2 + 1)
                    for h in range(HA):
                        mm = nc.tensor.transpose(ps[:, 2 * s + h // 4, (h % 4) * P:(h % 4) * P + P],
                                                 k_page[:, g % 4, h * P:h * P + P], ident[:])
                    mm.then_inc(self.k_turned, 1)

                def score(g):
                    s = g % 2
                    pe.wait_ge(self.kT_dve if s else self.kT_act, 4 * b + g // 2 + 2)
                    if g == 0:
                        pe.wait_ge(self.biased, b + 1)
                    for h in range(HA):
                        mm = nc.tensor.matmul(ps[:, 4, GC * g + 8 * h:GC * g + 8 * h + 8], kT[:, s, h * P:h * P + P],
                                              q_bd[:, bass.ds(b, 1), h], start=True, stop=True)
                    mm.then_inc(self.scored, 1)
                turn(0)
                for g in range(PAGES):
                    if g + 1 < PAGES:
                        turn(g + 1)
                    score(g)

            def pe_values(self, pe, b):
                pe.wait_ge(self.exped, 2 * b + 2)
                pe.wait_ge(self.kept, b + 1)
                for g in range(PAGES):
                    pe.wait_ge(self.v_landed[g % 4], 32 * b + 16 * (g // 4) + 16)
                    for h in range(HA):
                        mm = nc.tensor.matmul(ps[:, 5, 8 * h:8 * h + 8], v_page[:, g % 4, h * DV:h * DV + DV],
                                              dp_sb[:, GC * g + 8 * h:GC * g + 8 * h + 8],
                                              start=g == 0 and h == 0, stop=False, skip_group_check=True)
                    mm.then_inc(self.pv, 1)
                for h in range(HA):
                    nc.tensor.matmul(ps[:, 5, 8 * h:8 * h + 8], v_nat_s[0:NS, h * DV:h * DV + DV],
                                     s_new[0:NS, bass.ds(b, 1), 8 * h:8 * h + 8], start=False, stop=h == HA - 1,
                                     skip_group_check=True)
                pe.wait_ge(self.summed, b + 1)
                nc.tensor.matmul(ps[:, 6, 0:GC], ones[:], dpsum[:], start=True, stop=False)
                nc.tensor.matmul(ps[:, 6, 0:GC], ones[0:NS], s_new[0:NS, bass.ds(b, 1)], start=False, stop=True
                                 ).then_inc(self.lsum, 1)

            def pe_new(self, pe):
                pe.wait_ge(self.q_set, 2)
                for h in range(HA):
                    mm = nc.tensor.matmul(ps[0:NS, 7, 64 * h:64 * h + 64].rearrange("p (b c) -> p b c", c=8),
                                          kaT[:, h, SEQ:T], q_bd[:, :, h], start=True, stop=True)
                mm.then_inc(self.new_scored, 1)

            def pe_part(self, pe):
                self.pe_scores(pe, 0)
                with pe.Fori(1, DEC) as b:
                    self.pe_scores(pe, b)
                    self.pe_values(pe, b - 1)
                self.pe_values(pe, DEC - 1)

            def dve_setup(self, dve):
                nc.vector.memset(q_bd[:], 0.0).then_inc(self.q_zero, 1)
                dve.wait_ge(self.q_zero, 1)
                for m in range(2):
                    r = slice(DH * m, DH * m + DH)
                    nc.vector.tensor_copy(q_bd[r, :, :, TDEC * m:TDEC * m + TDEC].rearrange("p b h t -> p h b t"),
                                          qaT[r, :, SEQ:T].rearrange("p h (b t) -> p h b t", t=TDEC)
                                          ).then_inc(self.q_set, 1)

            def dve_new(self, dve):
                dve.wait_ge(self.new_scored, 1)
                for h in range(HA):
                    nc.vector.scalar_tensor_tensor(s_new[0:NS, :, 8 * h:8 * h + 8],
                                                   ps[0:NS, 7, 64 * h:64 * h + 64].rearrange("p (b c) -> p b c", c=8),
                                                   DH ** -0.5, s_new[0:NS, :, 8 * h:8 * h + 8], ALU.mult, ALU.add
                                                   ).then_inc(self.new_biased, 1)

            def dve_evict(self, dve, b, g):
                dve.wait_ge(self.k_turned, PAGES * b + g + 5)
                dve.wait_ge(self.scored, PAGES * b + g + 1)
                nc.vector.tensor_copy(kT[:, 1], ps[:, 2:4, :].rearrange("p a b -> p (a b)")).then_inc(self.kT_dve, 1)

            def dve_softmax(self, dve, b):
                one = bass.ds(b, 1)
                dve.wait_ge(self.scored, PAGES * b + PAGES + 2)
                nc.vector.scalar_tensor_tensor(ds_sb[:], ps[:, 4, :], DH ** -0.5, bias_past[:], ALU.mult, ALU.add
                                               ).then_inc(self.biased, 1)
                dve.wait_ge(self.biased, b + 2)
                nc.vector.tensor_reduce(dmax[:], ds_sb[:].rearrange("p (g c) -> p c g", c=GC), AX_X, ALU.max
                                        ).then_inc(self.max_past, 1)
                dve.wait_ge(self.max_past, b + 1)
                nc.vector.tensor_tensor(dmax[0:NS], dmax[0:NS], s_new[0:NS, one].rearrange("p o c -> p (o c)"),
                                        ALU.max).then_inc(self.max_both, 1)
                dve.wait_ge(self.max_all, b + 1)
                nc.vector.tensor_tensor(ds_sb[:].rearrange("p (g c) -> p g c", c=GC),
                                        ds_sb[:].rearrange("p (g c) -> p g c", c=GC),
                                        dmax_all[:].unsqueeze(1).broadcast_to([P, PAGES, GC]), ALU.subtract
                                        ).then_inc(self.shifted, 1)
                nc.vector.tensor_tensor(s_new[0:NS, one], s_new[0:NS, one], dmax_all[0:NS].unsqueeze(1), ALU.subtract
                                        ).then_inc(self.shifted, 1)

            def dve_sum(self, dve, b):
                dve.wait_ge(self.exped, 2 * b + 2)
                nc.vector.tensor_reduce(dpsum[:], dp_sb[:].rearrange("p (g c) -> p c g", c=GC), AX_X, ALU.add
                                        ).then_inc(self.summed, 1)

            def dve_part(self, dve):
                for g in range(1, PAGES, 2):
                    self.dve_evict(dve, 0, g)
                with dve.Fori(1, DEC) as b:
                    self.dve_softmax(dve, b - 1)
                    self.dve_evict(dve, b, 1)
                    self.dve_sum(dve, b - 1)
                    for g in range(3, PAGES, 2):
                        self.dve_evict(dve, b, g)
                self.dve_softmax(dve, DEC - 1)
                self.dve_sum(dve, DEC - 1)

            def act_evict(self, act, b, g):
                act.wait_ge(self.k_turned, PAGES * b + g + 5)
                act.wait_ge(self.scored, PAGES * b + g + 1)
                nc.scalar.copy(kT[:, 0], ps[:, 0:2, :].rearrange("p a b -> p (a b)")).then_inc(self.kT_act, 1)

            def act_exp(self, act, b):
                act.wait_ge(self.shifted, 2 * b + 2)
                act.wait_ge(self.lsum, b + 1)
                nc.scalar.activation(dp_sb[:], ds_sb[:], ACT.Exp).then_inc(self.exped, 1)
                nc.scalar.activation(s_new[0:NS, bass.ds(b, 1)], s_new[0:NS, bass.ds(b, 1)], ACT.Exp
                                     ).then_inc(self.exped, 1)

            def act_keep(self, act, b):
                act.wait_ge(self.lsum, b + 2)
                for bank, dst in ((5, dec_o), (6, dec_l)):
                    ins = nc.scalar.copy(dst[:, :, bass.ds(32 * b, 32)].rearrange("p m (h t) -> p m h t", t=TDEC),
                                         ps[:, bank, 0:GC].rearrange("p (h m t) -> p m h t", m=2, t=TDEC))
                ins.then_inc(self.kept, 1)

            def act_part(self, act):
                for g in range(0, PAGES, 2):
                    self.act_evict(act, 0, g)
                with act.Fori(1, DEC) as b:
                    self.act_evict(act, b, 0)
                    self.act_exp(act, b - 1)
                    for g in range(2, PAGES, 2):
                        self.act_evict(act, b, g)
                    self.act_keep(act, b - 1)
                self.act_exp(act, DEC - 1)
                self.act_keep(act, DEC - 1)

            def dve_finish(self, dve):
                dve.wait_ge(self.kept, DEC + 1)
                nc.vector.reciprocal(dec_l[:], dec_l[:]).then_inc(self.fin, 1)
                dve.wait_ge(self.fin, 1)
                nc.vector.tensor_tensor(dec_o[:], dec_o[:], dec_l[:], ALU.mult).then_inc(self.fin, 1)
                dve.wait_ge(self.fin, 2)
                nc.vector.tensor_scalar(dec_o[:, 1], dec_o[:, 1], lamv[:, 1:2], None, ALU.mult).then_inc(self.fin, 1)
                dve.wait_ge(self.fin, 3)
                nc.vector.tensor_tensor(dec_o[:, 0], dec_o[:, 0], dec_o[:, 1], ALU.subtract).then_inc(self.fin, 1)
                dve.wait_ge(self.fin, 4)
                nc.vector.tensor_tensor(dec_o[:, 1], dec_o[:, 0], dec_o[:, 0], ALU.mult).then_inc(self.fin, 1)
                dve.wait_ge(self.fin_ss, 1)
                nc.vector.tensor_scalar(dec_l[:, 0], ps[:, 7, 0:256], 1.0 / DV, EPS, ALU.mult, ALU.add
                                        ).then_inc(self.fin, 1)
                dve.wait_ge(self.fin_sd, 1)
                nc.vector.reciprocal(dec_l[:, 0], dec_l[:, 1]).then_inc(self.fin, 1)
                dve.wait_ge(self.fin, 7)
                nc.vector.tensor_tensor(dec_o[:, 1], dec_o[:, 0], dec_l[:, 0], ALU.mult).then_inc(self.fin, 1)
                dve.wait_ge(self.fin, 8)
                nc.vector.tensor_scalar(oaT[:, :, SEQ:T].rearrange("p h (b t) -> p h b t", t=TDEC),
                                        dec_o[:, 1].rearrange("p (b h t) -> p h b t", h=HA, t=TDEC),
                                        subln8[:, 0:1], None, ALU.mult).then_inc(self.oa_set, 1)

            def pe_finish(self, pe):
                pe.wait_ge(self.fin, 5)
                nc.tensor.matmul(ps[:, 7, 0:256], ones[:], dec_o[:, 1], start=True, stop=True).then_inc(self.fin_ss, 1)

            def act_finish(self, act):
                act.wait_ge(self.fin, 6)
                nc.scalar.activation(dec_l[:, 1], dec_l[:, 0], ACT.Sqrt).then_inc(self.fin_sd, 1)

            def credits_pe(self, pe):
                pe.sem_inc(self.k_turned, 4)
                pe.sem_inc(self.scored, 2)
                pe.sem_inc(self.pv, 4)
                pe.sem_inc(self.lsum, 1)

            def credits_dve(self, dve):
                dve.sem_inc(self.kT_dve, 1)
                dve.sem_inc(self.biased, 1)

            def credits_act(self, act):
                act.sem_inc(self.kT_act, 1)
                act.sem_inc(self.kept, 1)

        class Retention:
            def __init__(self):
                self.scored = sem("rt_scored")
                self.sc_set = sem("rt_sc_set")
                self.qx_set = sem("rt_qx_set")
                self.kw_set = sem("rt_kw_set")
                self.out = sem("rt_out")
                self.o_kept = sem("rt_o_kept")
                self.kv = sem("rt_kv")
                self.st_set = sem("rt_st_set")
                self.st_stored = sem("rt_st_stored")
                self.s_scored = sem("rs_scored")
                self.s_sc_set = sem("rs_sc_set")
                self.s_in = [sem(f"rs_in{j}") for j in range(2)]
                self.s_qm_zero = sem("rs_qm_zero")
                self.s_qm = sem("rs_qm")
                self.s_kw = sem("rs_kw")
                self.s_cross = sem("rs_cross")
                self.s_kv = sem("rs_kv")
                self.s_new = sem("rs_new")
                self.s_stored = [sem(f"rs_stored{j}") for j in range(2)]
                self.s_kept = sem("rs_kept")

            def chunk(self, c):
                return slice(c * P, c * P + P)

            def pe_part(self, pe):
                def scores(c):
                    if c >= 2:
                        pe.wait_ge(self.sc_set, c - 1)
                    for h in range(HR):
                        mm = nc.tensor.matmul(ps[:, c % 2, h * P:h * P + P], krT[:, h, self.chunk(c)],
                                              qrT[:, h, self.chunk(c)], start=True, stop=True)
                    mm.then_inc(self.scored, 1)

                def keys_values(c):
                    pe.wait_ge(self.kw_set, c + 1)
                    if c:
                        pe.wait_ge(self.st_set, HR * c)
                    for h in range(HR):
                        mm = nc.tensor.matmul(ps[:, 4 + h // 2, (h % 2) * RV:(h % 2) * RV + RV],
                                              kr_nat[:, c, h * RK:h * RK + RK], vr_nat[:, c, h * RV:h * RV + RV],
                                              start=True, stop=True)
                    mm.then_inc(self.kv, 1)

                def output(c):
                    pe.wait_ge(self.sc_set, c + 1)
                    if c:
                        pe.wait_ge(self.qx_set, c)
                        pe.wait_ge(self.st_set, HR * c)
                    if c >= 2:
                        pe.wait_ge(self.o_kept, c - 1)
                    for h in range(HR):
                        dst = ps[:, (6 if c % 2 else 2) + h // 2, (h % 2) * RV:(h % 2) * RV + RV]
                        mm = nc.tensor.matmul(dst, scT[:, c % 2, h * P:h * P + P], vr_nat[:, c, h * RV:h * RV + RV],
                                              start=True, stop=c == 0)
                        if c:
                            mm = nc.tensor.matmul(dst, qx[:, c % 2, h], state[:, c % 2, h * RV:h * RV + RV],
                                                  start=False, stop=True)
                    mm.then_inc(self.out, 1)

                scores(0)
                for c in range(NB):
                    if c + 1 < NB:
                        scores(c + 1)
                    keys_values(c)
                    output(c)
                pe.wait_ge(self.sc_set, NB)
                for h in range(HR):
                    mm = nc.tensor.matmul(ps[0:NS, 0, h * NS:h * NS + NS], krT[:, h, SEQ:T], qrT[:, h, SEQ:T],
                                          start=True, stop=True)
                mm.then_inc(self.s_scored, 1)
                pe.wait_ge(self.s_sc_set, 1)
                pe.wait_ge(self.o_kept, NB)
                pe.wait_ge(self.st_set, HR * NB)
                for h in range(HR):
                    nc.tensor.matmul(ps[0:NS, 2 + h // 2, (h % 2) * RV:(h % 2) * RV + RV],
                                     scT[0:NS, 0, h * NS:h * NS + NS], vr_nat_s[0:NS, h * RV:h * RV + RV],
                                     start=h % 2 == 0, stop=False, skip_group_check=True)
                pe.wait_ge(self.s_qm, DEC)
                for b in range(DEC):
                    pe.wait_ge(self.s_in[b % 2], 16 * (b // 2) + 16)
                    for h in range(HR):
                        mm = nc.tensor.matmul(ps[0:NS, 2 + h // 2, (h % 2) * RV:(h % 2) * RV + RV], qm[:, b, h],
                                              st_in[:, b % 2, h * RV:h * RV + RV], start=False,
                                              stop=b == DEC - 1, skip_group_check=True)
                    mm.then_inc(self.s_cross, 1)
                    pe.wait_ge(self.s_kw, b + 1)
                    if b >= 2:
                        pe.wait_ge(self.s_new, HR * (b - 1))
                    for h in range(HR):
                        mm = nc.tensor.matmul(ps[:, (6 if b % 2 else 4) + h // 2, (h % 2) * RV:(h % 2) * RV + RV],
                                              kw_s[0:NS, b % 2, h * RK:h * RK + RK],
                                              vr_nat_s[0:NS, h * RV:h * RV + RV], start=True, stop=True)
                    mm.then_inc(self.s_kv, 1)

            def dve_part(self, dve):
                def weigh(c):
                    dve.wait_ge(self.scored, c + 1)
                    if c >= 2:
                        dve.wait_ge(self.out, c - 1)
                    nc.vector.tensor_tensor(scT[:, c % 2], ps[:, c % 2, :], decay[:].rearrange("p h i -> p (h i)"),
                                            ALU.mult).then_inc(self.sc_set, 1)

                def advance(c):
                    dve.wait_ge(self.kv, c + 1)
                    if c >= 1:
                        dve.wait_ge(self.st_set, HR * c)
                        dve.wait_ge(self.out, c)
                    for h in range(HR):
                        e = slice(h * RV, h * RV + RV)
                        src = ps[:, 4 + h // 2, (h % 2) * RV:(h % 2) * RV + RV]
                        if c == 0:
                            ins = nc.vector.tensor_copy(state[:, 1, e], src)
                        else:
                            ins = nc.vector.scalar_tensor_tensor(state[:, (c + 1) % 2, e], state[:, c % 2, e],
                                                                 gamma[h] ** P, src, ALU.mult, ALU.add)
                        ins.then_inc(self.st_set, 1)

                weigh(0)
                for c in range(NB):
                    if c + 1 < NB:
                        weigh(c + 1)
                    advance(c)
                dve.wait_ge(self.s_scored, 1)
                dve.wait_ge(self.out, NB)
                nc.vector.tensor_tensor(scT[0:NS, 0, 0:HR * NS], ps[0:NS, 0, 0:HR * NS],
                                        decay_s[0:NS].rearrange("p h i -> p (h i)"), ALU.mult).then_inc(self.s_sc_set, 1)
                for b in range(DEC):
                    dve.wait_ge(self.s_kv, b + 1)
                    dve.wait_ge(self.s_in[b % 2], 16 * (b // 2) + 16)
                    if b >= 2:
                        dve.wait_ge(self.s_stored[b % 2], 16 * (b // 2))
                    for h in range(HR):
                        e = slice(h * RV, h * RV + RV)
                        nc.vector.scalar_tensor_tensor(st_out[:, b % 2, e], st_in[:, b % 2, e], gamma[h] ** TDEC,
                                                       ps[:, (6 if b % 2 else 4) + h // 2,
                                                          (h % 2) * RV:(h % 2) * RV + RV],
                                                       ALU.mult, ALU.add).then_inc(self.s_new, 1)

            def act_part(self, act):
                for c in range(NB):
                    act.wait_ge(self.out, c + 1)
                    b = 6 if c % 2 else 2
                    nc.scalar.copy(or_nat[:, c], ps[:, b:b + 2, :].rearrange("p a b -> p (a b)")
                                   ).then_inc(self.o_kept, 1)
                act.wait_ge(self.s_cross, DEC)
                act.wait_ge(self.s_kv, DEC)
                nc.scalar.copy(or_s[0:NS], ps[0:NS, 2:4, :].rearrange("p a b -> p (a b)")).then_inc(self.s_kept, 1)

            def pool_part(self, pool):
                for c in range(NB):
                    rows = kr_nat[:, c].rearrange("p (h d) -> p h d", d=RK)
                    nc.gpsimd.tensor_tensor(rows, rows, kdec[:].unsqueeze(2).broadcast_to([P, HR, RK]), ALU.mult
                                            ).then_inc(self.kw_set, 1)
                    if c:
                        if c >= 2:
                            pool.wait_ge(self.out, c - 1)
                        nc.gpsimd.tensor_tensor(qx[:, c % 2], qrT[:, :, self.chunk(c)], cross[:], ALU.mult
                                                ).then_inc(self.qx_set, 1)
                pool.wait_ge(self.out, NB)
                nc.gpsimd.memset(qm[:], 0.0).then_inc(self.s_qm_zero, 1)
                pool.wait_ge(self.s_qm_zero, 1)
                for b in range(DEC):
                    a = TDEC * b
                    nc.gpsimd.tensor_tensor(qm[:, b, :, a:a + TDEC], qrT[:, :, SEQ + a:SEQ + a + TDEC],
                                            cross[:, :, 0:TDEC], ALU.mult).then_inc(self.s_qm, 1)
                for b in range(DEC):
                    if b >= 2:
                        pool.wait_ge(self.s_kv, b - 1)
                    nc.gpsimd.tensor_tensor(kw_s[0:NS, b % 2].rearrange("p (h d) -> p h d", d=RK),
                                            kr_nat_s[0:NS].rearrange("p (h d) -> p h d", d=RK),
                                            kdec_s[0:NS, HR * b:HR * b + HR].unsqueeze(2).broadcast_to([NS, HR, RK]),
                                            ALU.mult).then_inc(self.s_kw, 1)

            def sp_part(self, sp):
                sp.wait_ge(self.st_set, HR * NB)
                sp.dma_start(ret_state_prompt[0, 0].rearrange("h d e -> d h e"),
                             state[:, 0].rearrange("p (h e) -> p h e", e=RV)).then_inc(out_stored, 16)
                sp.wait_ge(self.out, NB)

                def load(b):
                    sp.dma_start(st_in[:, b % 2].rearrange("p (h e) -> p h e", e=RV),
                                 state_ret[0, b].rearrange("h d e -> d h e")).then_inc(self.s_in[b % 2], 16)
                load(0)
                load(1)
                for b in range(DEC):
                    sp.wait_ge(self.s_new, HR * (b + 1))
                    sp.dma_start(ret_state_sample[0, b].rearrange("h d e -> d h e"),
                                 st_out[:, b % 2].rearrange("p (h e) -> p h e", e=RV)).then_inc(self.s_stored[b % 2], 16)
                    if b + 2 < DEC:
                        sp.wait_ge(self.s_cross, b + 1)
                        load(b + 2)

        class RetGate:
            def __init__(self, c):
                self.c = c
                self.silu_done = sem("rg_silu_done")
                self.prod_done = sem("rg_prod_done")
                self.o_hi, self.o_lo = sem("rg_o_hi"), sem("rg_o_lo")

            def loads(self, sp, first, last):
                for i in range(first, last):
                    for j in range(2):
                        load_chunk(sp, self.c + 2 * i + j, self.c // 2 + i, j,
                                   w_in, W_IN_COLS["gr"] + 512 * i + 256 * j)

            def pe_part(self, pe):
                with pe.Fori(0, 2) as i:
                    for t in range(4):
                        if t % 2 == 0:
                            chunk_ready(pe, self.c + 2 * i + t // 2)
                        pe.wait_ge(self.silu_done, 4 * i + t + 1)
                        gemm(4 + 2 * (t % 2), t // 2, t % 2, KD, xh, xl)

            def act_part(self, act):
                act.sem_inc(self.silu_done, 2)
                with act.Fori(0, 2) as i:
                    for t in range(4):
                        u, c = 4 * i + t, self.c + 2 * i + t // 2
                        tile_done(act, c, t % 2)
                        act.wait_ge(self.prod_done, u + 1)
                        nc.scalar.activation(halves(gated[:, t % 2]), banks(4 + 2 * (t % 2)), ACT.Silu
                                             ).then_inc(self.silu_done, 1)
                        act.wait_ge(self.prod_done, u + 3)
                        nc.scalar.copy(obh[:, bass.ds(u, 1)], prod[:, t % 2:t % 2 + 1]).then_inc(self.o_hi, 1)
                        if t % 2 == 1:
                            split_hi(act, c + 2, self.c // 2 + i + 1, t // 2)

            def dve_part(self, dve):
                dve.sem_inc(self.prod_done, 2)
                with dve.Fori(0, 2) as i:
                    for t in range(4):
                        u, c = 4 * i + t, self.c + 2 * i + t // 2
                        k, s = bass.ds(u, 1), slice(t % 2, t % 2 + 1)
                        dve.wait_ge(self.silu_done, u + 3)
                        nc.vector.tensor_tensor(prod[:, s], gated[:, s], onT[:, k], ALU.mult).then_inc(self.prod_done, 1)
                        dve.wait_ge(self.o_hi, u + 1)
                        nc.vector.tensor_tensor(obl[:, k], prod[:, s], obh[:, k].bitcast(F32), ALU.subtract
                                                ).then_inc(self.o_lo, 1)
                        if t % 2 == 1:
                            split_lo(dve, c + 2, t // 2)

        class OutProject:
            def __init__(self, c):
                self.c = c
                self.resid = sem("op_resid")

            def loads(self, sp):
                for i in range(2):
                    for j in range(2):
                        load_chunk(sp, self.c + 2 * i + j, self.c // 2 + i, j,
                                   w_out, 512 * i + 256 * j)

            def pe_part(self, pe):
                with pe.Fori(0, 2) as i:
                    for t in range(4):
                        if t % 2 == 0:
                            chunk_ready(pe, self.c + 2 * i + t // 2)
                        pe.wait_ge(self.resid, 4 * i + t + 1)
                        gemm(2 * t, t // 2, t % 2, KD, mh, ml)

            def act_part(self, act):
                with act.Fori(0, 2) as i:
                    for j in range(2):
                        split_hi(act, self.c + 2 * i + j + 2, self.c // 2 + i + 1, j)

            def dve_part(self, dve):
                dve.sem_inc(self.resid, 4)
                with dve.Fori(0, 2) as i:
                    for t in range(4):
                        c = self.c + 2 * i + t // 2
                        k = bass.ds(4 * i + t, 1)
                        tile_done(dve, c, t % 2)
                        xk = xT[:, k].rearrange("p o (a b) -> p (o a) b", b=HALF)
                        nc.vector.scalar_tensor_tensor(xk, banks(2 * t), 1.0 / ALPHA, xk, ALU.mult, ALU.add
                                                       ).then_inc(self.resid, 1)
                        if t % 2 == 1:
                            split_lo(dve, c + 2, t // 2)

        x_landed = [sem(f"x_landed{t}") for t in range(5)]
        turn_in = Norm(0, 0, 0, stats=False)
        turn_in.row_ready = lambda pe, t: pe.wait_ge(x_landed[t], 16)
        ffn1 = FFN("ffn1", C_FFN1_UP, ffn1_w_gu, ffn1_w_down)
        ln1 = Norm(0, 0, 1)
        pk = Project("pk", C_KA, 4, stage=turned, nat=k_nat, nat_s=k_nat_s, keep=kaT)
        pv = Project("pv", C_VA, 4, stage=turned, nat=v_nat, nat_s=v_nat_s)
        pq = Project("pq", C_QA, 4, direct=qaT)
        attn = PromptAttention()
        attn_norm = HeadNorm("an", [(o_nat[:, b], P * b, P) for b in range(NB)], sq, DV)
        dec = DecodeAttention()
        split_oa = Split("soa", oaT, oah, oal)
        split_x = Split("sx", xT, xh, xl)
        branch_a = Branch("ba", C_BRANCH_A, W_IN_COLS["ga"], w_branch_a, oah, oal, add=False)
        rq = Project("rq", C_QR, 2, direct=qrT)
        rk = Project("rk", C_KR, 2, stage=rturned, nat=kr_nat, nat_s=kr_nat_s, keep=krT, scale=RK ** -0.5)
        rv = Project("rv", C_VR, 4, stage=rturned, nat=vr_nat, nat_s=vr_nat_s)
        ret = Retention()
        ret_norm = HeadNorm("rn", [(or_nat[:, b], P * b, P) for b in range(NB)] + [(or_s[0:NS], SEQ, NS)], rsq, RV)
        ret_gate = RetGate(C_GR)
        branch_b = Branch("bb", C_BRANCH_B, W_IN_COLS["gb"], w_branch_b, obh, obl, add=True)
        out_proj = OutProject(C_OUT)
        ln2 = Norm(1, 1, 2)
        ffn2 = FFN("ffn2", C_FFN2_UP, ffn2_w_gu, ffn2_w_down, last=True)
        ln3 = Norm(2, 2, 3, back=False)

        att_const = sem("att_const")
        past_const = sem("past_const")
        ret_const = sem("ret_const")
        lam_sums, lam_exp, lam_set, subln_set = sem("lam_sums"), sem("lam_exp"), sem("lam_set"), sem("subln_set")
        k_stored, v_stored = sem("k_stored"), sem("v_stored")
        START_LOADS = 9

        block = ctx.enter_context(nc.Block())

        def const_load(eng, dst, name, signal, rows=P):
            a, n = const_at[name]
            eng.dma_start(dst, const[0:rows, a:a + n]).then_inc(signal, 16)

        def flat(t):
            return t.rearrange("p a b -> p (a b)")

        @block.sync
        def _(sp):
            for t, (t0, n) in enumerate(TOKENS):
                src = x_prompt[0, t0:t0 + n, :] if t < NB else x_sample.rearrange("b t d -> (b t) d")
                sp.dma_start(xn[0:n, t], src).then_inc(x_landed[t], 16)
                if t == 0:
                    const_load(sp, ident[:], "ident", const_landed)
            const_load(sp, ones[:], "ones", const_landed)
            const_load(sp, slope8[:], "slope8", const_landed)
            const_load(sp, map_rows[:], "map_rows", const_landed)
            const_load(sp, kdec[:], "kdec", const_landed)
            const_load(sp, kdec_s[:], "kdec_s", const_landed)
            sp.dma_start(lam_in[:], da_lambda[0:1].broadcast_to([P, 4, DH])).then_inc(const_landed, 16)
            sp.dma_start(subln[:], da_subln_g.rearrange("o d -> d o")).then_inc(const_landed, 16)
            sp.dma_start(pages[0:1], page_table.rearrange("b g -> (b g)").unsqueeze(0)).then_inc(const_landed, 16)
            ffn1.loads(sp)
            sp.wait_ge(ffn1.h_lo, KF)
            ln1.load_params(sp)
            sp.wait_ge(lam_set, 1)
            const_load(sp, flat(s_new[0:NS]), "bias_new", att_const, NS)
            const_load(sp, dist[:], "dist", att_const)
            pk.loads(sp, W_IN_COLS["ka"])
            pv.loads(sp, W_IN_COLS["va"])
            pq.loads(sp, W_IN_COLS["qa"])
            branch_a.loads(sp, 0, 1)
            sp.wait_ge(gemm_done, 2 * C_BRANCH_A + 4)
            sp.wait_ge(attn.scaled, HA * NB + 2)
            const_load(sp, bias_past[:], "bias_past", past_const)
            dec.sp_part(sp)
            branch_a.loads(sp, 1, KD // 2)
            rq.loads(sp, W_IN_COLS["qr"])
            sp.wait_ge(branch_a.prod_done, KD + 2)
            const_load(sp, flat(decay[:]), "decay", ret_const)
            const_load(sp, flat(cross[:]), "cross", ret_const)
            const_load(sp, flat(decay_s[0:NS]), "decay_s", ret_const, NS)
            rk.loads(sp, W_IN_COLS["kr"])
            rv.loads(sp, W_IN_COLS["vr"])
            ret_gate.loads(sp, 0, 1)
            ret.sp_part(sp)
            ret_gate.loads(sp, 1, 2)
            branch_b.loads(sp, 0, KD // 2)
            out_proj.loads(sp)
            sp.wait_ge(branch_b.m_lo, KD)
            ln2.load_params(sp)
            ffn2.loads(sp)
            sp.wait_ge(ffn2.h_lo, KF)
            ln3.load_params(sp)
            for t, (t0, n) in enumerate(TOKENS):
                sp.wait_ge(ln3.biased, ln3.s + t + 1)
                dst = y_prompt[0, t0:t0 + n, :] if t < NB else y_sample.rearrange("b t d -> (b t) d")
                sp.dma_start(dst, xn[0:n, t]).then_inc(out_stored, 16)
            sp.wait_ge(out_stored, 16 * 6)
            sp.wait_ge(k_stored, 32)
            sp.wait_ge(v_stored, 32)
            for stored in ret.s_stored:
                sp.wait_ge(stored, 8 * DEC)

        @block.scalar
        def _(act):
            turn_in.act_part(act)
            act.wait_ge(lam_sums, 2)
            nc.scalar.activation(lam_t[:, 2:4], lam_t[:, 0:2], ACT.Exp).then_inc(lam_exp, 1)
            split_hi(act, 0, 0, 0)
            split_hi(act, 1, 0, 1)
            ffn1.act_part(act)
            ln1.act_part(act)
            pk.act_part(act)
            act.wait_ge(pk.kept, 10)
            pv.act_part(act)
            pq.act_part(act)
            attn.credits_act(act)
            dec.credits_act(act)
            act.wait_ge(k_stored, 32)
            attn.act_part(act)
            act.wait_ge(attn.combined, HA * NB + 2)
            act.wait_ge(attn.o_set, HA * NB + 2)
            attn_norm.act_squares(act)
            act.wait_ge(subln_set, 1)
            attn_norm.act_evict(act, oaT, subln8[:, 0:1])
            dec.act_part(act)
            dec.act_finish(act)
            act.wait_ge(dec.lsum, DEC + 1)
            split_x.act_part(act)
            act.wait_ge(v_stored, 32)
            act.wait_ge(dec.oa_set, 1)
            split_oa.act_part(act)
            branch_a.act_part(act)
            rq.act_part(act)
            rk.act_part(act)
            act.wait_ge(rk.kept, 6)
            rv.act_part(act)
            ret.act_part(act)
            act.wait_ge(ret.s_kept, 1)
            ret_norm.act_squares(act)
            ret_norm.act_evict(act, onT)
            for stored in ret.s_stored:
                act.wait_ge(stored, 8 * DEC)
            ret_gate.act_part(act)
            branch_b.act_part(act)
            out_proj.act_part(act)
            ln2.act_part(act)
            ffn2.act_part(act)
            ln3.act_part(act)

        @block.vector
        def _(dve):
            dve.sem_inc(lo_split, 2)
            turn_in.dve_part(dve)
            dve.wait_ge(const_landed, 16 * START_LOADS)
            nc.vector.memset(lamv[:, 0:1], 1.0)
            for j in range(2):
                nc.vector.tensor_tensor_reduce(lam_in[:, 2 * j], lam_in[:, 2 * j], lam_in[:, 2 * j + 1], 1.0, 0.0,
                                               ALU.mult, ALU.add, lam_t[:, j:j + 1]).then_inc(lam_sums, 1)
            nc.vector.tensor_scalar(subln8[:], subln[:], 1.0 - LAM_INIT, None, ALU.mult).then_inc(subln_set, 1)
            dve.wait_ge(lam_exp, 1)
            nc.vector.scalar_tensor_tensor(lamv[:, 1:2], lam_t[:, 2:3], LAM_INIT, lam_t[:, 3:4], ALU.add, ALU.subtract
                                           ).then_inc(lam_set, 1)
            split_lo(dve, 0, 0)
            split_lo(dve, 1, 1)
            ffn1.dve_part(dve)
            ln1.dve_part(dve)
            pk.dve_part(dve)
            pv.dve_part(dve)
            pq.dve_part(dve)
            attn.credits_dve(dve)
            dec.credits_dve(dve)
            dve.wait_ge(pq.taken, 10)
            dec.dve_setup(dve)
            dve.wait_ge(att_const, 32)
            dec.dve_new(dve)
            dve.wait_ge(k_stored, 32)
            dve.wait_ge(lam_set, 1)
            attn.dve_part(dve)
            attn_norm.dve_scale(dve)
            dve.wait_ge(past_const, 16)
            dve.wait_ge(dec.new_biased, HA)
            dec.dve_part(dve)
            dec.dve_finish(dve)
            split_x.dve_part(dve)
            split_oa.dve_part(dve)
            branch_a.dve_part(dve)
            rq.dve_part(dve)
            rk.dve_part(dve)
            rv.dve_part(dve)
            dve.wait_ge(ret_const, 48)
            ret.dve_part(dve)
            ret_norm.dve_scale(dve)
            ret_gate.dve_part(dve)
            branch_b.dve_part(dve)
            out_proj.dve_part(dve)
            ln2.dve_part(dve)
            ffn2.dve_part(dve)
            ln3.dve_part(dve)

        @block.tensor
        def _(pe):
            pe.sem_inc(gemm_done, 4)
            attn.credits_pe(pe)
            dec.credits_pe(pe)
            for p in (pk, pv, rk, rv):
                pe.sem_inc(p.rows, 2)
            pe.wait_ge(const_landed, 16 * START_LOADS)
            turn_in.pe_part(pe)
            ffn1.pe_part(pe, turn_in.ready)
            pe.wait_ge(ffn1.resid, KD + 4)
            ln1.pe_part(pe)
            ln1.ready(pe)
            pk.pe_part(pe)
            pe.wait_ge(pk.taken, 10)
            pe.wait_ge(pk.stored, 10)
            pv.pe_part(pe)
            pe.wait_ge(pv.taken, 10)
            pq.pe_part(pe)
            pe.wait_ge(pq.taken, 10)
            pe.wait_ge(pv.stored, 10)
            dec.pe_new(pe)
            pe.wait_ge(dec.new_biased, HA)
            attn.pe_part(pe)
            attn_norm.pe_part(pe)
            pe.wait_ge(attn_norm.evicted, NB)
            pe.wait_ge(attn.aT_set, HA * NB + 2)
            pe.wait_ge(attn.o_set, HA * NB + 2)
            dec.pe_part(pe)
            dec.pe_finish(pe)
            split_x.ready(pe)
            split_oa.ready(pe)
            branch_a.pe_part(pe)
            pe.wait_ge(branch_a.sig_done, KD + 2)
            rq.pe_part(pe)
            pe.wait_ge(rq.taken, 6)
            pe.wait_ge(branch_a.prod_done, KD + 2)
            rk.pe_part(pe)
            pe.wait_ge(rk.taken, 6)
            pe.wait_ge(rk.stored, 6)
            rv.pe_part(pe)
            pe.wait_ge(rk.kept, 6)
            pe.wait_ge(rv.stored, 10)
            pe.wait_ge(rv.taken, 10)
            ret.pe_part(pe)
            pe.wait_ge(ret.s_kept, 1)
            ret_norm.pe_part(pe)
            pe.wait_ge(ret.s_new, HR * DEC)
            ret_gate.pe_part(pe)
            pe.wait_ge(ret_norm.evicted, 5)
            pe.wait_ge(ret_gate.o_lo, KD)
            branch_b.pe_part(pe)
            pe.wait_ge(branch_b.m_lo, KD)
            out_proj.pe_part(pe)
            pe.wait_ge(out_proj.resid, KD + 4)
            ln2.pe_part(pe)
            ffn2.pe_part(pe, ln2.ready)
            pe.wait_ge(ffn2.resid, KD + 4)
            ln3.pe_part(pe)

        @block.gpsimd
        def _(pool):
            ln1.pool_part(pool)
            pk.pool_part(pool)
            pk.all_stored(pool)
            pool.dma_start(k_prompt[0, 0].rearrange("(b p) h d -> p b (h d)", p=P), k_nat[:]).then_inc(k_stored, 16)
            pool.dma_start(k_sample[0].rearrange("b t h d -> (b t) (h d)"), k_nat_s[0:NS]).then_inc(k_stored, 16)
            pv.all_stored(pool)
            pool.dma_start(v_prompt[0, 0].rearrange("(b p) h d -> p b (h d)", p=P), v_nat[:]).then_inc(v_stored, 16)
            pool.dma_start(v_sample[0].rearrange("b t h d -> (b t) (h d)"), v_nat_s[0:NS]).then_inc(v_stored, 16)
            pool.wait_ge(pq.taken, 10)
            pool.wait_ge(att_const, 32)
            pool.wait_ge(ln1.biased, ln1.s + 5)
            attn.pool_part(pool)
            pool.wait_ge(gemm_done, 2 * C_BRANCH_A + 4)
            dec.pool_part(pool)
            rk.pool_part(pool)
            rk.all_stored(pool)
            rv.all_stored(pool)
            pool.wait_ge(ret_const, 48)
            ret.pool_part(pool)
            ln2.pool_part(pool)
            ln3.pool_part(pool)


_INS = ["x_prompt", "x_sample", "cache_k", "cache_v", "state_ret", "page_table", "ln_g", "ln_b", "ffn1_w_gu",
        "ffn1_w_down", "w_in", "da_lambda", "da_subln_g", "w_branch_a", "w_branch_b", "w_out", "ffn2_w_gu",
        "ffn2_w_down"]
_OUTS = [(1, SEQ, D), (DEC, TDEC, D), (1, 1, SEQ, HA, 2 * DH), (1, 1, SEQ, HA, DV), (1, 1, HR, RK, RV),
         (1, DEC, TDEC, HA, 2 * DH), (1, DEC, TDEC, HA, DV), (1, DEC, HR, RK, RV)]


def kernel(**inputs):
    import numpy as _np
    import concourse.bacc as _bacc
    from concourse import mybir as _mybir
    from concourse.bass_utils import run_bass_kernel_spmd as _run

    nc = _bacc.Bacc("TRN2", target_bir_lowering=False, num_devices=1)
    arrays, args = {}, []
    for name in _INS:
        arrays[f"in_{name}_dram"] = _np.ascontiguousarray(inputs[name])
    arrays["in_const_dram"] = constants()[1]
    for name, a in arrays.items():
        args.append(nc.dram_tensor(name, a.shape, _mybir.dt.from_np(a.dtype), kind="ExternalInput").ap())
    for i, shape in enumerate(_OUTS):
        args.append(nc.dram_tensor(f"out_{i}_dram", shape, _mybir.dt.float32, kind="ExternalOutput").ap())
    build(nc, *args)
    r = _run(nc, [arrays], core_ids=[0])
    return tuple(r.results[0][f"out_{i}_dram"] for i in range(len(_OUTS)))
```

```python
from contextlib import ExitStack

import numpy as np

import concourse.bass as bass
from concourse import mybir

F32 = mybir.dt.float32
F32R = mybir.dt.float32r
I32 = mybir.dt.int32
ALU = mybir.AluOpType
ACT = mybir.ActivationFunctionType
AX_X = mybir.AxisListType.X
RMAX = bass.bass_isa.ReduceOp.max

P = 128
D = 1024
KD = D // P
SEQ = 512
NB = SEQ // P
DEC, TDEC = 8, 4
NS = DEC * TDEC
T = SEQ + NS
HALF = T // 2
FF = 2816
KF = FF // P
PAST, PAGE = 1024, 128
PAGES = PAST // PAGE
HA, DH, DV = 8, 64, 128
HR, RK, RV = 4, 128, 256
ALPHA = 2.0 ** 0.25
EPS = 1e-5
LAM_INIT = 0.2
MASKED = -1e30
W_IN_COLS = dict(qa=0, ka=1024, va=2048, qr=3072, kr=3584, vr=4096, gr=5120, ga=6144, gb=7168)
TOKENS = [(P * j, P) for j in range(NB)] + [(SEQ, NS)]

FFN_UP, FFN_DOWN = KF, 12
C_FFN1_UP = 0
C_FFN1_DOWN = C_FFN1_UP + FFN_UP
C_KA = C_FFN1_DOWN + FFN_DOWN
C_VA = C_KA + 4
C_QA = C_VA + 4
C_BRANCH_A = C_QA + 4
C_QR = C_BRANCH_A + 8
C_KR = C_QR + 2
C_VR = C_KR + 2
C_GR = C_VR + 4
C_BRANCH_B = C_GR + 4
C_OUT = C_BRANCH_B + 8
C_FFN2_UP = C_OUT + 4
C_FFN2_DOWN = C_FFN2_UP + FFN_UP
C_END = C_FFN2_DOWN + FFN_DOWN


def constants():
    p = np.arange(P)
    slopes = 2.0 ** -(1.0 + np.arange(HA))
    gamma = 1.0 - 2.0 ** (-5.0 - np.arange(HR))
    t = {}
    t["ident"] = np.eye(P)
    t["ones"] = np.ones((P, P))
    u = np.arange(SEQ)[None, :] - (SEQ - P) - p[:, None]
    t["dist"] = np.where(u <= 0, u, MASKED)
    t["slope8"] = np.broadcast_to(8.0 * slopes, (P, HA))
    t["map_rows"] = np.stack([p < DH, p >= DH], 1)
    row = p % (HA * 2 * TDEC)
    rh, rm, rq = row // (2 * TDEC), row // TDEC % 2, row % TDEC
    past = 8.0 * slopes[rh][:, None] * (np.arange(PAST)[None, :] - PAST - rq[:, None])
    d = np.arange(NS)[None, None, :] - TDEC * np.arange(DEC)[None, :, None]
    new = np.where((d >= 0) & (d <= rq[:, None, None]), 8.0 * slopes[rh][:, None, None] * (d - rq[:, None, None]), MASKED)
    t["bias_dec"] = np.concatenate([past, new.reshape(P, -1)], 1)
    own = (np.arange(HA * TDEC)[None, :] == (TDEC * rh + rq)[:, None])
    t["minus_first"] = -1.0 * (own & (rm == 0)[:, None])
    t["minus_second"] = -1.0 * (own & (rm == 1)[:, None])
    i = np.arange(P)
    dd = i[None, None, :] - p[:, None, None]
    t["decay"] = np.where(dd >= 0, gamma[None, :, None] ** np.maximum(dd, 0), 0.0).reshape(P, -1)
    t["cross"] = np.broadcast_to(gamma[:, None] ** (i[None, :] + 1.0), (P, HR, P)).reshape(P, -1)
    t["kdec"] = gamma[None, :] ** (P - 1.0 - p[:, None])
    js = np.arange(NS)
    same = (p[:, None, None] // TDEC == js[None, None, :] // TDEC) & (js[None, None, :] >= p[:, None, None])
    ds = np.maximum(js[None, None, :] - p[:, None, None], 0)
    t["decay_s"] = np.where(same, gamma[None, :, None] ** ds, 0.0).reshape(P, -1)
    own = p[:, None, None] // TDEC == np.arange(DEC)[None, :, None]
    t["kdec_s"] = np.where(own, gamma[None, None, :] ** (TDEC - 1.0 - (p[:, None, None] % TDEC)), 0.0).reshape(P, -1)
    at, parts = {}, []
    n = 0
    for name, a in t.items():
        a = np.asarray(a, np.float32).reshape(P, -1)
        at[name] = (n, a.shape[1])
        n += a.shape[1]
        parts.append(a)
    return at, np.ascontiguousarray(np.concatenate(parts, 1), np.float32)


def build(nc, x_prompt, x_sample, cache_k, cache_v, state_ret, page_table, ln_g, ln_b, ffn1_w_gu,
          ffn1_w_down, w_in, da_lambda, da_subln_g, w_branch_a, w_branch_b, w_out, ffn2_w_gu,
          ffn2_w_down, const, y_prompt, y_sample, k_prompt, v_prompt, ret_state_prompt, k_sample,
          v_sample, ret_state_sample):
    const_at, _ = constants()
    gamma = [1.0 - 2.0 ** (-5.0 - h) for h in range(HR)]

    with ExitStack() as ctx:
        base = 16512

        def at(name, offset, shape, dt=F32):
            return nc.alloc_sbuf_tensor_at(name, [P, *shape], dt, offset=base + offset)

        def sem(name):
            return ctx.enter_context(nc.semaphore(name))

        ps = ctx.enter_context(nc.psum_tensor("ps", [P, 8, 512], F32))

        w_raw = at("w_raw", 0, [2, KD, 256])
        w_hi_t = at("w_hi_t", 16384, [2, KD, 256], F32R)
        w_lo_t = at("w_lo_t", 32768, [2, KD, 256], F32R)
        xT = at("xT", 49152, [KD, T])
        xh = at("xh", 66560, [KD, T], F32R)
        xl = at("xl", 83968, [KD, T], F32R)
        A = 101376
        hh = at("hh", A, [KF, T], F32R)
        hl = at("hl", A + 47872, [KF, T], F32R)
        xn = at("xn", A, [5, D])
        qaT = at("qaT", A, [HA, T])
        kaT = at("kaT", A + 17408, [HA, T])
        v_nat = at("v_nat", A + 34816, [NB, D])
        v_nat_s = at("v_nat_s", A + 51200, [D])
        k_nat = at("k_nat", A + 55296, [NB, D])
        k_nat_s = at("k_nat_s", A + 71680, [D])
        o_nat = at("o_nat", A + 55296, [NB, D])
        s_sb = at("s_sb", A + 71680, [2, 2, 512])
        p_sb = at("p_sb", A + 79872, [2, 2, 512])
        turned = at("turned", A + 79872, [2, T])
        a_sb = at("a_sb", A + 88064, [2, 512])
        aT = at("aT", A + 92160, [2, 512])
        oaT = at("oaT", A, [KD, T])
        oah = at("oah", A + 17408, [KD, T], F32R)
        oal = at("oal", A + 34816, [KD, T], F32R)
        kt_hi = at("kt_hi", 66560, [2, HA, 256], F32R)
        kt_lo = at("kt_lo", 82944, [2, HA, 256], F32R)
        ident_r = at("ident_r", 99328, [P], F32R)
        minus_first = at("minus_first", 99840, [HA * TDEC])
        minus_second = at("minus_second", 99968, [HA * TDEC])
        map_signs = at("map_signs", 100096, [HA * TDEC])
        weights = at("weights", 100224, [HA * TDEC])
        k_page = at("k_page", A + 17408, [4, D])
        v_page = at("v_page", A + 34816, [4, D])
        vn_lo = at("vn_lo", A + 51200, [D], F32R)
        vp_hi = at("vp_hi", A + 55296, [2, D], F32R)
        vp_lo = at("vp_lo", A + 63488, [2, D], F32R)
        p_s = at("p_s", A + 71680, [PAST + NS])
        bias_stage = at("bias_stage", A + 71680, [PAST + DEC * NS])
        o_rows = at("o_rows", A + 76800, [D])
        pT = at("pT", A + 80896, [PAGES + 1, P], F32R)
        q_stat = at("q_stat", A + 85504, [1152], F32R)
        vn_hi = at("vn_hi", A + 90112, [D], F32R)
        dec_o = at("dec_o", A + 17408, [2, 256])
        dec_l = at("dec_l", A + 19456, [2, 256])
        sq = at("sq", A + 79872, [2, D])
        mT = at("mT", A, [KD, T])
        mh = at("mh", A + 52224, [KD, T], F32R)
        ml = at("ml", A + 69632, [KD, T], F32R)
        R = A + 17408
        qrT = at("qrT", R, [HR, T])
        krT = at("krT", R + 8704, [HR, T])
        vr_nat = at("vr_nat", R + 17408, [NB, D])
        vr_nat_s = at("vr_nat_s", R + 33792, [D])
        kr_nat = at("kr_nat", R + 37888, [NB, HR * RK])
        kr_nat_s = at("kr_nat_s", R + 46080, [HR * RK])
        rturned = at("rturned", R + 48128, [2, T])
        state = at("state", R + 52480, [2, D])
        or_s = at("or_s", R + 58368, [D])
        or_nat = at("or_nat", R + 62464, [NB, D])
        rsq = at("rsq", R, [2, D])
        st_in = at("st_in", R + 17408, [2, D])
        st_out = at("st_out", R + 25600, [2, D])
        kw_s = at("kw_s", R + 37888, [2, HR * RK])
        onT = at("onT", A + 52224, [KD, T])
        obh = at("obh", A + 17408, [KD, T], F32R)
        obl = at("obl", A + 34816, [KD, T], F32R)
        C = A + 96256
        ident = at("ident", C, [P])
        ones = at("ones", C + 512, [P])
        M = C + 1024
        gated = at("gated", M, [2, T])
        prod = at("prod", M + 4352, [2, T])
        ln_gain = at("ln_gain", M, [D])
        ln_bias = at("ln_bias", M + 4096, [D])
        bias8 = at("bias8", M, [2, 512])
        q_stage = at("q_stage", M + 4096, [2, 2, P])
        qs_hi = at("qs_hi", M + 6144, [HA, NS], F32R)
        qs_lo = at("qs_lo", M + 7168, [HA, NS], F32R)
        bias_r = at("bias_r", M, [PAST + DEC * NS], F32R)
        decay = at("decay", M, [HR, P])
        cross = at("cross", M + 2048, [HR, P])
        scT = at("scT", M + 4096, [2, HR * P])
        decay_s = at("decay_s", M + 8192, [HR, NS])
        kn_hi = at("kn_hi", C + 9728, [HA, NS], F32R)
        kn_lo = at("kn_lo", C + 10752, [HA, NS], F32R)
        dist = at("dist", C + 11776, [512])
        lam_in = at("lam_in", C + 9728, [4, DH])
        qm = at("qm", C + 9728, [DEC, HR, NS])
        qx = at("qx", C + 9728, [2, HR, P])      
        small = at("small", C + 13824, [240])
        pages = at("pages", C + 14784, [DEC * PAGES], I32)
        col = {}
        used = [0]

        def tiny(name, n):
            a = used[0]
            used[0] += n
            assert used[0] <= 240
            col[name] = small[:, a:a + n]
            return col[name]

        bn = tiny("bn", 60)
        mv = tiny("mv", 10)
        sd = tiny("sd", 5)
        rstd = tiny("rstd", 5)
        slope8 = tiny("slope8", HA)
        lamv = tiny("lamv", 2)
        map_rows = tiny("map_rows", 2)
        lam_t = tiny("lam_t", 4)
        subln = tiny("subln", 1)
        subln8 = tiny("subln8", 1)
        nmax = tiny("nmax", 4)
        rsum = tiny("rsum", 4)
        rr = tiny("rr", 4)
        ss = bn[:, 0:32]
        ssd = tiny("ssd", 32)
        srs = tiny("srs", 32)
        kdec = tiny("kdec", HR)
        kdec_s = tiny("kdec_s", DEC * HR)

        raw_landed = [sem(f"raw_landed{j}") for j in range(2)]
        hi_split = sem("hi_split")
        lo_split = sem("lo_split")
        gemm_done = sem("gemm_done")
        const_landed = sem("const_landed")
        out_stored = sem("out_stored")

        def score_ps(row):
            return ps[row:row + 64, 2:5, :].rearrange("p a b -> p (a b)")[:, 0:PAST + NS]

        def load_chunk(sp, c, half, j, w, col, row=0, nk=KD):
            sp.wait_ge(lo_split, c + 1)
            src = w[0, row:row + nk * P, :].rearrange("(k p) n -> p k n", p=P)[:, :, bass.ds(col, 256)]
            sp.dma_start(w_raw[:, j, 0:nk], src).then_inc(raw_landed[j], 16)

        def split_hi(act, c, half, j, nk=KD):
            act.wait_ge(raw_landed[j], 16 * half + 16)
            act.wait_ge(gemm_done, 2 * c + 2)
            nc.scalar.copy(w_hi_t[:, j, 0:nk], w_raw[:, j, 0:nk]).then_inc(hi_split, 1)

        def split_lo(dve, c, j, nk=KD):
            dve.wait_ge(hi_split, c + 1)
            nc.vector.tensor_tensor(w_lo_t[:, j, 0:nk], w_raw[:, j, 0:nk], w_hi_t[:, j, 0:nk].bitcast(F32),
                                    ALU.subtract).then_inc(lo_split, 1)

        def chunk_ready(pe, c):
            pe.wait_ge(lo_split, c + 3)

        def gemm(bank, j, n, nk, mh_, ml_, k0=0, start=True, stop=True):
            for k in range(nk):
                w_cols = slice(n * P, n * P + P)
                for pas, (w, m) in enumerate(((w_hi_t, mh_), (w_hi_t, ml_), (w_lo_t, mh_))):
                    for half in range(2):
                        mm = nc.tensor.matmul(ps[:, bank + half, 0:HALF], w[:, j, k, w_cols],
                                              m[:, k0 + k, half * HALF:half * HALF + HALF],
                                              start=start and k == 0 and pas == 0,
                                              stop=stop and k == nk - 1 and pas == 2)
            mm.then_inc(gemm_done, 1)

        def tile_done(eng, c, n):
            eng.wait_ge(gemm_done, 2 * c + n + 5)

        def banks(b):
            return ps[:, b:b + 2, 0:HALF]

        def halves(tile):
            return tile.rearrange("p (a b) -> p a b", b=HALF)

        class FFN:
            def __init__(self, tag, c_up, w_gu, w_down, last=False):
                self.c, self.gu, self.down, self.last = c_up, w_gu, w_down, last
                self.silu_done = sem(f"{tag}_silu_done")
                self.prod_done = sem(f"{tag}_prod_done")
                self.h_hi = sem(f"{tag}_h_hi")
                self.h_lo = sem(f"{tag}_h_lo")
                self.resid = sem(f"{tag}_resid")

            def loads(self, sp):
                c = self.c
                with sp.Fori(0, KF // 2) as i:
                    for j in range(2):
                        load_chunk(sp, c + 2 * i + j, c // 2 + i, j,
                                   self.gu, 256 * i + FF * j)
                c += FFN_UP
                with sp.Fori(0, 2) as q:
                    for m in range(6):
                        r, s = m // 3, m % 3
                        load_chunk(sp, c + 6 * q + m, c // 2 + 3 * q + m // 2, m % 2,
                                   self.down, 512 * q + 256 * r, 8 * s * P, [8, 8, 6][s])

            def pe_part(self, pe, ready):
                ready(pe)
                c = self.c
                with pe.Fori(0, KF // 2) as i:
                    for j in range(2):
                        chunk_ready(pe, c + 2 * i + j)
                        for n in range(2):
                            pe.wait_ge(self.prod_done if j else self.silu_done, 2 * i + n + 1)
                            gemm(4 * j + 2 * n, j, n, KD, xh, xl)
                c += FFN_UP
                pe.wait_ge(self.h_lo, KF)
                with pe.Fori(0, 2) as q:
                    for r in range(2):
                        for s in range(3):
                            m = 3 * r + s
                            chunk_ready(pe, c + 6 * q + m)
                            for n in range(2):
                                if s == 0:
                                    pe.wait_ge(self.resid, 4 * q + 2 * r + n + 1)
                                gemm(4 * r + 2 * n, m % 2, n, [8, 8, 6][s], hh, hl, 8 * s, s == 0, s == 2)

            def act_part(self, act):
                c = self.c
                act.sem_inc(self.silu_done, 2)
                with act.Fori(0, KF // 2) as i:
                    for n in range(2):
                        tile_done(act, c + 2 * i, n)
                        act.wait_ge(self.prod_done, 2 * i + n + 1)
                        nc.scalar.activation(halves(gated[:, n]), banks(2 * n), ACT.Silu).then_inc(self.silu_done, 1)
                    split_hi(act, c + 2 * i + 2, c // 2 + i + 1, 0)
                    for n in range(2):
                        act.wait_ge(self.prod_done, 2 * i + n + 3)
                        nc.scalar.copy(hh[:, bass.ds(2 * i + n, 1)], prod[:, n:n + 1]).then_inc(self.h_hi, 1)
                    split_hi(act, c + 2 * i + 3, c // 2 + i + 1, 1)
                c += FFN_UP
                for q in range(2):
                    for m in range(6):
                        nxt = 6 * q + m + 2
                        if not (self.last and nxt >= FFN_DOWN):
                            split_hi(act, c + nxt, (c + nxt) // 2, m % 2, 6 if m % 3 == 0 else KD)

            def dve_part(self, dve):
                c = self.c
                dve.sem_inc(self.prod_done, 2)
                with dve.Fori(0, KF // 2) as i:
                    split_lo(dve, c + 2 * i + 2, 0)
                    for n in range(2):
                        tile_done(dve, c + 2 * i + 1, n)
                        dve.wait_ge(self.silu_done, 2 * i + n + 3)
                        nc.vector.tensor_tensor(halves(prod[:, n]), banks(4 + 2 * n), halves(gated[:, n]),
                                                ALU.mult).then_inc(self.prod_done, 1)
                        dve.wait_ge(self.h_hi, 2 * i + n + 1)
                        nc.vector.tensor_tensor(hl[:, bass.ds(2 * i + n, 1)], prod[:, n:n + 1],
                                                hh[:, bass.ds(2 * i + n, 1)].bitcast(F32),
                                                ALU.subtract).then_inc(self.h_lo, 1)
                    split_lo(dve, c + 2 * i + 3, 1)
                c += FFN_UP
                dve.sem_inc(self.resid, 4)
                for q in range(2):
                    for m in range(6):
                        nxt = 6 * q + m + 2
                        r, s = m // 3, m % 3
                        if s == 2:
                            for n in range(2):
                                tile_done(dve, c + 6 * q + m, n)
                                k = 4 * q + 2 * r + n
                                nc.vector.scalar_tensor_tensor(halves(xT[:, k]), banks(4 * r + 2 * n), 0.5 / ALPHA,
                                                               halves(xT[:, k]), ALU.mult, ALU.add
                                                               ).then_inc(self.resid, 1)
                        if not (self.last and nxt >= FFN_DOWN):
                            split_lo(dve, c + nxt, m % 2, 6 if s == 0 else KD)

        class Norm:

            params = sem("ln_params")
            rows = sem("ln_rows")
            bn = sem("ln_bn")
            mean = sem("ln_mean")
            var = sem("ln_var")
            sd = sem("ln_sd")
            rs = sem("ln_rs")
            normed = sem("ln_normed")
            gained = sem("ln_gained")
            biased = sem("ln_biased")
            turned = sem("ln_turned")
            x_hi = sem("ln_x_hi")
            x_lo = sem("ln_x_lo")

            def __init__(self, index, stats_before, backs_before, stats=True, back=True):
                self.index, self.stats, self.back = index, stats, back
                self.s, self.b = 5 * stats_before, 5 * backs_before

            def back_ps(self, t):
                b, n = 4 + 2 * (t % 2), TOKENS[t][1]
                return ps[:, b:b + 2, :].rearrange("p a (k c) -> p (a k) c", c=P)[:, :, 0:n]

            def load_params(self, sp):
                for src, dst in ((ln_g, ln_gain), (ln_b, ln_bias)):
                    sp.dma_start(dst[:], src[0, self.index:self.index + 1, :].broadcast_to([P, D])
                                 ).then_inc(self.params, 16)

            def row_ready(self, pe, t):
                pe.wait_ge(self.biased, self.s + t + 1)

            def pe_part(self, pe):
                def to_rows(t):
                    if t >= 2:
                        pe.wait_ge(self.normed, self.s + t - 1)
                    t0, n = TOKENS[t]
                    for k in range(KD):
                        mm = nc.tensor.transpose(ps[0:n, 2 * (t % 2) + k // 4, (k % 4) * P:(k % 4) * P + P],
                                                 xT[:, k, t0:t0 + n], ident[:])
                    mm.then_inc(self.rows, 1)

                def to_channels(t):
                    if t >= 2:
                        pe.wait_ge(self.x_hi, self.b + t - 1)
                    self.row_ready(pe, t)
                    n = TOKENS[t][1]
                    for k in range(KD):
                        mm = nc.tensor.transpose(ps[:, 4 + 2 * (t % 2) + k // 4, (k % 4) * P:(k % 4) * P + n],
                                                 xn[0:n, t, k * P:k * P + P], ident[0:n, 0:n])
                    mm.then_inc(self.turned, 1)

                if self.stats:
                    to_rows(0)
                    to_rows(1)
                for t in range(5):
                    if self.stats and 2 <= t + 1 < 5:
                        to_rows(t + 1)
                    if self.back:
                        to_channels(t)

            def ready(self, eng):
                eng.wait_ge(self.x_lo, self.b + 5)

            def act_part(self, act):
                def sqrt(t):
                    n = TOKENS[t][1]
                    act.wait_ge(self.var, self.s + t + 1)
                    nc.scalar.activation(sd[0:n, t:t + 1], mv[0:n, 2 * t + 1:2 * t + 2], ACT.Sqrt
                                         ).then_inc(self.sd, 1)

                def evict(t):
                    t0, n = TOKENS[t]
                    act.wait_ge(self.turned, self.b + t + 1)
                    nc.scalar.copy(xT[:, :, t0:t0 + n], self.back_ps(t))
                    nc.scalar.copy(xh[:, :, t0:t0 + n], self.back_ps(t)).then_inc(self.x_hi, 1)

                if self.stats:
                    sqrt(0)
                for t in range(5):
                    if self.stats and t + 1 < 5:
                        sqrt(t + 1)
                    if self.back:
                        evict(t)

            def dve_part(self, dve):
                def stats(t):
                    n = TOKENS[t][1]
                    m = slice(2 * t, 2 * t + 2)
                    v = slice(2 * t + 1, 2 * t + 2)
                    dve.wait_ge(self.rows, self.s + t + 1)
                    for a in range(2):
                        nc.vector.bn_stats(bn[0:n, 12 * t + 6 * a:12 * t + 6 * a + 6],
                                           ps[0:n, 2 * (t % 2) + a, :]).then_inc(self.bn, 1)
                    dve.wait_ge(self.bn, 2 * (self.s + t + 1))
                    nc.vector.bn_aggr(mv[0:n, m], bn[0:n, 12 * t:12 * t + 12]).then_inc(self.mean, 1)
                    dve.wait_ge(self.mean, self.s + t + 1)
                    nc.vector.tensor_scalar(mv[0:n, v], mv[0:n, v], EPS / ALPHA ** 2, None, ALU.add
                                            ).then_inc(self.var, 1)

                def norm(t):
                    n = TOKENS[t][1]
                    dve.wait_ge(self.sd, self.s + t + 1)
                    nc.vector.reciprocal(rstd[0:n, t:t + 1], sd[0:n, t:t + 1]).then_inc(self.rs, 1)
                    dve.wait_ge(self.rs, self.s + t + 1)
                    nc.vector.tensor_scalar(xn[0:n, t], ps[0:n, 2 * (t % 2):2 * (t % 2) + 2, :].rearrange("p a b -> p (a b)"),
                                            mv[0:n, 2 * t:2 * t + 1], rstd[0:n, t:t + 1],
                                            ALU.subtract, ALU.mult).then_inc(self.normed, 1)

                def low(t):
                    t0, n = TOKENS[t]
                    dve.wait_ge(self.x_hi, self.b + t + 1)
                    nc.vector.tensor_tensor(xl[:, :, t0:t0 + n], xT[:, :, t0:t0 + n],
                                            xh[:, :, t0:t0 + n].bitcast(F32), ALU.subtract).then_inc(self.x_lo, 1)

                if self.stats:
                    stats(0)
                for t in range(5):
                    if self.stats:
                        if t + 1 < 5:
                            stats(t + 1)
                        norm(t)
                    if self.back and t >= 1:
                        low(t - 1)
                if self.back:
                    low(4)

            def pool_part(self, pool):
                pool.wait_ge(self.params, 32 * (self.s // 5 + 1))
                for t in range(5):
                    n = TOKENS[t][1]
                    pool.wait_ge(self.normed, self.s + t + 1)
                    nc.gpsimd.tensor_tensor(xn[0:n, t], xn[0:n, t], ln_gain[0:n], ALU.mult).then_inc(self.gained, 1)
                    pool.wait_ge(self.gained, self.s + t + 1)
                    nc.gpsimd.tensor_tensor(xn[0:n, t], xn[0:n, t], ln_bias[0:n], ALU.add).then_inc(self.biased, 1)

        class Project:

            def __init__(self, tag, c, n_chunks, stage=None, nat=None, nat_s=None, keep=None, direct=None, scale=1.0):
                self.c, self.rounds = c, n_chunks // 2
                self.stage, self.nat, self.nat_s, self.keep, self.direct = stage, nat, nat_s, keep, direct
                self.scale = scale
                self.tiles = 2 * n_chunks
                self.taken = sem(f"{tag}_taken")
                if nat is not None:
                    self.rows = sem(f"{tag}_rows")
                    self.stored = sem(f"{tag}_stored")
                if keep is not None:
                    self.kept = sem(f"{tag}_kept")

            def loads(self, sp, col):
                for i in range(self.rounds):
                    for j in range(2):
                        load_chunk(sp, self.c + 2 * i + j, self.c // 2 + i, j,
                                   w_in, col + 512 * i + 256 * j)

            def pe_part(self, pe):
                def turn(i, t):
                    u = 4 * i + t
                    pe.wait_ge(self.taken, u + 3)
                    pe.wait_ge(self.stored, u + 1)
                    b = 4 + 2 * (t % 2)
                    for blk in range(NB):
                        nc.tensor.transpose(ps[:, b, blk * P:blk * P + P], self.stage[:, t % 2, blk * P:blk * P + P],
                                            ident[:])
                    nc.tensor.transpose(ps[0:NS, b + 1, 0:P], self.stage[:, t % 2, SEQ:T], ident[:]
                                        ).then_inc(self.rows, 1)

                with pe.Fori(0, self.rounds) as i:
                    for t in range(4):
                        if t % 2 == 0:
                            chunk_ready(pe, self.c + 2 * i + t // 2)
                        pe.wait_ge(self.taken, 4 * i + t + 1)
                        gemm(2 * (t % 2), t // 2, t % 2, KD, xh, xl)
                        if self.nat is not None and t > 0:
                            turn(i, t - 1)
                    if self.nat is not None:
                        turn(i, 3)

            def act_part(self, act):
                act.sem_inc(self.taken, 2)
                with act.Fori(0, self.rounds) as i:
                    for t in range(4):
                        c = self.c + 2 * i + t // 2
                        tile_done(act, c, t % 2)
                        if self.nat is not None:
                            act.wait_ge(self.rows, 4 * i + t + 1)
                            if self.keep is not None:
                                act.wait_ge(self.kept, 4 * i + t + 1)
                            dst = self.stage[:, t % 2:t % 2 + 1]
                        else:
                            dst = self.direct[:, bass.ds(4 * i + t, 1)]
                        nc.scalar.mul(dst.rearrange("p o (a b) -> p (o a) b", b=HALF), banks(2 * (t % 2)), self.scale
                                      ).then_inc(self.taken, 1)
                        if t % 2 == 1:
                            split_hi(act, c + 2, self.c // 2 + i + 1, t // 2)

            def dve_part(self, dve):
                if self.nat is not None:
                    dve.sem_inc(self.stored, 2)
                with dve.Fori(0, self.rounds) as i:
                    for t in range(4):
                        c = self.c + 2 * i + t // 2
                        if t % 2 == 1:
                            split_lo(dve, c + 2, t // 2)
                        if self.nat is not None:
                            b = 4 + 2 * (t % 2)
                            dve.wait_ge(self.rows, 4 * i + t + 3)
                            nc.vector.tensor_copy(self.nat[:, :, bass.ds(512 * i + P * t, P)],
                                                  ps[:, b, :].rearrange("p (a b) -> p a b", b=P))
                            nc.vector.tensor_copy(self.nat_s[0:NS, bass.ds(512 * i + P * t, P)],
                                                  ps[0:NS, b + 1, 0:P]).then_inc(self.stored, 1)

            def pool_part(self, pool):
                pool.sem_inc(self.kept, 2)
                with pool.Fori(0, self.rounds) as i:
                    for t in range(4):
                        pool.wait_ge(self.taken, 4 * i + t + 3)
                        nc.gpsimd.tensor_copy(self.keep[:, bass.ds(4 * i + t, 1)], self.stage[:, t % 2:t % 2 + 1]
                                              ).then_inc(self.kept, 1)

            def all_stored(self, eng):
                eng.wait_ge(self.stored, self.tiles + 2)

        class Branch:
            def __init__(self, tag, c, col, w, oh, ol, add):
                self.c, self.col, self.w, self.oh, self.ol, self.add = c, col, w, oh, ol, add
                self.sig_done = sem(f"{tag}_sig_done")
                self.prod_done = sem(f"{tag}_prod_done")
                if add:
                    self.merged = sem(f"{tag}_merged")
                    self.m_hi = sem(f"{tag}_m_hi")
                    self.m_lo = sem(f"{tag}_m_lo")

            def loads(self, sp, first, last):
                for i in range(first, last):
                    load_chunk(sp, self.c + 2 * i, self.c // 2 + i, 0,
                               w_in, self.col + 256 * i)
                    load_chunk(sp, self.c + 2 * i + 1, self.c // 2 + i, 1,
                               self.w, 256 * i)

            def pe_part(self, pe):
                with pe.Fori(0, KD // 2) as i:
                    for j in range(2):
                        chunk_ready(pe, self.c + 2 * i + j)
                        for n in range(2):
                            pe.wait_ge(self.prod_done if j else self.sig_done, 2 * i + n + 1)
                            gemm(4 * j + 2 * n, j, n, KD, self.oh if j else xh, self.ol if j else xl)

            def act_part(self, act):
                act.sem_inc(self.sig_done, 2)
                with act.Fori(0, KD // 2) as i:
                    for n in range(2):
                        tile_done(act, self.c + 2 * i, n)
                        act.wait_ge(self.prod_done, 2 * i + n + 1)
                        nc.scalar.activation(halves(gated[:, n]), banks(2 * n), ACT.Sigmoid).then_inc(self.sig_done, 1)
                    split_hi(act, self.c + 2 * i + 2, self.c // 2 + i + 1, 0)
                    if self.add:
                        for n in range(2):
                            act.wait_ge(self.merged, 2 * i + n + 1)
                            nc.scalar.copy(mh[:, bass.ds(2 * i + n, 1)], prod[:, n:n + 1]).then_inc(self.m_hi, 1)
                    split_hi(act, self.c + 2 * i + 3, self.c // 2 + i + 1, 1)

            def dve_part(self, dve):
                dve.sem_inc(self.prod_done, 2)
                with dve.Fori(0, KD // 2) as i:
                    split_lo(dve, self.c + 2 * i + 2, 0)
                    for n in range(2):
                        k = bass.ds(2 * i + n, 1)
                        tile_done(dve, self.c + 2 * i + 1, n)
                        dve.wait_ge(self.sig_done, 2 * i + n + 3)
                        dst = prod[:, n:n + 1] if self.add else mT[:, k]
                        nc.vector.tensor_tensor(dst.rearrange("p o (a b) -> p (o a) b", b=HALF), banks(4 + 2 * n),
                                                halves(gated[:, n]), ALU.mult).then_inc(self.prod_done, 1)
                        if self.add:
                            dve.wait_ge(self.prod_done, 2 * i + n + 3)
                            nc.vector.tensor_tensor(prod[:, n:n + 1], prod[:, n:n + 1], mT[:, k], ALU.add
                                                    ).then_inc(self.merged, 1)
                            dve.wait_ge(self.m_hi, 2 * i + n + 1)
                            nc.vector.tensor_tensor(ml[:, k], prod[:, n:n + 1], mh[:, k].bitcast(F32), ALU.subtract
                                                    ).then_inc(self.m_lo, 1)
                    split_lo(dve, self.c + 2 * i + 3, 1)

        class HeadNorm:
            sq_done = sem("hn_sq_done")
            summed = sem("hn_summed")
            guarded = sem("hn_guarded")
            sd = sem("hn_sd")
            rs = sem("hn_rs")
            scaled = sem("hn_scaled")
            turned = sem("hn_turned")
            evicted = sem("hn_evicted")

            def __init__(self, b0, p0, blocks, squares, n):
                self.b0, self.p0 = b0, p0
                self.blocks, self.squares, self.n, self.g = blocks, squares, n, D // n
                full = sum(n == P for _, _, n in blocks)
                self.parts = [(P, slice(0, full * self.g))]
                if full < len(blocks):
                    self.parts.append((NS, slice(full * self.g, (full + 1) * self.g)))

            def act_squares(self, act):
                for b, (src, _, r) in enumerate(self.blocks):
                    act.wait_ge(self.summed, self.b0 + b + 1)
                    nc.scalar.activation(self.squares[0:r, b % 2], src, ACT.Square).then_inc(self.sq_done, 1)
                for p, (r, c) in enumerate(self.parts):
                    act.wait_ge(self.guarded, self.p0 + p + 1)
                    nc.scalar.activation(ssd[0:r, c], ss[0:r, c], ACT.Sqrt).then_inc(self.sd, 1)

            def dve_scale(self, dve):
                g, n = self.g, self.n
                for b, (_, _, r) in enumerate(self.blocks):
                    dve.wait_ge(self.sq_done, self.b0 + b + 1)
                    nc.vector.tensor_reduce(ss[0:r, b * g:b * g + g],
                                            self.squares[0:r, b % 2].rearrange("p (h d) -> p h d", d=n), AX_X, ALU.add
                                            ).then_inc(self.summed, 1)
                dve.wait_ge(self.summed, self.b0 + len(self.blocks) + 2)
                for r, c in self.parts:
                    nc.vector.tensor_scalar(ss[0:r, c], ss[0:r, c], 1.0 / n, EPS, ALU.mult, ALU.add
                                            ).then_inc(self.guarded, 1)
                for p, (r, c) in enumerate(self.parts):
                    dve.wait_ge(self.sd, self.p0 + p + 1)
                    nc.vector.reciprocal(srs[0:r, c], ssd[0:r, c]).then_inc(self.rs, 1)
                dve.wait_ge(self.rs, self.p0 + len(self.parts))
                for b, (src, _, r) in enumerate(self.blocks):
                    rows = src.rearrange("p (h d) -> p h d", d=n)
                    nc.vector.tensor_tensor(rows, rows, srs[0:r, b * g:b * g + g].unsqueeze(2).broadcast_to([r, g, n]),
                                            ALU.mult).then_inc(self.scaled, 1)

            def pe_part(self, pe):
                for b, (src, _, r) in enumerate(self.blocks):
                    pe.wait_ge(self.scaled, self.b0 + b + 1)
                    if b >= 2:
                        pe.wait_ge(self.evicted, self.b0 + b - 1)
                    for k in range(KD):
                        mm = nc.tensor.transpose(ps[:, 2 * (b % 2) + k // 4, (k % 4) * P:(k % 4) * P + r],
                                                 src[:, k * P:k * P + P], ident[0:r, 0:r])
                    mm.then_inc(self.turned, 1)

            def all_evicted(self, eng):
                eng.wait_ge(self.evicted, self.b0 + len(self.blocks))

            def act_evict(self, act, dst, scale=1.0):
                for b, (_, t0, r) in enumerate(self.blocks):
                    act.wait_ge(self.turned, self.b0 + b + 1)
                    src = ps[:, 2 * (b % 2):2 * (b % 2) + 2, :].rearrange("p a (k c) -> p (a k) c", c=P)[:, :, 0:r]
                    nc.scalar.mul(dst[:, :, t0:t0 + r], src, scale).then_inc(self.evicted, 1)

        class Split:
            def __init__(self, tag, src, hi, lo):
                self.src, self.hi, self.lo = src, hi, lo
                self.hi_done, self.lo_done = sem(f"{tag}_hi_done"), sem(f"{tag}_lo_done")

            def act_part(self, act):
                for k in range(0, KD, 2):
                    nc.scalar.copy(self.hi[:, k:k + 2], self.src[:, k:k + 2]).then_inc(self.hi_done, 1)

            def dve_part(self, dve):
                for k in range(0, KD, 2):
                    dve.wait_ge(self.hi_done, k // 2 + 1)
                    nc.vector.tensor_tensor(self.lo[:, k:k + 2], self.src[:, k:k + 2],
                                            self.hi[:, k:k + 2].bitcast(F32), ALU.subtract).then_inc(self.lo_done, 1)

            def ready(self, pe):
                pe.wait_ge(self.lo_done, KD // 2)

        class PromptAttention:
            def __init__(self):
                self.q_staged = sem("pa_q_staged")
                self.bias_set = sem("pa_bias_set")
                self.scored = sem("pa_scored")
                self.scaled = sem("pa_scaled")
                self.exped = sem("pa_exped")
                self.recip = sem("pa_recip")
                self.lammed = sem("pa_lammed")
                self.second = sem("pa_second")
                self.combined = sem("pa_combined")
                self.turned = sem("pa_turned")
                self.aT_set = sem("pa_aT_set")
                self.pv = sem("pa_pv")
                self.o_set = sem("pa_o_set")

            def keys(self, i):
                return P * (i + 1)

            def pool_unit(self, pool, i, h, s, u):
                pool.wait_ge(self.scored, u + 1)
                nc.gpsimd.tensor_tensor(q_stage[:, s], qaT[:, h, P * i:P * i + P].broadcast_to([P, 2, P]),
                                        map_rows[:].unsqueeze(2).broadcast_to([P, 2, P]), ALU.mult
                                        ).then_inc(self.q_staged, 1)
                n = self.keys(i)
                pool.wait_ge(self.scaled, u + 1)
                nc.gpsimd.tensor_tensor(bias8[:, s:s + 1, 0:n], dist[:, SEQ - n:SEQ].unsqueeze(1),
                                        slope8[:, h].unsqueeze(2).broadcast_to([P, 1, n]), ALU.mult
                                        ).then_inc(self.bias_set, 1)

            def pool_part(self, pool):
                for i in range(NB):
                    with pool.Fori(0, HA // 2) as hp:
                        for s in range(2):
                            self.pool_unit(pool, i, bass.ds(2 * hp + s, 1), s, HA * i + 2 * hp + s)

            def scores(self, pe, i, h, s, u):
                n = self.keys(i)
                pe.wait_ge(self.q_staged, u + 1)
                pe.wait_ge(self.scaled, u + 1)
                for m in range(2):
                    mm = nc.tensor.matmul(ps[:, 2 * s + m, 0:n], q_stage[:, s, m], kaT[:, h, 0:n], start=True, stop=True)
                mm.then_inc(self.scored, 1)

            def turn(self, pe, i, s, u):
                pe.wait_ge(self.combined, u + 3)
                pe.wait_ge(self.aT_set, u + 1)
                for j in range(i + 1):
                    mm = nc.tensor.transpose(ps[:, 4 + s, P * j:P * j + P], a_sb[:, s, P * j:P * j + P], ident[:])
                mm.then_inc(self.turned, 1)

            def values(self, pe, i, h, s, u):
                pe.wait_ge(self.aT_set, u + 3)
                pe.wait_ge(self.o_set, u + 1)
                for j in range(i + 1):
                    mm = nc.tensor.matmul(ps[:, 6 + s, 0:DV], aT[:, s, P * j:P * j + P],
                                          v_nat[:, j, bass.ds(h * DV, DV)], start=j == 0, stop=j == i)
                mm.then_inc(self.pv, 1)

            def pe_part(self, pe):
                def head(h):
                    return bass.ds(h, 1)
                self.scores(pe, 0, head(0), 0, 0)
                self.scores(pe, 0, head(1), 1, 1)
                for i in range(NB):
                    u0 = HA * i
                    with pe.Fori(0, HA // 2 - 1) as hp:
                        for s in range(2):
                            self.turn(pe, i, s, u0 + 2 * hp + s)
                            self.scores(pe, i, head(2 * hp + s + 2), s, u0 + 2 * hp + s + 2)
                            self.values(pe, i, 2 * hp + s, s, u0 + 2 * hp + s)
                    for s in range(2):
                        self.turn(pe, i, s, u0 + HA - 2 + s)
                        if i + 1 < NB:
                            self.scores(pe, i + 1, head(s), s, u0 + HA + s)
                        self.values(pe, i, HA - 2 + s, s, u0 + HA - 2 + s)

            def scale(self, dve, i, s, u):
                n = self.keys(i)
                dve.wait_ge(self.scored, u + 3)
                dve.wait_ge(self.bias_set, u + 1)
                dve.wait_ge(self.exped, u + 1)
                nc.vector.memset(rsum[:, 2 * s:2 * s + 2], 0.0)
                for m in range(2):
                    ins = nc.vector.tensor_tensor_reduce(s_sb[:, s, m, 0:n], ps[:, 2 * s + m, 0:n], bias8[:, s, 0:n],
                                                         -DH ** -0.5, -MASKED, ALU.add, ALU.min,
                                                         nmax[:, 2 * s + m:2 * s + m + 1])
                ins.then_inc(self.scaled, 1)

            def combine(self, dve, i, s, u):
                n = self.keys(i)
                r = slice(2 * s, 2 * s + 2)
                dve.wait_ge(self.exped, u + 3)
                nc.vector.reciprocal(rr[:, r], rsum[:, r]).then_inc(self.recip, 1)
                dve.wait_ge(self.recip, u + 1)
                nc.vector.tensor_tensor(rr[:, r], rr[:, r], lamv[:], ALU.mult).then_inc(self.lammed, 1)
                dve.wait_ge(self.lammed, u + 1)
                nc.vector.tensor_scalar(p_sb[:, s, 1, 0:n], p_sb[:, s, 1, 0:n], rr[:, 2 * s + 1:2 * s + 2], None,
                                        ALU.mult).then_inc(self.second, 1)
                dve.wait_ge(self.second, u + 1)
                dve.wait_ge(self.turned, u + 1)
                nc.vector.scalar_tensor_tensor(a_sb[:, s, 0:n], p_sb[:, s, 0, 0:n], rr[:, 2 * s:2 * s + 1],
                                               p_sb[:, s, 1, 0:n], ALU.mult, ALU.subtract).then_inc(self.combined, 1)

            def dve_part(self, dve):
                self.scale(dve, 0, 0, 0)
                for i in range(NB):
                    u0 = HA * i
                    with dve.Fori(0, HA // 2 - 1) as hp:
                        for s in range(2):
                            self.scale(dve, i, 1 - s, u0 + 2 * hp + s + 1)
                            self.combine(dve, i, s, u0 + 2 * hp + s)
                    self.scale(dve, i, 1, u0 + HA - 1)
                    self.combine(dve, i, 0, u0 + HA - 2)
                    if i + 1 < NB:
                        self.scale(dve, i + 1, 0, u0 + HA)
                    self.combine(dve, i, 1, u0 + HA - 1)

            def exp(self, act, i, s, u):
                n = self.keys(i)
                act.wait_ge(self.scaled, u + 3)
                act.wait_ge(self.combined, u + 1)
                for m in range(2):
                    k = slice(2 * s + m, 2 * s + m + 1)
                    ins = nc.scalar.activation(p_sb[:, s, m, 0:n], s_sb[:, s, m, 0:n], ACT.Exp, bias=nmax[:, k],
                                               scale=-1.0, accum_out=rsum[:, k])
                ins.then_inc(self.exped, 1)

            def keep_turned(self, act, i, s, u):
                n = self.keys(i)
                act.wait_ge(self.turned, u + 3)
                act.wait_ge(self.pv, u + 1)
                nc.scalar.copy(aT[:, s, 0:n], ps[:, 4 + s, 0:n]).then_inc(self.aT_set, 1)

            def keep_output(self, act, s, u, i, h):
                act.wait_ge(self.pv, u + 3)
                nc.scalar.copy(o_nat[:, i, bass.ds(h * DV, DV)], ps[:, 6 + s, 0:DV]).then_inc(self.o_set, 1)

            def act_part(self, act):
                self.exp(act, 0, 0, 0)
                for i in range(NB):
                    u0 = HA * i
                    self.exp(act, i, 1, u0 + 1)
                    self.keep_turned(act, i, 0, u0)
                    if i:
                        self.keep_output(act, 1, u0 - 1, i - 1, HA - 1)
                    with act.Fori(0, HA // 2 - 1) as hp:
                        for s in range(2):
                            h = 2 * hp + 1 + s
                            self.exp(act, i, s, u0 + h + 1)
                            self.keep_turned(act, i, 1 - s, u0 + h)
                            self.keep_output(act, s, u0 + h - 1, i, h - 1)
                    if i + 1 < NB:
                        self.exp(act, i + 1, 0, u0 + HA)
                    self.keep_turned(act, i, 1, u0 + HA - 1)
                    self.keep_output(act, 0, u0 + HA - 2, i, HA - 2)
                self.keep_output(act, 1, HA * NB - 1, NB - 1, HA - 1)

            def credits_pe(self, pe):
                pe.sem_inc(self.scored, 2)
                pe.sem_inc(self.turned, 2)
                pe.sem_inc(self.pv, 2)

            def credits_dve(self, dve):
                dve.sem_inc(self.scaled, 2)
                dve.sem_inc(self.combined, 2)

            def credits_act(self, act):
                act.sem_inc(self.exped, 2)
                act.sem_inc(self.aT_set, 2)
                act.sem_inc(self.o_set, 2)

        ROWS = HA * 2 * TDEC
        NKEYS = PAST + NS

        class DecodeAttention:
            def __init__(self):
                self.k_landed = [sem(f"da_k_landed{r}") for r in range(4)]
                self.v_landed = [sem(f"da_v_landed{r}") for r in range(4)]
                self.qk_hi, self.qk_lo = sem("da_qk_hi"), sem("da_qk_lo")
                self.setup = sem("da_setup")
                self.vn_hi, self.vn_lo = sem("da_vn_hi"), sem("da_vn_lo")
                self.k_half = sem("da_k_half")
                self.kT_hi = sem("da_kT_hi")
                self.kT_lo = sem("da_kT_lo")
                self.q_built = sem("da_q_built")
                self.scored = sem("da_scored")
                self.s_low = sem("da_s_low")
                self.s_min = sem("da_s_min")
                self.exped = sem("da_exped")
                self.p_turned = sem("da_p_turned")
                self.pT_hi = sem("da_pT_hi")
                self.pT_lo = sem("da_pT_lo")
                self.v_hi = sem("da_v_hi")
                self.v_lo = sem("da_v_lo")
                self.pv = sem("da_pv")
                self.o_done = sem("da_o_done")
                self.o_kept = sem("da_o_kept")
                self.coef = sem("da_coef")
                self.weighed = sem("da_weighed")
                self.merged = sem("da_merged")
                self.fin = sem("da_fin")
                self.fin_ss = sem("da_fin_ss")
                self.fin_sd = sem("da_fin_sd")
                self.oa_set = sem("da_oa_set")

            def load_page(self, sp, cache, ring, landed, free, steps, b, g):
                page = sp.value_load(pages[0:1, bass.ds(PAGES * b + g, 1)], min_val=0, max_val=cache.shape[1] - 1)
                sp.wait_ge(free, steps * PAGES * b + steps * (g + 1))
                sp.dma_start(ring[:, g % 4], cache[0, bass.ds(page, 1)].rearrange("o p h d -> p (o h d)")
                             ).then_inc(landed[g % 4], 16)

            def load_k(self, sp, b, g):
                self.load_page(sp, cache_k, k_page, self.k_landed, self.k_half, 2, b, g)

            def load_v(self, sp, b, g):
                self.load_page(sp, cache_v, v_page, self.v_landed, self.v_lo, 1, b, g)

            def sp_step(self, sp, b):
                for g in range(0, PAGES, 2):
                    for n in (g, g + 1):
                        self.load_k(sp, b, n)
                    for n in (g, g + 1):
                        self.load_v(sp, b - 1, n)

            def sp_part(self, sp):
                for g in range(4):
                    self.load_k(sp, 0, g)
                sp.wait_ge(attn.pv, HA * NB + 2)
                sp.wait_ge(v_stored, 32)
                for g in range(4, PAGES):
                    self.load_k(sp, 0, g)
                with sp.Fori(1, DEC) as b:
                    self.sp_step(sp, b)
                for g in range(PAGES):
                    self.load_v(sp, DEC - 1, g)

            def turn(self, pe, b, g):
                for half in range(2):
                    if half == 0:
                        pe.wait_ge(self.k_landed[g % 4], 32 * b + 16 * (g // 4) + 16)
                    pe.wait_ge(self.kT_lo, 16 * b + 2 * g + half + 1)
                    for h in range(4):
                        mm = nc.tensor.transpose(ps[:, half, h * P:h * P + P],
                                                 k_page[:, g % 4, (4 * half + h) * P:(4 * half + h) * P + P], ident[:])
                    mm.then_inc(self.k_half, 1)

            def score_pair(self, pe, b, q):
                pe.wait_ge(self.kT_lo, 16 * b + 4 * q + 6)
                if q == 0:
                    pe.wait_ge(self.q_built, 4 * b + 4)
                    pe.wait_ge(self.s_min, b + 1)
                dst = ps[:, 2 + q // 2, 256 * (q % 2):256 * (q % 2) + 256]
                nc.tensor.matmul(dst, ident_r[0:ROWS], bias_r[0:ROWS, 256 * q:256 * q + 256], start=True, stop=False)
                for h in range(HA):
                    for kt in (kt_hi, kt_lo):
                        mm = nc.tensor.matmul(dst, q_stat[:, P * h:P * h + P], kt[:, q % 2, h],
                                              start=False, stop=h == HA - 1 and kt is kt_lo)
                mm.then_inc(self.scored, 1)

            def score_new(self, pe, b):
                dst = ps[:, 4, 0:NS]
                nc.tensor.matmul(dst, ident_r[0:ROWS], bias_r[0:ROWS, bass.ds(NS * b + PAST, NS)], start=True, stop=False)
                for h in range(HA):
                    for kn in (kn_hi, kn_lo):
                        nc.tensor.matmul(dst, q_stat[:, P * h:P * h + P], kn[:, h],
                                         start=False, stop=h == HA - 1 and kn is kn_lo)

            def turn_p(self, pe, b):
                pe.wait_ge(self.exped, b + 1)
                pe.wait_ge(self.pT_lo, 2 * b + 2)
                nc.tensor.matmul(ps[:, 5, 0:ROWS], p_s[:, 0:P], ident[:, 0:ROWS], start=True, stop=True)
                for g in range(1, PAGES):
                    nc.tensor.transpose(ps[:, 5, ROWS * g:ROWS * g + ROWS], p_s[0:ROWS, P * g:P * g + P],
                                        ident[0:ROWS, 0:ROWS])
                nc.tensor.transpose(ps[0:NS, 4, NS:NS + ROWS], p_s[0:ROWS, PAST:NKEYS], ident[0:ROWS, 0:ROWS]
                                    ).then_inc(self.p_turned, 1)

            def values(self, pe, b, g):
                if g == 0:
                    pe.wait_ge(self.pT_lo, 2 * b + 4)
                    pe.wait_ge(self.o_kept, b + 1)
                pe.wait_ge(self.v_lo, PAGES * b + g + 5)
                for half in range(2):
                    for v in (vp_hi, vp_lo):
                        mm = nc.tensor.matmul(ps[:, 6 + half, :], pT[:, g], v[:, g % 2, 512 * half:512 * half + 512],
                                              start=g == 0 and v is vp_hi, stop=False)
                mm.then_inc(self.pv, 1)

            def values_new(self, pe, b):
                for half in range(2):
                    for v in (vn_hi, vn_lo):
                        mm = nc.tensor.matmul(ps[:, 6 + half, :], pT[0:NS, PAGES], v[0:NS, 512 * half:512 * half + 512],
                                              start=False, stop=v is vn_lo)
                mm.then_inc(self.o_done, 1)

            def merge(self, pe, b):
                pe.wait_ge(self.o_kept, b + 2)
                pe.wait_ge(self.weighed, b + 1)
                for h in range(HA):
                    mm = nc.tensor.matmul(ps[:, 4, bass.ds(32 * b + (256 + TDEC * h), TDEC)],
                                          o_rows[:, P * h:P * h + P], weights[:, TDEC * h:TDEC * h + TDEC],
                                          start=True, stop=True)
                mm.then_inc(self.merged, 1)

            def pe_step(self, pe, b, past=True, older=True):
                def two(f, bb, g):
                    f(pe, bb, g)
                    f(pe, bb, g + 1)
                two(self.turn, b, 0)
                if older:
                    self.merge(pe, b - 2)
                if past:
                    self.turn_p(pe, b - 1)
                for q in range(PAGES // 2):
                    if q + 1 < PAGES // 2:
                        two(self.turn, b, 2 * q + 2)
                    else:
                        self.score_new(pe, b)
                    self.score_pair(pe, b, q)
                    if past:
                        two(self.values, b - 1, 2 * q)
                if past:
                    self.values_new(pe, b - 1)

            def pe_part(self, pe):
                pe.wait_ge(self.setup, 5)
                pe.wait_ge(self.qk_lo, 2)
                pe.wait_ge(self.vn_lo, 1)
                self.pe_step(pe, 0, past=False, older=False)
                self.pe_step(pe, 1, older=False)
                with pe.Fori(2, DEC) as b:
                    self.pe_step(pe, b)
                self.merge(pe, DEC - 2)
                self.turn_p(pe, DEC - 1)
                for g in range(PAGES):
                    self.values(pe, DEC - 1, g)
                self.values_new(pe, DEC - 1)
                self.merge(pe, DEC - 1)

            def key_half(self, b, g, half, hi):
                src = ps[:, half, :].rearrange("p (h c) -> p h c", c=P)
                n = slice(P * (g % 2), P * (g % 2) + P)
                at_hi = kt_hi[:, (g // 2) % 2, 4 * half:4 * half + 4, n]
                at_lo = kt_lo[:, (g // 2) % 2, 4 * half:4 * half + 4, n]
                if hi:
                    return nc.scalar.copy(at_hi, src)
                return nc.vector.tensor_tensor(at_lo, src, at_hi.bitcast(F32), ALU.subtract)

            def act_key(self, act, b, g):
                for half in range(2):
                    if g % 2 == 0 and half == 0:
                        act.wait_ge(self.scored, 4 * b + g // 2 + 1)
                    act.wait_ge(self.k_half, 16 * b + 2 * g + half + 9)
                    self.key_half(b, g, half, True).then_inc(self.kT_hi, 1)

            def dve_key(self, dve, b, g):
                for half in range(2):
                    dve.wait_ge(self.kT_hi, 16 * b + 2 * g + half + 1)
                    self.key_half(b, g, half, False).then_inc(self.kT_lo, 1)

            def act_value(self, act, b, g):
                act.wait_ge(self.v_landed[g % 4], 32 * b + 16 * (g // 4) + 16)
                act.wait_ge(self.pv, PAGES * b + g + 1)
                nc.scalar.copy(vp_hi[:, g % 2], v_page[:, g % 4]).then_inc(self.v_hi, 1)

            def dve_value(self, dve, b, g):
                dve.wait_ge(self.v_hi, PAGES * b + g + 1)
                nc.vector.tensor_tensor(vp_lo[:, g % 2], v_page[:, g % 4], vp_hi[:, g % 2].bitcast(F32), ALU.subtract
                                        ).then_inc(self.v_lo, 1)

            def p_parts(self):
                return ((ps[:, 5, :].rearrange("p (g c) -> p g c", c=ROWS), pT[:, 0:PAGES, 0:ROWS],
                         pT[:, 0:PAGES, ROWS:P]),
                        (ps[0:NS, 4, NS:NS + ROWS].unsqueeze(1), pT[0:NS, PAGES:PAGES + 1, 0:ROWS],
                         pT[0:NS, PAGES:PAGES + 1, ROWS:P]))

            def act_setup_early(self, act):
                nc.scalar.copy(qs_hi[:], qaT[:, :, SEQ:T]).then_inc(self.qk_hi, 1)
                nc.scalar.copy(kn_hi[:], kaT[:, :, SEQ:T]).then_inc(self.qk_hi, 1)

            def act_setup(self, act):
                nc.scalar.copy(ident_r[0:ROWS], ident[0:ROWS]).then_inc(self.setup, 1)
                act.wait_ge(dec_const, 48)
                nc.scalar.copy(bias_r[0:ROWS], bias_stage[0:ROWS]).then_inc(self.setup, 1)
                act.wait_ge(v_stored, 32)
                nc.scalar.copy(vn_hi[0:NS], v_nat_s[0:NS]).then_inc(self.vn_hi, 1)

            def act_queries(self, act, b):
                act.wait_ge(self.scored, 4 * b + 2)
                act.wait_ge(self.setup, 5)
                for src, first in ((qs_hi, 0), (qs_lo, ROWS)):
                    cols = q_stat[:, first:first + HA * (P + 8)].rearrange("p (h c) -> p h c", c=P + 8)
                    for m in range(2):
                        r = slice(DH * m, DH * m + DH)
                        nc.scalar.copy(cols[r, :, TDEC * m:TDEC * m + TDEC], src[r, :, bass.ds(TDEC * b, TDEC)]
                                       ).then_inc(self.q_built, 1)

            def act_low_rows(self, act, b):
                act.wait_ge(self.scored, 4 * b + 6)
                act.wait_ge(self.p_turned, b + 1)
                nc.scalar.copy(p_s[0:ROWS], score_ps(ROWS)).then_inc(self.s_low, 1)

            def act_exp(self, act, b):
                act.wait_ge(self.s_min, b + 2)
                nc.scalar.activation(p_s[0:ROWS], p_s[0:ROWS], ACT.Exp, bias=nmax[0:ROWS, 0:1], scale=-1.0,
                                     accum_out=rsum[0:ROWS, 0:1]).then_inc(self.exped, 1)

            def act_p(self, act, b):
                act.wait_ge(self.p_turned, b + 2)
                act.wait_ge(self.o_done, b + 1)
                for src, hi, _ in self.p_parts():
                    nc.scalar.copy(hi, src).then_inc(self.pT_hi, 1)

            def act_keep(self, act, b):
                act.wait_ge(self.o_done, b + 2)
                act.wait_ge(self.merged, b + 1)
                nc.scalar.copy(o_rows[:], ps[:, 6:8, :].rearrange("p a b -> p (a b)")).then_inc(self.o_kept, 1)

            def act_step(self, act, b, past=True, older=True):
                self.act_key(act, b, 0)
                if past:
                    self.act_exp(act, b - 1)
                if older:
                    self.act_keep(act, b - 2)
                self.act_key(act, b, 1)
                if past:
                    self.act_p(act, b - 1)
                self.act_queries(act, b)
                for g in range(PAGES):
                    if past:
                        self.act_value(act, b - 1, g)
                    if g + 2 < PAGES:
                        self.act_key(act, b, g + 2)
                self.act_low_rows(act, b)

            def act_part(self, act):
                self.act_step(act, 0, past=False, older=False)
                self.act_step(act, 1, older=False)
                with act.Fori(2, DEC) as b:
                    self.act_step(act, b)
                self.act_exp(act, DEC - 1)
                self.act_keep(act, DEC - 2)
                self.act_p(act, DEC - 1)
                for g in range(PAGES):
                    self.act_value(act, DEC - 1, g)
                self.act_keep(act, DEC - 1)

            def dve_setup_early(self, dve):
                dve.wait_ge(self.qk_hi, 1)
                nc.vector.tensor_tensor(qs_lo[:], qaT[:, :, SEQ:T], qs_hi[:].bitcast(F32), ALU.subtract
                                        ).then_inc(self.qk_lo, 1)
                dve.wait_ge(self.qk_hi, 2)
                nc.vector.tensor_tensor(kn_lo[:], kaT[:, :, SEQ:T], kn_hi[:].bitcast(F32), ALU.subtract
                                        ).then_inc(self.qk_lo, 1)

            def dve_setup(self, dve):
                nc.vector.memset(q_stat[:].bitcast(F32), 0.0).then_inc(self.setup, 1)
                nc.vector.memset(p_s[ROWS:P, 0:P], 0.0).then_inc(self.setup, 1)
                dve.wait_ge(dec_const, 48)
                nc.vector.scalar_tensor_tensor(map_signs[:], minus_second[:], lamv[:, 1:2], minus_first[:],
                                               ALU.mult, ALU.subtract).then_inc(self.setup, 1)
                dve.wait_ge(self.vn_hi, 1)
                nc.vector.tensor_tensor(vn_lo[0:NS], v_nat_s[0:NS], vn_hi[0:NS].bitcast(F32), ALU.subtract
                                        ).then_inc(self.vn_lo, 1)

            def dve_min(self, dve, b):
                dve.wait_ge(self.s_low, b + 1)
                nc.vector.memset(rsum[0:ROWS, 0:1], 0.0)
                nc.vector.tensor_tensor_reduce(p_s[0:ROWS], score_ps(0), p_s[0:ROWS], -DH ** -0.5, -MASKED,
                                               ALU.add, ALU.min, nmax[0:ROWS, 0:1]).then_inc(self.s_min, 1)

            def dve_p(self, dve, b):
                dve.wait_ge(self.pT_hi, 2 * b + 2)
                for src, hi, lo in self.p_parts():
                    nc.vector.tensor_tensor(lo, src, hi.bitcast(F32), ALU.subtract).then_inc(self.pT_lo, 1)

            def dve_weigh(self, dve, b):
                dve.wait_ge(self.exped, b + 1)
                nc.vector.reciprocal(rr[0:ROWS, 0:1], rsum[0:ROWS, 0:1]).then_inc(self.coef, 1)
                dve.wait_ge(self.coef, 2 * b + 1)
                nc.vector.tensor_copy(rr[ROWS:P, 0:1], rr[0:ROWS, 0:1]).then_inc(self.coef, 1)
                dve.wait_ge(self.coef, 2 * b + 2)
                dve.wait_ge(self.merged, b + 1)
                nc.vector.tensor_scalar(weights[:], map_signs[:], rr[:, 0:1], None, ALU.mult
                                        ).then_inc(self.weighed, 1)

            def dve_step(self, dve, b, past=True):
                self.dve_key(dve, b, 0)
                self.dve_key(dve, b, 1)
                if past:
                    self.dve_p(dve, b - 1)
                    self.dve_weigh(dve, b - 1)
                for g in range(PAGES):
                    if past:
                        self.dve_value(dve, b - 1, g)
                    if g + 2 < PAGES:
                        self.dve_key(dve, b, g + 2)
                self.dve_min(dve, b)

            def dve_part(self, dve):
                self.dve_step(dve, 0, past=False)
                with dve.Fori(1, DEC) as b:
                    self.dve_step(dve, b)
                self.dve_p(dve, DEC - 1)
                self.dve_weigh(dve, DEC - 1)
                for g in range(PAGES):
                    self.dve_value(dve, DEC - 1, g)

            def dve_finish(self, dve):
                dve.wait_ge(self.merged, DEC + 1)
                nc.vector.tensor_copy(dec_o[:, 0], ps[:, 4, 256:512]).then_inc(self.fin, 1)
                dve.wait_ge(self.fin, 1)
                nc.vector.tensor_tensor(dec_o[:, 1], dec_o[:, 0], dec_o[:, 0], ALU.mult).then_inc(self.fin, 1)
                dve.wait_ge(self.fin_ss, 1)
                nc.vector.tensor_scalar(dec_l[:, 0], ps[:, 7, 0:256], 1.0 / DV, EPS, ALU.mult, ALU.add
                                        ).then_inc(self.fin, 1)
                dve.wait_ge(self.fin_sd, 1)
                nc.vector.reciprocal(dec_l[:, 0], dec_l[:, 1]).then_inc(self.fin, 1)
                dve.wait_ge(self.fin, 4)
                nc.vector.tensor_tensor(dec_o[:, 1], dec_o[:, 0], dec_l[:, 0], ALU.mult).then_inc(self.fin, 1)
                dve.wait_ge(self.fin, 5)
                nc.vector.tensor_scalar(oaT[:, :, SEQ:T].rearrange("p h (b t) -> p h b t", t=TDEC),
                                        dec_o[:, 1].rearrange("p (b h t) -> p h b t", h=HA, t=TDEC),
                                        subln8[:, 0:1], None, ALU.mult).then_inc(self.oa_set, 1)

            def pe_finish(self, pe):
                pe.wait_ge(self.fin, 2)
                nc.tensor.matmul(ps[:, 7, 0:256], ones[:], dec_o[:, 1], start=True, stop=True).then_inc(self.fin_ss, 1)

            def act_finish(self, act):
                act.wait_ge(self.fin, 3)
                nc.scalar.activation(dec_l[:, 1], dec_l[:, 0], ACT.Sqrt).then_inc(self.fin_sd, 1)

            def credits_pe(self, pe):
                pe.sem_inc(self.k_half, 8)
                pe.sem_inc(self.scored, 2)
                pe.sem_inc(self.p_turned, 1)
                pe.sem_inc(self.pv, 2)
                pe.sem_inc(self.o_done, 1)
                pe.sem_inc(self.merged, 1)

            def credits_dve(self, dve):
                dve.sem_inc(self.kT_lo, 2)
                dve.sem_inc(self.s_min, 1)
                dve.sem_inc(self.pT_lo, 2)
                dve.sem_inc(self.v_lo, 4)

            def credits_act(self, act):
                act.sem_inc(self.o_kept, 1)

        class Retention:
            def __init__(self):
                self.scored = sem("rt_scored")
                self.sc_set = sem("rt_sc_set")
                self.qx_set = sem("rt_qx_set")
                self.kw_set = sem("rt_kw_set")
                self.out = sem("rt_out")
                self.o_kept = sem("rt_o_kept")
                self.kv = sem("rt_kv")
                self.st_set = sem("rt_st_set")
                self.st_stored = sem("rt_st_stored")
                self.s_scored = sem("rs_scored")
                self.s_sc_set = sem("rs_sc_set")
                self.s_in = [sem(f"rs_in{j}") for j in range(2)]
                self.s_qm_zero = sem("rs_qm_zero")
                self.s_qm = sem("rs_qm")
                self.s_kw = sem("rs_kw")
                self.s_cross = sem("rs_cross")
                self.s_kv = sem("rs_kv")
                self.s_new = sem("rs_new")
                self.s_stored = [sem(f"rs_stored{j}") for j in range(2)]
                self.s_kept = sem("rs_kept")

            def chunk(self, c):
                return slice(c * P, c * P + P)

            def pe_part(self, pe):
                def scores(c):
                    if c >= 2:
                        pe.wait_ge(self.sc_set, c - 1)
                    for h in range(HR):
                        mm = nc.tensor.matmul(ps[:, c % 2, h * P:h * P + P], krT[:, h, self.chunk(c)],
                                              qrT[:, h, self.chunk(c)], start=True, stop=True)
                    mm.then_inc(self.scored, 1)

                def keys_values(c):
                    pe.wait_ge(self.kw_set, c + 1)
                    if c:
                        pe.wait_ge(self.st_set, HR * c)
                    for h in range(HR):
                        mm = nc.tensor.matmul(ps[:, 4 + h // 2, (h % 2) * RV:(h % 2) * RV + RV],
                                              kr_nat[:, c, h * RK:h * RK + RK], vr_nat[:, c, h * RV:h * RV + RV],
                                              start=True, stop=True)
                    mm.then_inc(self.kv, 1)

                def output(c):
                    pe.wait_ge(self.sc_set, c + 1)
                    if c:
                        pe.wait_ge(self.qx_set, c)
                        pe.wait_ge(self.st_set, HR * c)
                    if c >= 2:
                        pe.wait_ge(self.o_kept, c - 1)
                    for h in range(HR):
                        dst = ps[:, (6 if c % 2 else 2) + h // 2, (h % 2) * RV:(h % 2) * RV + RV]
                        mm = nc.tensor.matmul(dst, scT[:, c % 2, h * P:h * P + P], vr_nat[:, c, h * RV:h * RV + RV],
                                              start=True, stop=c == 0)
                        if c:
                            mm = nc.tensor.matmul(dst, qx[:, c % 2, h], state[:, c % 2, h * RV:h * RV + RV],
                                                  start=False, stop=True)
                    mm.then_inc(self.out, 1)

                scores(0)
                for c in range(NB):
                    if c + 1 < NB:
                        scores(c + 1)
                    keys_values(c)
                    output(c)
                pe.wait_ge(self.sc_set, NB)
                for h in range(HR):
                    mm = nc.tensor.matmul(ps[0:NS, 0, h * NS:h * NS + NS], krT[:, h, SEQ:T], qrT[:, h, SEQ:T],
                                          start=True, stop=True)
                mm.then_inc(self.s_scored, 1)
                pe.wait_ge(self.s_sc_set, 1)
                pe.wait_ge(self.o_kept, NB)
                pe.wait_ge(self.st_set, HR * NB)
                for h in range(HR):
                    nc.tensor.matmul(ps[0:NS, 2 + h // 2, (h % 2) * RV:(h % 2) * RV + RV],
                                     scT[0:NS, 0, h * NS:h * NS + NS], vr_nat_s[0:NS, h * RV:h * RV + RV],
                                     start=h % 2 == 0, stop=False, skip_group_check=True)
                pe.wait_ge(self.s_qm, DEC)
                for b in range(DEC):
                    pe.wait_ge(self.s_in[b % 2], 16 * (b // 2) + 16)
                    for h in range(HR):
                        mm = nc.tensor.matmul(ps[0:NS, 2 + h // 2, (h % 2) * RV:(h % 2) * RV + RV], qm[:, b, h],
                                              st_in[:, b % 2, h * RV:h * RV + RV], start=False,
                                              stop=b == DEC - 1, skip_group_check=True)
                    mm.then_inc(self.s_cross, 1)
                    pe.wait_ge(self.s_kw, b + 1)
                    if b >= 2:
                        pe.wait_ge(self.s_new, HR * (b - 1))
                    for h in range(HR):
                        mm = nc.tensor.matmul(ps[:, (6 if b % 2 else 4) + h // 2, (h % 2) * RV:(h % 2) * RV + RV],
                                              kw_s[0:NS, b % 2, h * RK:h * RK + RK],
                                              vr_nat_s[0:NS, h * RV:h * RV + RV], start=True, stop=True)
                    mm.then_inc(self.s_kv, 1)

            def dve_part(self, dve):
                def weigh(c):
                    dve.wait_ge(self.scored, c + 1)
                    if c >= 2:
                        dve.wait_ge(self.out, c - 1)
                    nc.vector.tensor_tensor(scT[:, c % 2], ps[:, c % 2, :], decay[:].rearrange("p h i -> p (h i)"),
                                            ALU.mult).then_inc(self.sc_set, 1)

                def advance(c):
                    dve.wait_ge(self.kv, c + 1)
                    if c >= 1:
                        dve.wait_ge(self.st_set, HR * c)
                        dve.wait_ge(self.out, c)
                    for h in range(HR):
                        e = slice(h * RV, h * RV + RV)
                        src = ps[:, 4 + h // 2, (h % 2) * RV:(h % 2) * RV + RV]
                        if c == 0:
                            ins = nc.vector.tensor_copy(state[:, 1, e], src)
                        else:
                            ins = nc.vector.scalar_tensor_tensor(state[:, (c + 1) % 2, e], state[:, c % 2, e],
                                                                 gamma[h] ** P, src, ALU.mult, ALU.add)
                        ins.then_inc(self.st_set, 1)

                weigh(0)
                for c in range(NB):
                    if c + 1 < NB:
                        weigh(c + 1)
                    advance(c)
                dve.wait_ge(self.s_scored, 1)
                dve.wait_ge(self.out, NB)
                nc.vector.tensor_tensor(scT[0:NS, 0, 0:HR * NS], ps[0:NS, 0, 0:HR * NS],
                                        decay_s[0:NS].rearrange("p h i -> p (h i)"), ALU.mult).then_inc(self.s_sc_set, 1)
                for b in range(DEC):
                    dve.wait_ge(self.s_kv, b + 1)
                    dve.wait_ge(self.s_in[b % 2], 16 * (b // 2) + 16)
                    if b >= 2:
                        dve.wait_ge(self.s_stored[b % 2], 16 * (b // 2))
                    for h in range(HR):
                        e = slice(h * RV, h * RV + RV)
                        nc.vector.scalar_tensor_tensor(st_out[:, b % 2, e], st_in[:, b % 2, e], gamma[h] ** TDEC,
                                                       ps[:, (6 if b % 2 else 4) + h // 2,
                                                          (h % 2) * RV:(h % 2) * RV + RV],
                                                       ALU.mult, ALU.add).then_inc(self.s_new, 1)

            def act_part(self, act):
                for c in range(NB):
                    act.wait_ge(self.out, c + 1)
                    b = 6 if c % 2 else 2
                    nc.scalar.copy(or_nat[:, c], ps[:, b:b + 2, :].rearrange("p a b -> p (a b)")
                                   ).then_inc(self.o_kept, 1)
                act.wait_ge(self.s_cross, DEC)
                act.wait_ge(self.s_kv, DEC)
                nc.scalar.copy(or_s[0:NS], ps[0:NS, 2:4, :].rearrange("p a b -> p (a b)")).then_inc(self.s_kept, 1)

            def pool_part(self, pool):
                for c in range(NB):
                    rows = kr_nat[:, c].rearrange("p (h d) -> p h d", d=RK)
                    nc.gpsimd.tensor_tensor(rows, rows, kdec[:].unsqueeze(2).broadcast_to([P, HR, RK]), ALU.mult
                                            ).then_inc(self.kw_set, 1)
                    if c:
                        if c >= 2:
                            pool.wait_ge(self.out, c - 1)
                        nc.gpsimd.tensor_tensor(qx[:, c % 2], qrT[:, :, self.chunk(c)], cross[:], ALU.mult
                                                ).then_inc(self.qx_set, 1)
                pool.wait_ge(self.out, NB)
                nc.gpsimd.memset(qm[:], 0.0).then_inc(self.s_qm_zero, 1)
                pool.wait_ge(self.s_qm_zero, 1)
                for b in range(DEC):
                    a = TDEC * b
                    nc.gpsimd.tensor_tensor(qm[:, b, :, a:a + TDEC], qrT[:, :, SEQ + a:SEQ + a + TDEC],
                                            cross[:, :, 0:TDEC], ALU.mult).then_inc(self.s_qm, 1)
                for b in range(DEC):
                    if b >= 2:
                        pool.wait_ge(self.s_kv, b - 1)
                    nc.gpsimd.tensor_tensor(kw_s[0:NS, b % 2].rearrange("p (h d) -> p h d", d=RK),
                                            kr_nat_s[0:NS].rearrange("p (h d) -> p h d", d=RK),
                                            kdec_s[0:NS, HR * b:HR * b + HR].unsqueeze(2).broadcast_to([NS, HR, RK]),
                                            ALU.mult).then_inc(self.s_kw, 1)

            def sp_part(self, sp):
                sp.wait_ge(self.st_set, HR * NB)
                sp.dma_start(ret_state_prompt[0, 0].rearrange("h d e -> d h e"),
                             state[:, 0].rearrange("p (h e) -> p h e", e=RV)).then_inc(out_stored, 16)
                sp.wait_ge(self.out, NB)

                def load(b):
                    sp.dma_start(st_in[:, b % 2].rearrange("p (h e) -> p h e", e=RV),
                                 state_ret[0, b].rearrange("h d e -> d h e")).then_inc(self.s_in[b % 2], 16)
                load(0)
                load(1)
                for b in range(DEC):
                    sp.wait_ge(self.s_new, HR * (b + 1))
                    sp.dma_start(ret_state_sample[0, b].rearrange("h d e -> d h e"),
                                 st_out[:, b % 2].rearrange("p (h e) -> p h e", e=RV)).then_inc(self.s_stored[b % 2], 16)
                    if b + 2 < DEC:
                        sp.wait_ge(self.s_cross, b + 1)
                        load(b + 2)

        class RetGate:
            def __init__(self, c):
                self.c = c
                self.silu_done = sem("rg_silu_done")
                self.prod_done = sem("rg_prod_done")
                self.o_hi, self.o_lo = sem("rg_o_hi"), sem("rg_o_lo")

            def loads(self, sp, first, last):
                for i in range(first, last):
                    for j in range(2):
                        load_chunk(sp, self.c + 2 * i + j, self.c // 2 + i, j,
                                   w_in, W_IN_COLS["gr"] + 512 * i + 256 * j)

            def pe_part(self, pe):
                with pe.Fori(0, 2) as i:
                    for t in range(4):
                        if t % 2 == 0:
                            chunk_ready(pe, self.c + 2 * i + t // 2)
                        pe.wait_ge(self.silu_done, 4 * i + t + 1)
                        gemm(4 + 2 * (t % 2), t // 2, t % 2, KD, xh, xl)

            def act_part(self, act):
                act.sem_inc(self.silu_done, 2)
                with act.Fori(0, 2) as i:
                    for t in range(4):
                        u, c = 4 * i + t, self.c + 2 * i + t // 2
                        tile_done(act, c, t % 2)
                        act.wait_ge(self.prod_done, u + 1)
                        nc.scalar.activation(halves(gated[:, t % 2]), banks(4 + 2 * (t % 2)), ACT.Silu
                                             ).then_inc(self.silu_done, 1)
                        act.wait_ge(self.prod_done, u + 3)
                        nc.scalar.copy(obh[:, bass.ds(u, 1)], prod[:, t % 2:t % 2 + 1]).then_inc(self.o_hi, 1)
                        if t % 2 == 1:
                            split_hi(act, c + 2, self.c // 2 + i + 1, t // 2)

            def dve_part(self, dve):
                dve.sem_inc(self.prod_done, 2)
                with dve.Fori(0, 2) as i:
                    for t in range(4):
                        u, c = 4 * i + t, self.c + 2 * i + t // 2
                        k, s = bass.ds(u, 1), slice(t % 2, t % 2 + 1)
                        dve.wait_ge(self.silu_done, u + 3)
                        nc.vector.tensor_tensor(prod[:, s], gated[:, s], onT[:, k], ALU.mult).then_inc(self.prod_done, 1)
                        dve.wait_ge(self.o_hi, u + 1)
                        nc.vector.tensor_tensor(obl[:, k], prod[:, s], obh[:, k].bitcast(F32), ALU.subtract
                                                ).then_inc(self.o_lo, 1)
                        if t % 2 == 1:
                            split_lo(dve, c + 2, t // 2)

        class OutProject:
            def __init__(self, c):
                self.c = c
                self.resid = sem("op_resid")

            def loads(self, sp):
                for i in range(2):
                    for j in range(2):
                        load_chunk(sp, self.c + 2 * i + j, self.c // 2 + i, j,
                                   w_out, 512 * i + 256 * j)

            def pe_part(self, pe):
                with pe.Fori(0, 2) as i:
                    for t in range(4):
                        if t % 2 == 0:
                            chunk_ready(pe, self.c + 2 * i + t // 2)
                        pe.wait_ge(self.resid, 4 * i + t + 1)
                        gemm(2 * t, t // 2, t % 2, KD, mh, ml)

            def act_part(self, act):
                with act.Fori(0, 2) as i:
                    for j in range(2):
                        split_hi(act, self.c + 2 * i + j + 2, self.c // 2 + i + 1, j)

            def dve_part(self, dve):
                dve.sem_inc(self.resid, 4)
                with dve.Fori(0, 2) as i:
                    for t in range(4):
                        c = self.c + 2 * i + t // 2
                        k = bass.ds(4 * i + t, 1)
                        tile_done(dve, c, t % 2)
                        xk = xT[:, k].rearrange("p o (a b) -> p (o a) b", b=HALF)
                        nc.vector.scalar_tensor_tensor(xk, banks(2 * t), 1.0 / ALPHA, xk, ALU.mult, ALU.add
                                                       ).then_inc(self.resid, 1)
                        if t % 2 == 1:
                            split_lo(dve, c + 2, t // 2)

        x_landed = [sem(f"x_landed{t}") for t in range(5)]
        turn_in = Norm(0, 0, 0, stats=False)
        turn_in.row_ready = lambda pe, t: pe.wait_ge(x_landed[t], 16)
        ffn1 = FFN("ffn1", C_FFN1_UP, ffn1_w_gu, ffn1_w_down)
        ln1 = Norm(0, 0, 1)
        pk = Project("pk", C_KA, 4, stage=turned, nat=k_nat, nat_s=k_nat_s, keep=kaT)
        pv = Project("pv", C_VA, 4, stage=turned, nat=v_nat, nat_s=v_nat_s)
        pq = Project("pq", C_QA, 4, direct=qaT)
        attn = PromptAttention()
        attn_norm = HeadNorm(0, 0, [(o_nat[:, b], P * b, P) for b in range(NB)], sq, DV)
        dec = DecodeAttention()
        split_oa = Split("soa", oaT, oah, oal)
        split_x = Split("sx", xT, xh, xl)
        branch_a = Branch("ba", C_BRANCH_A, W_IN_COLS["ga"], w_branch_a, oah, oal, add=False)
        rq = Project("rq", C_QR, 2, direct=qrT)
        rk = Project("rk", C_KR, 2, stage=rturned, nat=kr_nat, nat_s=kr_nat_s, keep=krT, scale=RK ** -0.5)
        rv = Project("rv", C_VR, 4, stage=rturned, nat=vr_nat, nat_s=vr_nat_s)
        ret = Retention()
        ret_norm = HeadNorm(NB, 1, [(or_nat[:, b], P * b, P) for b in range(NB)] + [(or_s[0:NS], SEQ, NS)], rsq, RV)
        ret_gate = RetGate(C_GR)
        branch_b = Branch("bb", C_BRANCH_B, W_IN_COLS["gb"], w_branch_b, obh, obl, add=True)
        out_proj = OutProject(C_OUT)
        ln2 = Norm(1, 1, 2)
        ffn2 = FFN("ffn2", C_FFN2_UP, ffn2_w_gu, ffn2_w_down, last=True)
        ln3 = Norm(2, 2, 3, back=False)

        att_const = sem("att_const")
        dec_const = sem("dec_const")
        ret_const = sem("ret_const")
        lam_sums, lam_exp, lam_set, subln_set = sem("lam_sums"), sem("lam_exp"), sem("lam_set"), sem("subln_set")
        k_stored, v_stored = sem("k_stored"), sem("v_stored")
        START_LOADS = 9

        block = ctx.enter_context(nc.Block())

        def const_load(eng, dst, name, signal, rows=P):
            a, n = const_at[name]
            eng.dma_start(dst, const[0:rows, a:a + n]).then_inc(signal, 16)

        def flat(t):
            return t.rearrange("p a b -> p (a b)")

        @block.sync
        def _(sp):
            for t, (t0, n) in enumerate(TOKENS):
                src = x_prompt[0, t0:t0 + n, :] if t < NB else x_sample.rearrange("b t d -> (b t) d")
                sp.dma_start(xn[0:n, t], src).then_inc(x_landed[t], 16)
                if t == 0:
                    const_load(sp, ident[:], "ident", const_landed)
            const_load(sp, ones[:], "ones", const_landed)
            const_load(sp, slope8[:], "slope8", const_landed)
            const_load(sp, map_rows[:], "map_rows", const_landed)
            const_load(sp, kdec[:], "kdec", const_landed)
            const_load(sp, kdec_s[:], "kdec_s", const_landed)
            sp.dma_start(lam_in[:], da_lambda[0:1].broadcast_to([P, 4, DH])).then_inc(const_landed, 16)
            sp.dma_start(subln[:], da_subln_g.rearrange("o d -> d o")).then_inc(const_landed, 16)
            sp.dma_start(pages[0:1], page_table.rearrange("b g -> (b g)").unsqueeze(0)).then_inc(const_landed, 16)
            ffn1.loads(sp)
            sp.wait_ge(ffn1.h_lo, KF)
            ln1.load_params(sp)
            const_load(sp, dist[:], "dist", att_const)
            pk.loads(sp, W_IN_COLS["ka"])
            pv.loads(sp, W_IN_COLS["va"])
            pq.loads(sp, W_IN_COLS["qa"])
            branch_a.loads(sp, 0, 1)
            sp.wait_ge(gemm_done, 2 * C_BRANCH_A + 4)
            const_load(sp, minus_first[:], "minus_first", dec_const)
            const_load(sp, minus_second[:], "minus_second", dec_const)
            sp.wait_ge(attn.combined, HA * NB + 2)
            const_load(sp, bias_stage[0:ROWS], "bias_dec", dec_const, ROWS)
            sp.wait_ge(attn.scored, HA * NB + 2)
            dec.sp_part(sp)
            branch_a.loads(sp, 1, KD // 2)
            rq.loads(sp, W_IN_COLS["qr"])
            sp.wait_ge(branch_a.prod_done, KD + 2)
            const_load(sp, flat(decay[:]), "decay", ret_const)
            const_load(sp, flat(cross[:]), "cross", ret_const)
            const_load(sp, flat(decay_s[0:NS]), "decay_s", ret_const, NS)
            rk.loads(sp, W_IN_COLS["kr"])
            rv.loads(sp, W_IN_COLS["vr"])
            ret_gate.loads(sp, 0, 1)
            ret.sp_part(sp)
            ret_gate.loads(sp, 1, 2)
            branch_b.loads(sp, 0, KD // 2)
            out_proj.loads(sp)
            sp.wait_ge(branch_b.m_lo, KD)
            ln2.load_params(sp)
            ffn2.loads(sp)
            sp.wait_ge(ffn2.h_lo, KF)
            ln3.load_params(sp)
            for t, (t0, n) in enumerate(TOKENS):
                sp.wait_ge(ln3.biased, ln3.s + t + 1)
                dst = y_prompt[0, t0:t0 + n, :] if t < NB else y_sample.rearrange("b t d -> (b t) d")
                sp.dma_start(dst, xn[0:n, t]).then_inc(out_stored, 16)
            sp.wait_ge(out_stored, 16 * 6)
            sp.wait_ge(k_stored, 32)
            sp.wait_ge(v_stored, 32)
            for stored in ret.s_stored:
                sp.wait_ge(stored, 8 * DEC)

        @block.scalar
        def _(act):
            turn_in.act_part(act)
            act.wait_ge(lam_sums, 2)
            nc.scalar.activation(lam_t[:, 2:4], lam_t[:, 0:2], ACT.Exp).then_inc(lam_exp, 1)
            split_hi(act, 0, 0, 0)
            split_hi(act, 1, 0, 1)
            ffn1.act_part(act)
            ln1.act_part(act)
            pk.act_part(act)
            act.wait_ge(pk.kept, 10)
            pv.act_part(act)
            pq.act_part(act)
            attn.credits_act(act)
            dec.credits_act(act)
            act.wait_ge(pq.taken, 10)
            dec.act_setup_early(act)
            act.wait_ge(k_stored, 32)
            attn.act_part(act)
            act.wait_ge(attn.combined, HA * NB + 2)
            act.wait_ge(attn.o_set, HA * NB + 2)
            attn_norm.act_squares(act)
            act.wait_ge(subln_set, 1)
            attn_norm.act_evict(act, oaT, subln8[:, 0:1])
            dec.act_setup(act)
            dec.act_part(act)
            dec.act_finish(act)
            split_x.act_part(act)
            act.wait_ge(v_stored, 32)
            act.wait_ge(dec.oa_set, 1)
            split_oa.act_part(act)
            branch_a.act_part(act)
            rq.act_part(act)
            rk.act_part(act)
            act.wait_ge(rk.kept, 6)
            rv.act_part(act)
            ret.act_part(act)
            act.wait_ge(ret.s_kept, 1)
            ret_norm.act_squares(act)
            ret_norm.act_evict(act, onT)
            for stored in ret.s_stored:
                act.wait_ge(stored, 8 * DEC)
            ret_gate.act_part(act)
            branch_b.act_part(act)
            out_proj.act_part(act)
            ln2.act_part(act)
            ffn2.act_part(act)
            ln3.act_part(act)

        @block.vector
        def _(dve):
            dve.sem_inc(lo_split, 2)
            dve.sem_inc(HeadNorm.summed, 2)
            turn_in.dve_part(dve)
            dve.wait_ge(const_landed, 16 * START_LOADS)
            nc.vector.memset(lamv[:, 0:1], 1.0)
            for j in range(2):
                nc.vector.tensor_tensor_reduce(lam_in[:, 2 * j], lam_in[:, 2 * j], lam_in[:, 2 * j + 1], 1.0, 0.0,
                                               ALU.mult, ALU.add, lam_t[:, j:j + 1]).then_inc(lam_sums, 1)
            nc.vector.tensor_scalar(subln8[:], subln[:], 1.0 - LAM_INIT, None, ALU.mult).then_inc(subln_set, 1)
            dve.wait_ge(lam_exp, 1)
            nc.vector.scalar_tensor_tensor(lamv[:, 1:2], lam_t[:, 2:3], LAM_INIT, lam_t[:, 3:4], ALU.add, ALU.subtract
                                           ).then_inc(lam_set, 1)
            split_lo(dve, 0, 0)
            split_lo(dve, 1, 1)
            ffn1.dve_part(dve)
            ln1.dve_part(dve)
            pk.dve_part(dve)
            pv.dve_part(dve)
            pq.dve_part(dve)
            attn.credits_dve(dve)
            dec.credits_dve(dve)
            dec.dve_setup_early(dve)
            dve.wait_ge(k_stored, 32)
            dve.wait_ge(lam_set, 1)
            attn.dve_part(dve)
            attn_norm.dve_scale(dve)
            dec.dve_setup(dve)
            dec.dve_part(dve)
            dec.dve_finish(dve)
            split_x.dve_part(dve)
            split_oa.dve_part(dve)
            branch_a.dve_part(dve)
            rq.dve_part(dve)
            rk.dve_part(dve)
            rv.dve_part(dve)
            dve.wait_ge(ret_const, 48)
            ret.dve_part(dve)
            ret_norm.dve_scale(dve)
            ret_gate.dve_part(dve)
            branch_b.dve_part(dve)
            out_proj.dve_part(dve)
            ln2.dve_part(dve)
            ffn2.dve_part(dve)
            ln3.dve_part(dve)

        @block.tensor
        def _(pe):
            pe.sem_inc(gemm_done, 4)
            attn.credits_pe(pe)
            dec.credits_pe(pe)
            for p in (pk, pv, rk, rv):
                pe.sem_inc(p.rows, 2)
            pe.wait_ge(const_landed, 16 * START_LOADS)
            turn_in.pe_part(pe)
            ffn1.pe_part(pe, turn_in.ready)
            pe.wait_ge(ffn1.resid, KD + 4)
            ln1.pe_part(pe)
            ln1.ready(pe)
            pk.pe_part(pe)
            pe.wait_ge(pk.taken, 10)
            pe.wait_ge(pk.stored, 10)
            pv.pe_part(pe)
            pe.wait_ge(pv.taken, 10)
            pq.pe_part(pe)
            pe.wait_ge(pq.taken, 10)
            pe.wait_ge(pv.stored, 10)
            attn.pe_part(pe)
            attn_norm.pe_part(pe)
            attn_norm.all_evicted(pe)
            pe.wait_ge(attn.aT_set, HA * NB + 2)
            pe.wait_ge(attn.o_set, HA * NB + 2)
            dec.pe_part(pe)
            dec.pe_finish(pe)
            split_x.ready(pe)
            split_oa.ready(pe)
            branch_a.pe_part(pe)
            pe.wait_ge(branch_a.sig_done, KD + 2)
            rq.pe_part(pe)
            pe.wait_ge(rq.taken, 6)
            pe.wait_ge(branch_a.prod_done, KD + 2)
            rk.pe_part(pe)
            pe.wait_ge(rk.taken, 6)
            pe.wait_ge(rk.stored, 6)
            rv.pe_part(pe)
            pe.wait_ge(rk.kept, 6)
            pe.wait_ge(rv.stored, 10)
            pe.wait_ge(rv.taken, 10)
            ret.pe_part(pe)
            pe.wait_ge(ret.s_kept, 1)
            ret_norm.pe_part(pe)
            pe.wait_ge(ret.s_new, HR * DEC)
            ret_gate.pe_part(pe)
            ret_norm.all_evicted(pe)
            pe.wait_ge(ret_gate.o_lo, KD)
            branch_b.pe_part(pe)
            pe.wait_ge(branch_b.m_lo, KD)
            out_proj.pe_part(pe)
            pe.wait_ge(out_proj.resid, KD + 4)
            ln2.pe_part(pe)
            ffn2.pe_part(pe, ln2.ready)
            pe.wait_ge(ffn2.resid, KD + 4)
            ln3.pe_part(pe)

        @block.gpsimd
        def _(pool):
            ln1.pool_part(pool)
            pk.pool_part(pool)
            pk.all_stored(pool)
            pool.dma_start(k_prompt[0, 0].rearrange("(b p) h d -> p b (h d)", p=P), k_nat[:]).then_inc(k_stored, 16)
            pool.dma_start(k_sample[0].rearrange("b t h d -> (b t) (h d)"), k_nat_s[0:NS]).then_inc(k_stored, 16)
            pv.all_stored(pool)
            pool.dma_start(v_prompt[0, 0].rearrange("(b p) h d -> p b (h d)", p=P), v_nat[:]).then_inc(v_stored, 16)
            pool.dma_start(v_sample[0].rearrange("b t h d -> (b t) (h d)"), v_nat_s[0:NS]).then_inc(v_stored, 16)
            pool.wait_ge(pq.taken, 10)
            pool.wait_ge(att_const, 16)
            pool.wait_ge(ln1.biased, ln1.s + 5)
            attn.pool_part(pool)
            rk.pool_part(pool)
            rk.all_stored(pool)
            rv.all_stored(pool)
            pool.wait_ge(ret_const, 48)
            ret.pool_part(pool)
            ln2.pool_part(pool)
            ln3.pool_part(pool)


_INS = ["x_prompt", "x_sample", "cache_k", "cache_v", "state_ret", "page_table", "ln_g", "ln_b", "ffn1_w_gu",
        "ffn1_w_down", "w_in", "da_lambda", "da_subln_g", "w_branch_a", "w_branch_b", "w_out", "ffn2_w_gu",
        "ffn2_w_down"]
_OUTS = [(1, SEQ, D), (DEC, TDEC, D), (1, 1, SEQ, HA, 2 * DH), (1, 1, SEQ, HA, DV), (1, 1, HR, RK, RV),
         (1, DEC, TDEC, HA, 2 * DH), (1, DEC, TDEC, HA, DV), (1, DEC, HR, RK, RV)]


def kernel(**inputs):
    import numpy as _np
    import concourse.bacc as _bacc
    from concourse import mybir as _mybir
    from concourse.bass_utils import run_bass_kernel_spmd as _run

    nc = _bacc.Bacc("TRN2", target_bir_lowering=False, num_devices=1)
    arrays, args = {}, []
    for name in _INS:
        arrays[f"in_{name}_dram"] = _np.ascontiguousarray(inputs[name])
    arrays["in_const_dram"] = constants()[1]
    for name, a in arrays.items():
        args.append(nc.dram_tensor(name, a.shape, _mybir.dt.from_np(a.dtype), kind="ExternalInput").ap())
    for i, shape in enumerate(_OUTS):
        args.append(nc.dram_tensor(f"out_{i}_dram", shape, _mybir.dt.float32, kind="ExternalOutput").ap())
    build(nc, *args)
    r = _run(nc, [arrays], core_ids=[0])
    return tuple(r.results[0][f"out_{i}_dram"] for i in range(len(_OUTS)))
```

```python
from contextlib import ExitStack

import numpy as np

import concourse.bass as bass
from concourse import mybir

F32 = mybir.dt.float32
F32R = mybir.dt.float32r
I32 = mybir.dt.int32
ALU = mybir.AluOpType
ACT = mybir.ActivationFunctionType
AX_X = mybir.AxisListType.X
RMAX = bass.bass_isa.ReduceOp.max

P = 128
D = 1024
KD = D // P
SEQ = 512
NB = SEQ // P
DEC, TDEC = 8, 4
NS = DEC * TDEC
T = SEQ + NS
HALF = T // 2
FF = 2816
KF = FF // P
PAST, PAGE = 1024, 128
PAGES = PAST // PAGE
HA, DH, DV = 8, 64, 128
HR, RK, RV = 4, 128, 256
ALPHA = 2.0 ** 0.25
EPS = 1e-5
LAM_INIT = 0.2
MASKED = -1e30
W_IN_COLS = dict(qa=0, ka=1024, va=2048, qr=3072, kr=3584, vr=4096, gr=5120, ga=6144, gb=7168)
TOKENS = [(P * j, P) for j in range(NB)] + [(SEQ, NS)]

FFN_UP, FFN_DOWN = KF, 12
C_FFN1_UP = 0
C_FFN1_DOWN = C_FFN1_UP + FFN_UP
C_KA = C_FFN1_DOWN + FFN_DOWN
C_VA = C_KA + 4
C_QA = C_VA + 4
C_BRANCH_A = C_QA + 4
C_QR = C_BRANCH_A + 8
C_KR = C_QR + 2
C_VR = C_KR + 2
C_GR = C_VR + 4
C_BRANCH_B = C_GR + 4
C_OUT = C_BRANCH_B + 8
C_FFN2_UP = C_OUT + 4
C_FFN2_DOWN = C_FFN2_UP + FFN_UP
C_END = C_FFN2_DOWN + FFN_DOWN


def constants():
    p = np.arange(P)
    slopes = 2.0 ** -(1.0 + np.arange(HA))
    gamma = 1.0 - 2.0 ** (-5.0 - np.arange(HR))
    t = {}
    t["ident"] = np.eye(P)
    t["ones"] = np.ones((P, P))
    u = np.arange(SEQ)[None, :] - (SEQ - P) - p[:, None]
    t["dist"] = np.where(u <= 0, u, MASKED)
    t["slope8"] = np.broadcast_to(8.0 * slopes, (P, HA))
    t["map_rows"] = np.stack([p < DH, p >= DH], 1)
    row = p % (HA * 2 * TDEC)
    rh, rm, rq = row // (2 * TDEC), row // TDEC % 2, row % TDEC
    past = 8.0 * slopes[rh][:, None] * (np.arange(PAST)[None, :] - PAST - rq[:, None])
    d = np.arange(NS)[None, None, :] - TDEC * np.arange(DEC)[None, :, None]
    new = np.where((d >= 0) & (d <= rq[:, None, None]), 8.0 * slopes[rh][:, None, None] * (d - rq[:, None, None]), MASKED)
    t["bias_dec"] = np.concatenate([past, new.reshape(P, -1)], 1)
    own = (np.arange(HA * TDEC)[None, :] == (TDEC * rh + rq)[:, None])
    t["minus_first"] = -1.0 * (own & (rm == 0)[:, None])
    t["minus_second"] = -1.0 * (own & (rm == 1)[:, None])
    i = np.arange(P)
    dd = i[None, None, :] - p[:, None, None]
    t["decay"] = np.where(dd >= 0, gamma[None, :, None] ** np.maximum(dd, 0), 0.0).reshape(P, -1)
    t["cross"] = np.broadcast_to(gamma[:, None] ** (i[None, :] + 1.0), (P, HR, P)).reshape(P, -1)
    t["kdec"] = gamma[None, :] ** (P - 1.0 - p[:, None])
    js = np.arange(NS)
    same = (p[:, None, None] // TDEC == js[None, None, :] // TDEC) & (js[None, None, :] >= p[:, None, None])
    ds = np.maximum(js[None, None, :] - p[:, None, None], 0)
    t["decay_s"] = np.where(same, gamma[None, :, None] ** ds, 0.0).reshape(P, -1)
    own = p[:, None, None] // TDEC == np.arange(DEC)[None, :, None]
    t["kdec_s"] = np.where(own, gamma[None, None, :] ** (TDEC - 1.0 - (p[:, None, None] % TDEC)), 0.0).reshape(P, -1)
    at, parts = {}, []
    n = 0
    for name, a in t.items():
        a = np.asarray(a, np.float32).reshape(P, -1)
        at[name] = (n, a.shape[1])
        n += a.shape[1]
        parts.append(a)
    return at, np.ascontiguousarray(np.concatenate(parts, 1), np.float32)


def build(nc, x_prompt, x_sample, cache_k, cache_v, state_ret, page_table, ln_g, ln_b, ffn1_w_gu,
          ffn1_w_down, w_in, da_lambda, da_subln_g, w_branch_a, w_branch_b, w_out, ffn2_w_gu,
          ffn2_w_down, const, y_prompt, y_sample, k_prompt, v_prompt, ret_state_prompt, k_sample,
          v_sample, ret_state_sample):
    const_at, _ = constants()
    gamma = [1.0 - 2.0 ** (-5.0 - h) for h in range(HR)]

    with ExitStack() as ctx:
        base = 16512

        def at(name, offset, shape, dt=F32):
            return nc.alloc_sbuf_tensor_at(name, [P, *shape], dt, offset=base + offset)

        def sem(name):
            return ctx.enter_context(nc.semaphore(name))

        ps = ctx.enter_context(nc.psum_tensor("ps", [P, 8, 512], F32))

        w_raw = at("w_raw", 0, [2, KD, 256])
        w_hi_t = at("w_hi_t", 16384, [2, KD, 256], F32R)
        w_lo_t = at("w_lo_t", 32768, [2, KD, 256], F32R)
        xT = at("xT", 49152, [KD, T])
        xh = at("xh", 66560, [KD, T], F32R)
        xl = at("xl", 83968, [KD, T], F32R)
        A = 101376
        hh = at("hh", A, [KF, T], F32R)
        hl = at("hl", A + 47872, [KF, T], F32R)
        xn = at("xn", A, [5, D])
        qaT = at("qaT", A, [HA, T])
        kaT = at("kaT", A + 17408, [HA, T])
        v_nat = at("v_nat", A + 34816, [NB, D])
        v_nat_s = at("v_nat_s", A + 51200, [D])
        k_nat = at("k_nat", A + 55296, [NB, D])
        k_nat_s = at("k_nat_s", A + 71680, [D])
        o_nat = at("o_nat", A + 55296, [NB, D])
        s_sb = at("s_sb", A + 71680, [2, 2, 512])
        p_sb = at("p_sb", A + 79872, [2, 2, 512])
        turned = at("turned", A + 79872, [2, T])
        a_sb = at("a_sb", A + 88064, [2, 512])
        aT = at("aT", A + 92160, [2, 512])
        oaT = at("oaT", A, [KD, T])
        oah = at("oah", A + 17408, [KD, T], F32R)
        oal = at("oal", A + 34816, [KD, T], F32R)
        kt_hi = at("kt_hi", 66560, [2, HA, 256], F32R)
        kt_lo = at("kt_lo", 82944, [2, HA, 256], F32R)
        ident_r = at("ident_r", 99328, [P], F32R)
        minus_first = at("minus_first", 99840, [HA * TDEC])
        minus_second = at("minus_second", 99968, [HA * TDEC])
        map_signs = at("map_signs", A + 94208, [HA * TDEC])
        weights = at("weights", A + 94336, [HA * TDEC])
        k_page = at("k_page", A + 17408, [4, D])
        v_page = at("v_page", A + 34816, [4, D])
        vn_lo = at("vn_lo", A + 51200, [D], F32R)
        vp_hi = at("vp_hi", A + 55296, [2, D], F32R)
        vp_lo = at("vp_lo", A + 63488, [2, D], F32R)
        p_s = at("p_s", A + 71680, [PAST + NS])
        bias_stage = at("bias_stage", A + 71680, [PAST + DEC * NS])
        o_rows = at("o_rows", A + 76800, [D])
        pT = at("pT", A + 80896, [PAGES + 1, P], F32R)
        q_stat = at("q_stat", A + 85504, [1152], F32R)
        vn_hi = at("vn_hi", A + 90112, [D], F32R)
        dec_o = at("dec_o", A + 71680, [2, 256])
        dec_l = at("dec_l", A + 73728, [2, 256])
        sq = at("sq", A + 79872, [2, D])
        mT = at("mT", A, [KD, T])
        mh = at("mh", A + 52224, [KD, T], F32R)
        ml = at("ml", A + 69632, [KD, T], F32R)
        R = A + 17408
        qrT = at("qrT", R, [HR, T])
        krT = at("krT", R + 8704, [HR, T])
        vr_nat = at("vr_nat", R + 17408, [NB, D])
        vr_nat_s = at("vr_nat_s", R + 33792, [D])
        kr_nat = at("kr_nat", R + 37888, [NB, HR * RK])
        kr_nat_s = at("kr_nat_s", R + 46080, [HR * RK])
        rturned = at("rturned", R + 48128, [2, T])
        state = at("state", R + 52480, [2, D])
        or_s = at("or_s", R + 58368, [D])
        or_nat = at("or_nat", R + 62464, [NB, D])
        rsq = at("rsq", R + 17408, [2, D])
        st_in = at("st_in", R + 17408, [4, D])
        st_out = at("st_out", R, [2, D])
        kw_s = at("kw_s", R + 37888, [2, HR * RK])
        onT = at("onT", A + 52224, [KD, T])
        obh = at("obh", A + 17408, [KD, T], F32R)
        obl = at("obl", A + 34816, [KD, T], F32R)
        C = A + 96256
        ident = at("ident", C, [P])
        ones = at("ones", C + 512, [P])
        M = C + 1024
        gated = at("gated", M, [2, T])
        prod = at("prod", M + 4352, [2, T])
        ln_gain = at("ln_gain", M, [D])
        ln_bias = at("ln_bias", M + 4096, [D])
        x_sum = at("x_sum", M, [T])
        x_rs = at("x_rs", M + 2176, [T])
        x_sq = at("x_sq", M + 4352, [2, T])
        bias8 = at("bias8", M, [2, 512])
        q_stage = at("q_stage", M + 4096, [2, 2, P])
        qs_hi = at("qs_hi", M + 6144, [HA, NS], F32R)
        qs_lo = at("qs_lo", M + 7168, [HA, NS], F32R)
        bias_r = at("bias_r", M, [PAST + DEC * NS], F32R)
        decay = at("decay", M, [HR, P])
        cross = at("cross", M + 2048, [HR, P])
        scT = at("scT", M + 4096, [2, HR * P])
        decay_s = at("decay_s", M + 8192, [HR, NS])
        kn_hi = at("kn_hi", C + 9728, [HA, NS], F32R)
        kn_lo = at("kn_lo", C + 10752, [HA, NS], F32R)
        dist = at("dist", C + 11776, [512])
        lam_in = at("lam_in", C + 9728, [4, DH])
        qm = at("qm", C + 9728, [DEC, HR, NS])
        qx = at("qx", C + 9728, [2, HR, P])      
        small = at("small", C + 13824, [240])
        pages = at("pages", C + 14784, [DEC * PAGES], I32)
        ln_cols = at("ln_cols", C + 15040, [4, KD])
        ln_rows = at("ln_rows", M, [P])
        col = {}
        used = [0]

        def tiny(name, n):
            a = used[0]
            used[0] += n
            assert used[0] <= 240
            col[name] = small[:, a:a + n]
            return col[name]

        bn = tiny("bn", 60)
        mv = tiny("mv", 10)
        sd = tiny("sd", 5)
        rstd = tiny("rstd", 5)
        slope8 = tiny("slope8", HA)
        lamv = tiny("lamv", 2)
        map_rows = tiny("map_rows", 2)
        lam_t = tiny("lam_t", 4)
        subln = tiny("subln", 1)
        subln8 = tiny("subln8", 1)
        nmax = tiny("nmax", 4)
        rsum = tiny("rsum", 4)
        rr = tiny("rr", 4)
        ss = bn[:, 0:32]
        ssd = tiny("ssd", 32)
        srs = tiny("srs", 32)
        kdec = tiny("kdec", HR)
        kdec_s = tiny("kdec_s", DEC * HR)
        guard = tiny("guard", 1)

        raw_landed = [sem(f"raw_landed{j}") for j in range(2)]
        hi_split = sem("hi_split")
        lo_split = sem("lo_split")
        gemm_done = sem("gemm_done")
        const_landed = sem("const_landed")
        out_stored = sem("out_stored")

        def score_ps(row):
            return ps[row:row + 64, 2:5, :].rearrange("p a b -> p (a b)")[:, 0:PAST + NS]

        def load_chunk(sp, c, half, j, w, col, row=0, nk=KD):
            sp.wait_ge(lo_split, c + 1)
            src = w[0, row:row + nk * P, :].rearrange("(k p) n -> p k n", p=P)[:, :, bass.ds(col, 256)]
            sp.dma_start(w_raw[:, j, 0:nk], src).then_inc(raw_landed[j], 16)

        def split_hi(act, c, half, j, nk=KD):
            act.wait_ge(raw_landed[j], 16 * half + 16)
            act.wait_ge(gemm_done, 2 * c + 2)
            nc.scalar.copy(w_hi_t[:, j, 0:nk], w_raw[:, j, 0:nk]).then_inc(hi_split, 1)

        def split_lo(dve, c, j, nk=KD):
            dve.wait_ge(hi_split, c + 1)
            nc.vector.tensor_tensor(w_lo_t[:, j, 0:nk], w_raw[:, j, 0:nk], w_hi_t[:, j, 0:nk].bitcast(F32),
                                    ALU.subtract).then_inc(lo_split, 1)

        def chunk_ready(pe, c):
            pe.wait_ge(lo_split, c + 3)

        def gemm(bank, j, n, nk, mh_, ml_, k0=0, start=True, stop=True, tile_ready=None):
            for k in range(nk):
                if tile_ready:
                    tile_ready(k)
                w_cols = slice(n * P, n * P + P)
                for pas, (w, m) in enumerate(((w_hi_t, mh_), (w_hi_t, ml_), (w_lo_t, mh_))):
                    for half in range(2):
                        mm = nc.tensor.matmul(ps[:, bank + half, 0:HALF], w[:, j, k, w_cols],
                                              m[:, k0 + k, half * HALF:half * HALF + HALF],
                                              start=start and k == 0 and pas == 0,
                                              stop=stop and k == nk - 1 and pas == 2)
            mm.then_inc(gemm_done, 1)

        def tile_done(eng, c, n):
            eng.wait_ge(gemm_done, 2 * c + n + 5)

        def banks(b):
            return ps[:, b:b + 2, 0:HALF]

        def halves(tile):
            return tile.rearrange("p (a b) -> p a b", b=HALF)

        class FFN:
            silu_done = sem("ffn_silu_done")
            prod_done = sem("ffn_prod_done")
            h_hi = sem("ffn_h_hi")
            h_lo = sem("ffn_h_lo")
            resid = sem("ffn_resid")

            def __init__(self, index, c_up, w_gu, w_down, last=False):
                self.c, self.gu, self.down, self.last = c_up, w_gu, w_down, last
                self.h0, self.r0 = KF * index, KD * index

            def hidden(self, eng):
                eng.wait_ge(self.h_lo, self.h0 + KF)

            def loads(self, sp):
                c = self.c
                with sp.Fori(0, KF // 2) as i:
                    for j in range(2):
                        load_chunk(sp, c + 2 * i + j, c // 2 + i, j,
                                   self.gu, 256 * i + FF * j)
                c += FFN_UP
                with sp.Fori(0, 2) as q:
                    for m in range(6):
                        r, s = m // 3, m % 3
                        load_chunk(sp, c + 6 * q + m, c // 2 + 3 * q + m // 2, m % 2,
                                   self.down, 512 * q + 256 * r, 8 * s * P, [8, 8, 6][s])

            def pe_part(self, pe, tile_ready=None):
                c = self.c
                with pe.Fori(0, KF // 2) as i:
                    for j in range(2):
                        chunk_ready(pe, c + 2 * i + j)
                        for n in range(2):
                            pe.wait_ge(self.prod_done if j else self.silu_done, self.h0 + 2 * i + n + 1)
                            gemm(4 * j + 2 * n, j, n, KD, xh, xl, tile_ready=None if j or n else tile_ready)
                c += FFN_UP
                pe.wait_ge(self.silu_done, self.h0 + KF + 2)
                with pe.Fori(0, 2) as q:
                    for r in range(2):
                        for s in range(3):
                            m = 3 * r + s
                            chunk_ready(pe, c + 6 * q + m)
                            for n in range(2):
                                if s == 0:
                                    pe.wait_ge(self.resid, self.r0 + 4 * q + 2 * r + n + 1)
                                first = r == 0 and n == 0
                                gemm(4 * r + 2 * n, m % 2, n, [8, 8, 6][s], hh, hl, 8 * s, s == 0, s == 2,
                                     (lambda k: pe.wait_ge(self.h_lo, self.h0 + 8 * s + k + 1)) if first else None)

            def act_part(self, act):
                c = self.c
                with act.Fori(0, KF // 2) as i:
                    for n in range(2):
                        tile_done(act, c + 2 * i, n)
                        act.wait_ge(self.prod_done, self.h0 + 2 * i + n + 1)
                        nc.scalar.activation(halves(gated[:, n]), banks(2 * n), ACT.Silu).then_inc(self.silu_done, 1)
                    split_hi(act, c + 2 * i + 2, c // 2 + i + 1, 0)
                    for n in range(2):
                        act.wait_ge(self.prod_done, self.h0 + 2 * i + n + 3)
                        nc.scalar.copy(hh[:, bass.ds(2 * i + n, 1)], prod[:, n:n + 1]).then_inc(self.h_hi, 1)
                    split_hi(act, c + 2 * i + 3, c // 2 + i + 1, 1)
                c += FFN_UP
                for q in range(2):
                    for m in range(6):
                        nxt = 6 * q + m + 2
                        if not (self.last and nxt >= FFN_DOWN):
                            split_hi(act, c + nxt, (c + nxt) // 2, m % 2, 6 if m % 3 == 0 else KD)

            def dve_part(self, dve, norm=None):
                c = self.c
                with dve.Fori(0, KF // 2) as i:
                    split_lo(dve, c + 2 * i + 2, 0)
                    for n in range(2):
                        tile_done(dve, c + 2 * i + 1, n)
                        dve.wait_ge(self.silu_done, self.h0 + 2 * i + n + 3)
                        nc.vector.tensor_tensor(halves(prod[:, n]), banks(4 + 2 * n), halves(gated[:, n]),
                                                ALU.mult).then_inc(self.prod_done, 1)
                        dve.wait_ge(self.h_hi, self.h0 + 2 * i + n + 1)
                        nc.vector.tensor_tensor(hl[:, bass.ds(2 * i + n, 1)], prod[:, n:n + 1],
                                                hh[:, bass.ds(2 * i + n, 1)].bitcast(F32),
                                                ALU.subtract).then_inc(self.h_lo, 1)
                    split_lo(dve, c + 2 * i + 3, 1)
                c += FFN_UP
                if norm:
                    dve.wait_ge(self.h_lo, self.h0 + KF)
                    norm.dve_clear(dve)
                for q in range(2):
                    for m in range(6):
                        nxt = 6 * q + m + 2
                        r, s = m // 3, m % 3
                        if s == 2:
                            for n in range(2):
                                tile_done(dve, c + 6 * q + m, n)
                                k = 4 * q + 2 * r + n
                                nc.vector.scalar_tensor_tensor(halves(xT[:, k]), banks(4 * r + 2 * n), 0.5 / ALPHA,
                                                               halves(xT[:, k]), ALU.mult, ALU.add
                                                               ).then_inc(self.resid, 1)
                        if s == 2 and norm:
                            for k in (4 * q + 2 * r, 4 * q + 2 * r + 1):
                                dve.wait_ge(self.resid, self.r0 + k + 5)
                                norm.dve_add(dve, k, xT[:, k])
                        if not (self.last and nxt >= FFN_DOWN):
                            split_lo(dve, c + nxt, m % 2, 6 if s == 0 else KD)

        class Norm:

            params = sem("ln_params")
            rows = sem("ln_rows")
            bn = sem("ln_bn")
            mean = sem("ln_mean")
            var = sem("ln_var")
            sd = sem("ln_sd")
            rs = sem("ln_rs")
            normed = sem("ln_normed")
            gained = sem("ln_gained")
            biased = sem("ln_biased")
            turned = sem("ln_turned")
            x_hi = sem("ln_x_hi")
            x_lo = sem("ln_x_lo")

            def __init__(self, index, stats_before, backs_before, stats=True, back=True):
                self.index, self.stats, self.back = index, stats, back
                self.s, self.b = 5 * stats_before, 5 * backs_before

            def back_ps(self, t):
                b, n = 4 + 2 * (t % 2), TOKENS[t][1]
                return ps[:, b:b + 2, :].rearrange("p a (k c) -> p (a k) c", c=P)[:, :, 0:n]

            def load_params(self, sp):
                for src, dst in ((ln_g, ln_gain), (ln_b, ln_bias)):
                    sp.dma_start(dst[:], src[0, self.index:self.index + 1, :].broadcast_to([P, D])
                                 ).then_inc(self.params, 16)

            def row_ready(self, pe, t):
                pe.wait_ge(self.biased, self.s + t + 1)

            def pe_part(self, pe):
                def to_rows(t):
                    if t >= 2:
                        pe.wait_ge(self.normed, self.s + t - 1)
                    t0, n = TOKENS[t]
                    for k in range(KD):
                        mm = nc.tensor.transpose(ps[0:n, 2 * (t % 2) + k // 4, (k % 4) * P:(k % 4) * P + P],
                                                 xT[:, k, t0:t0 + n], ident[:])
                    mm.then_inc(self.rows, 1)

                def to_channels(t):
                    if t >= 2:
                        pe.wait_ge(self.x_hi, self.b + t - 1)
                    self.row_ready(pe, t)
                    n = TOKENS[t][1]
                    for k in range(KD):
                        mm = nc.tensor.transpose(ps[:, 4 + 2 * (t % 2) + k // 4, (k % 4) * P:(k % 4) * P + n],
                                                 xn[0:n, t, k * P:k * P + P], ident[0:n, 0:n])
                    mm.then_inc(self.turned, 1)

                if self.stats:
                    to_rows(0)
                    to_rows(1)
                for t in range(5):
                    if self.stats and 2 <= t + 1 < 5:
                        to_rows(t + 1)
                    if self.back:
                        to_channels(t)

            def ready(self, eng):
                eng.wait_ge(self.x_lo, self.b + 5)

            def act_part(self, act):
                def sqrt(t):
                    n = TOKENS[t][1]
                    act.wait_ge(self.var, self.s + t + 1)
                    nc.scalar.activation(sd[0:n, t:t + 1], mv[0:n, 2 * t + 1:2 * t + 2], ACT.Sqrt
                                         ).then_inc(self.sd, 1)

                def evict(t):
                    t0, n = TOKENS[t]
                    act.wait_ge(self.turned, self.b + t + 1)
                    nc.scalar.copy(xT[:, :, t0:t0 + n], self.back_ps(t))
                    nc.scalar.copy(xh[:, :, t0:t0 + n], self.back_ps(t)).then_inc(self.x_hi, 1)

                def scale(t):
                    n = TOKENS[t][1]
                    act.wait_ge(self.rs, self.s + t + 1)
                    act.wait_ge(self.normed, self.s + t + 1)
                    nc.scalar.mul(xn[0:n, t], xn[0:n, t], rstd[0:n, t:t + 1]).then_inc(self.gained, 1)

                for t in range(5):
                    if self.stats:
                        sqrt(t)
                        scale(t)
                    if self.back:
                        evict(t)
                        if t == 2:
                            split_hi(act, 0, 0, 0)

            def dve_part(self, dve):
                def stats(t):
                    n = TOKENS[t][1]
                    m = slice(2 * t, 2 * t + 2)
                    v = slice(2 * t + 1, 2 * t + 2)
                    dve.wait_ge(self.rows, self.s + t + 1)
                    for a in range(2):
                        nc.vector.bn_stats(bn[0:n, 12 * t + 6 * a:12 * t + 6 * a + 6],
                                           ps[0:n, 2 * (t % 2) + a, :]).then_inc(self.bn, 1)
                    dve.wait_ge(self.bn, 2 * (self.s + t + 1))
                    nc.vector.bn_aggr(mv[0:n, m], bn[0:n, 12 * t:12 * t + 12]).then_inc(self.mean, 1)
                    dve.wait_ge(self.mean, self.s + t + 1)
                    nc.vector.tensor_scalar(mv[0:n, v], mv[0:n, v], EPS / ALPHA ** 2, None, ALU.add
                                            ).then_inc(self.var, 1)

                def norm(t):
                    n = TOKENS[t][1]
                    nc.vector.scalar_tensor_tensor(xn[0:n, t], ps[0:n, 2 * (t % 2):2 * (t % 2) + 2, :].rearrange("p a b -> p (a b)"),
                                                   mv[0:n, 2 * t:2 * t + 1], ln_gain[0:n],
                                                   ALU.subtract, ALU.mult).then_inc(self.normed, 1)
                    dve.wait_ge(self.sd, self.s + t + 1)
                    nc.vector.reciprocal(rstd[0:n, t:t + 1], sd[0:n, t:t + 1]).then_inc(self.rs, 1)

                def low(t):
                    t0, n = TOKENS[t]
                    dve.wait_ge(self.x_hi, self.b + t + 1)
                    nc.vector.tensor_tensor(xl[:, :, t0:t0 + n], xT[:, :, t0:t0 + n],
                                            xh[:, :, t0:t0 + n].bitcast(F32), ALU.subtract).then_inc(self.x_lo, 1)

                if self.stats:
                    dve.wait_ge(self.params, 32)
                    stats(0)
                for t in range(5):
                    if self.stats:
                        norm(t)
                        if t + 1 < 5:
                            stats(t + 1)
                    if self.back and t >= 1:
                        low(t - 1)
                        if t == 3:
                            split_lo(dve, 0, 0)
                if self.back:
                    low(4)

            def pool_part(self, pool):
                for t in range(5):
                    n = TOKENS[t][1]
                    pool.wait_ge(self.gained, self.s + t + 1)
                    nc.gpsimd.tensor_tensor(xn[0:n, t], xn[0:n, t], ln_bias[0:n], ALU.add).then_inc(self.biased, 1)

        class ChannelNorm:

            added = sem("cn_added")
            mean = sem("cn_mean")
            centered = sem("cn_centered")
            squared = sem("cn_squared")
            sq_used = sem("cn_sq_used")
            sd = sem("cn_sd")
            rs = sem("cn_rs")
            scaled = sem("cn_scaled")
            y_hi = sem("cn_y_hi")
            y = sem("cn_y")
            x_lo = sem("cn_x_lo")

            def __init__(self, i):
                self.i = i

            def gain(self, k):
                return ln_cols[:, self.i, k:k + 1]

            def bias(self, k):
                return ln_cols[:, 2 + self.i, k:k + 1]

            def dve_clear(self, dve):
                nc.vector.memset(x_sum[:], 0.0).then_inc(self.added, 1)

            def dve_add(self, dve, k, tile):
                dve.wait_ge(self.added, (KD + 1) * self.i + k + 1)
                nc.vector.tensor_tensor(x_sum[:], x_sum[:], tile, ALU.add).then_inc(self.added, 1)

            def pe_part(self, pe):
                pe.wait_ge(self.added, (KD + 1) * (self.i + 1))
                for a in range(2):
                    mm = nc.tensor.matmul(ps[:, a, 0:HALF], ones[:], x_sum[:, a * HALF:a * HALF + HALF],
                                          start=True, stop=True)
                mm.then_inc(self.mean, 1)
                for k in range(KD):
                    pe.wait_ge(self.squared, KD * self.i + k + 1)
                    for a in range(2):
                        mm = nc.tensor.matmul(ps[:, 2 + a, 0:HALF], ones[:], x_sq[:, k % 2, a * HALF:a * HALF + HALF],
                                              start=k == 0, stop=k == KD - 1)
                    mm.then_inc(self.sq_used, 1)

            def ready(self, eng, k=KD - 1):
                eng.wait_ge(self.x_lo, KD * self.i + k + 1)

            def act_part(self, act):
                nc.scalar.activation(sd[:, 1:2], guard[:], ACT.Sqrt)
                for k in range(KD):
                    act.wait_ge(self.centered, KD * self.i + k + 1)
                    act.wait_ge(self.sq_used, KD * self.i + k + 1)
                    nc.scalar.activation(x_sq[:, k % 2], xT[:, k], ACT.Square).then_inc(self.squared, 1)
                act.wait_ge(self.sq_used, KD * (self.i + 1) + 2)
                nc.scalar.activation(halves(x_rs[:]), banks(2), ACT.Sqrt, bias=guard[:], scale=1.0 / D
                                     ).then_inc(self.sd, 1)
                for k in range(KD):
                    act.wait_ge(self.scaled, KD * self.i + k + 1)
                    nc.scalar.activation(xh[:, k], xT[:, k], ACT.Identity, bias=self.bias(k)).then_inc(self.y_hi, 1)
                    nc.scalar.activation(xT[:, k], xT[:, k], ACT.Identity, bias=self.bias(k)).then_inc(self.y, 1)

            def dve_part(self, dve):
                dve.wait_ge(self.mean, self.i + 1)
                for k in range(KD):
                    nc.vector.scalar_tensor_tensor(halves(xT[:, k]), banks(0), -1.0 / D, halves(xT[:, k]),
                                                   ALU.mult, ALU.add).then_inc(self.centered, 1)
                dve.wait_ge(self.sd, self.i + 1)
                nc.vector.reciprocal(x_rs[:], x_rs[:]).then_inc(self.rs, 1)
                dve.wait_ge(self.rs, self.i + 1)

                def scale(k):
                    nc.vector.scalar_tensor_tensor(xT[:, k], xT[:, k], self.gain(k), x_rs[:], ALU.mult, ALU.mult
                                                   ).then_inc(self.scaled, 1)

                def low(k):
                    dve.wait_ge(self.y, KD * self.i + k + 1)
                    nc.vector.tensor_tensor(xl[:, k], xT[:, k], xh[:, k].bitcast(F32), ALU.subtract
                                            ).then_inc(self.x_lo, 1)
                scale(0)
                scale(1)
                for k in range(KD):
                    low(k)
                    if k + 2 < KD:
                        scale(k + 2)
        class Project:

            taken = sem("pr_taken")
            rows = sem("pr_rows")
            stored = sem("pr_stored")
            kept = sem("pr_kept")
            counted = [0, 0, 0]

            def __init__(self, c, n_chunks, stage=None, nat=None, nat_s=None, keep=None, direct=None, scale=1.0):
                self.c, self.rounds = c, n_chunks // 2
                self.stage, self.nat, self.nat_s, self.keep, self.direct = stage, nat, nat_s, keep, direct
                self.scale = scale
                self.tiles = 2 * n_chunks
                self.t0, self.r0, self.k0 = self.counted
                self.counted[0] += self.tiles
                self.counted[1] += self.tiles * (nat is not None)
                self.counted[2] += self.tiles * (keep is not None)

            def all_taken(self, eng):
                eng.wait_ge(self.taken, self.t0 + self.tiles + 2)

            def all_kept(self, eng):
                eng.wait_ge(self.kept, self.k0 + self.tiles + 2)

            def loads(self, sp, col):
                for i in range(self.rounds):
                    for j in range(2):
                        load_chunk(sp, self.c + 2 * i + j, self.c // 2 + i, j,
                                   w_in, col + 512 * i + 256 * j)

            def turn(self, pe, u):
                pe.wait_ge(self.taken, self.t0 + u + 3)
                pe.wait_ge(self.stored, self.r0 + u + 1)
                b = 4 + 2 * (u % 2)
                for blk in range(NB):
                    nc.tensor.transpose(ps[:, b, blk * P:blk * P + P], self.stage[:, u % 2, blk * P:blk * P + P],
                                        ident[:])
                nc.tensor.transpose(ps[0:NS, b + 1, 0:P], self.stage[:, u % 2, SEQ:T], ident[:]
                                    ).then_inc(self.rows, 1)

            def pe_part(self, pe, tile_ready=None, before=None):
                for u in range(self.tiles):
                    if u % 2 == 0:
                        chunk_ready(pe, self.c + u // 2)
                    pe.wait_ge(self.taken, self.t0 + u + 1)
                    gemm(2 * (u % 2), (u // 2) % 2, u % 2, KD, xh, xl, tile_ready=None if u else tile_ready)
                    if u == 0 and before is not None:
                        before.turn(pe, before.tiles - 1)
                    if self.nat is not None and u > 0:
                        self.turn(pe, u - 1)

            def act_part(self, act):
                with act.Fori(0, self.rounds) as i:
                    for t in range(4):
                        c = self.c + 2 * i + t // 2
                        tile_done(act, c, t % 2)
                        if self.nat is not None:
                            act.wait_ge(self.rows, self.r0 + 4 * i + t + 1)
                            if self.keep is not None:
                                act.wait_ge(self.kept, self.k0 + 4 * i + t + 1)
                            dst = self.stage[:, t % 2:t % 2 + 1]
                        else:
                            dst = self.direct[:, bass.ds(4 * i + t, 1)]
                        nc.scalar.mul(dst.rearrange("p o (a b) -> p (o a) b", b=HALF), banks(2 * (t % 2)), self.scale
                                      ).then_inc(self.taken, 1)
                        if t % 2 == 1:
                            split_hi(act, c + 2, self.c // 2 + i + 1, t // 2)

            def dve_part(self, dve):
                with dve.Fori(0, self.rounds) as i:
                    for t in range(4):
                        c = self.c + 2 * i + t // 2
                        if t % 2 == 1:
                            split_lo(dve, c + 2, t // 2)
                        if self.nat is not None:
                            b = 4 + 2 * (t % 2)
                            dve.wait_ge(self.rows, self.r0 + 4 * i + t + 3)
                            nc.vector.tensor_copy(self.nat[:, :, bass.ds(512 * i + P * t, P)],
                                                  ps[:, b, :].rearrange("p (a b) -> p a b", b=P))
                            nc.vector.tensor_copy(self.nat_s[0:NS, bass.ds(512 * i + P * t, P)],
                                                  ps[0:NS, b + 1, 0:P]).then_inc(self.stored, 1)

            def pool_part(self, pool):
                with pool.Fori(0, self.rounds) as i:
                    for t in range(4):
                        pool.wait_ge(self.taken, self.t0 + 4 * i + t + 3)
                        nc.gpsimd.tensor_copy(self.keep[:, bass.ds(4 * i + t, 1)], self.stage[:, t % 2:t % 2 + 1]
                                              ).then_inc(self.kept, 1)

            def all_stored(self, eng):
                eng.wait_ge(self.stored, self.r0 + self.tiles + 2)

        class Branch:
            sig_done = sem("br_sig_done")
            prod_done = sem("br_prod_done")
            merged = sem("br_merged")
            m_hi = sem("br_m_hi")
            m_lo = sem("br_m_lo")

            def __init__(self, c, col, w, oh, ol, add):
                self.c, self.col, self.w, self.oh, self.ol, self.add = c, col, w, oh, ol, add
                self.t0 = KD * add

            def loads(self, sp, first, last):
                for i in range(first, last):
                    load_chunk(sp, self.c + 2 * i, self.c // 2 + i, 0,
                               w_in, self.col + 256 * i)
                    load_chunk(sp, self.c + 2 * i + 1, self.c // 2 + i, 1,
                               self.w, 256 * i)

            def pe_gate(self, pe, i, n):
                if n == 0:
                    chunk_ready(pe, self.c + 2 * i)
                pe.wait_ge(self.sig_done, self.t0 + 2 * i + n + 1)
                gemm(2 * n, 0, n, KD, xh, xl)

            def pe_branch(self, pe, i, tile_ready=None):
                chunk_ready(pe, self.c + 2 * i + 1)
                for n in range(2):
                    pe.wait_ge(self.prod_done, self.t0 + 2 * i + n + 1)
                    gemm(4 + 2 * n, 1, n, KD, self.oh, self.ol, tile_ready=None if n else tile_ready)

            def pe_part(self, pe, tile_ready):
                with pe.Fori(0, KD // 2 - 1) as i:
                    self.pe_branch(pe, i, tile_ready)
                    for n in range(2):
                        self.pe_gate(pe, i + 1, n)
                self.pe_branch(pe, KD // 2 - 1)

            def act_part(self, act):
                with act.Fori(0, KD // 2) as i:
                    for n in range(2):
                        tile_done(act, self.c + 2 * i, n)
                        act.wait_ge(self.prod_done, self.t0 + 2 * i + n + 1)
                        nc.scalar.activation(halves(gated[:, n]), banks(2 * n), ACT.Sigmoid).then_inc(self.sig_done, 1)
                    split_hi(act, self.c + 2 * i + 2, self.c // 2 + i + 1, 0)
                    if self.add:
                        for n in range(2):
                            act.wait_ge(self.merged, 2 * i + n + 1)
                            nc.scalar.copy(mh[:, bass.ds(2 * i + n, 1)], prod[:, n:n + 1]).then_inc(self.m_hi, 1)
                    split_hi(act, self.c + 2 * i + 3, self.c // 2 + i + 1, 1)

            def dve_part(self, dve):
                with dve.Fori(0, KD // 2) as i:
                    split_lo(dve, self.c + 2 * i + 2, 0)
                    for n in range(2):
                        k = bass.ds(2 * i + n, 1)
                        tile_done(dve, self.c + 2 * i + 1, n)
                        dve.wait_ge(self.sig_done, self.t0 + 2 * i + n + 3)
                        dst = prod[:, n:n + 1] if self.add else mT[:, k]
                        nc.vector.tensor_tensor(dst.rearrange("p o (a b) -> p (o a) b", b=HALF), banks(4 + 2 * n),
                                                halves(gated[:, n]), ALU.mult).then_inc(self.prod_done, 1)
                        if self.add:
                            dve.wait_ge(self.prod_done, self.t0 + 2 * i + n + 3)
                            nc.vector.tensor_tensor(prod[:, n:n + 1], prod[:, n:n + 1], mT[:, k], ALU.add
                                                    ).then_inc(self.merged, 1)
                            dve.wait_ge(self.m_hi, 2 * i + n + 1)
                            nc.vector.tensor_tensor(ml[:, k], prod[:, n:n + 1], mh[:, k].bitcast(F32), ALU.subtract
                                                    ).then_inc(self.m_lo, 1)
                    split_lo(dve, self.c + 2 * i + 3, 1)

        class HeadNorm:
            sq_done = sem("hn_sq_done")
            summed = sem("hn_summed")
            guarded = sem("hn_guarded")
            sd = sem("hn_sd")
            rs = sem("hn_rs")
            scaled = sem("hn_scaled")
            turned = sem("hn_turned")
            evicted = sem("hn_evicted")

            def __init__(self, b0, p0, blocks, squares, n):
                self.b0, self.p0 = b0, p0
                self.blocks, self.squares, self.n, self.g = blocks, squares, n, D // n
                full = sum(n == P for _, _, n in blocks)
                self.parts = [(P, slice(0, full * self.g))]
                if full < len(blocks):
                    self.parts.append((NS, slice(full * self.g, (full + 1) * self.g)))

            def act_squares(self, act):
                nc.scalar.activation(sd[:, 0:1], guard[:], ACT.Sqrt)
                for b, (src, _, r) in enumerate(self.blocks):
                    act.wait_ge(self.summed, self.b0 + b + 1)
                    nc.scalar.activation(self.squares[0:r, b % 2], src, ACT.Square).then_inc(self.sq_done, 1)
                for p, (r, c) in enumerate(self.parts):
                    act.wait_ge(self.guarded, self.p0 + p + 1)
                    nc.scalar.activation(ssd[0:r, c], ss[0:r, c], ACT.Sqrt).then_inc(self.sd, 1)

            def dve_scale(self, dve):
                g, n = self.g, self.n
                for b, (_, _, r) in enumerate(self.blocks):
                    dve.wait_ge(self.sq_done, self.b0 + b + 1)
                    nc.vector.tensor_reduce(ss[0:r, b * g:b * g + g],
                                            self.squares[0:r, b % 2].rearrange("p (h d) -> p h d", d=n), AX_X, ALU.add
                                            ).then_inc(self.summed, 1)
                dve.wait_ge(self.summed, self.b0 + len(self.blocks) + 2)
                for r, c in self.parts:
                    nc.vector.tensor_scalar(ss[0:r, c], ss[0:r, c], 1.0 / n, EPS, ALU.mult, ALU.add
                                            ).then_inc(self.guarded, 1)
                for p, (r, c) in enumerate(self.parts):
                    dve.wait_ge(self.sd, self.p0 + p + 1)
                    nc.vector.reciprocal(srs[0:r, c], ssd[0:r, c]).then_inc(self.rs, 1)
                dve.wait_ge(self.rs, self.p0 + len(self.parts))
                for b, (src, _, r) in enumerate(self.blocks):
                    rows = src.rearrange("p (h d) -> p h d", d=n)
                    nc.vector.tensor_tensor(rows, rows, srs[0:r, b * g:b * g + g].unsqueeze(2).broadcast_to([r, g, n]),
                                            ALU.mult).then_inc(self.scaled, 1)

            def pe_part(self, pe):
                for b, (src, _, r) in enumerate(self.blocks):
                    pe.wait_ge(self.scaled, self.b0 + b + 1)
                    if b >= 2:
                        pe.wait_ge(self.evicted, self.b0 + b - 1)
                    for k in range(KD):
                        mm = nc.tensor.transpose(ps[:, 2 * (b % 2) + k // 4, (k % 4) * P:(k % 4) * P + r],
                                                 src[:, k * P:k * P + P], ident[0:r, 0:r])
                    mm.then_inc(self.turned, 1)

            def all_evicted(self, eng):
                eng.wait_ge(self.evicted, self.b0 + len(self.blocks))

            def act_evict(self, act, dst, scale=1.0):
                for b, (_, t0, r) in enumerate(self.blocks):
                    act.wait_ge(self.turned, self.b0 + b + 1)
                    src = ps[:, 2 * (b % 2):2 * (b % 2) + 2, :].rearrange("p a (k c) -> p (a k) c", c=P)[:, :, 0:r]
                    nc.scalar.mul(dst[:, :, t0:t0 + r], src, scale).then_inc(self.evicted, 1)

        class Split:
            hi_done, lo_done = sem("sp_hi_done"), sem("sp_lo_done")

            def __init__(self, index, src, hi, lo):
                self.src, self.hi, self.lo = src, hi, lo
                self.s0 = KD // 2 * index

            def act_pair(self, act, q):
                k = 2 * q
                nc.scalar.copy(self.hi[:, k:k + 2], self.src[:, k:k + 2]).then_inc(self.hi_done, 1)

            def dve_pair(self, dve, q):
                k = 2 * q
                dve.wait_ge(self.hi_done, self.s0 + q + 1)
                nc.vector.tensor_tensor(self.lo[:, k:k + 2], self.src[:, k:k + 2],
                                        self.hi[:, k:k + 2].bitcast(F32), ALU.subtract).then_inc(self.lo_done, 1)

            def act_part(self, act):
                for q in range(KD // 2):
                    self.act_pair(act, q)

            def dve_part(self, dve):
                for q in range(KD // 2):
                    self.dve_pair(dve, q)

            def ready(self, pe, k=KD - 1):
                pe.wait_ge(self.lo_done, self.s0 + k // 2 + 1)

        class PromptAttention:
            def __init__(self):
                self.q_staged = sem("pa_q_staged")
                self.bias_set = sem("pa_bias_set")
                self.scored = sem("pa_scored")
                self.scaled = sem("pa_scaled")
                self.exped = sem("pa_exped")
                self.recip = sem("pa_recip")
                self.lammed = sem("pa_lammed")
                self.second = sem("pa_second")
                self.combined = sem("pa_combined")
                self.turned = sem("pa_turned")
                self.aT_set = sem("pa_aT_set")
                self.pv = sem("pa_pv")
                self.o_set = sem("pa_o_set")

            def keys(self, i):
                return P * (i + 1)

            def pool_unit(self, pool, i, h, s, u):
                pool.wait_ge(self.scored, u + 1)
                nc.gpsimd.tensor_tensor(q_stage[:, s], qaT[:, h, P * i:P * i + P].broadcast_to([P, 2, P]),
                                        map_rows[:].unsqueeze(2).broadcast_to([P, 2, P]), ALU.mult
                                        ).then_inc(self.q_staged, 1)
                n = self.keys(i)
                pool.wait_ge(self.scaled, u + 1)
                nc.gpsimd.tensor_tensor(bias8[:, s:s + 1, 0:n], dist[:, SEQ - n:SEQ].unsqueeze(1),
                                        slope8[:, h].unsqueeze(2).broadcast_to([P, 1, n]), ALU.mult
                                        ).then_inc(self.bias_set, 1)

            def pool_part(self, pool):
                for i in range(NB):
                    with pool.Fori(0, HA // 2) as hp:
                        for s in range(2):
                            self.pool_unit(pool, i, bass.ds(2 * hp + s, 1), s, HA * i + 2 * hp + s)

            def scores(self, pe, i, h, s, u):
                n = self.keys(i)
                pe.wait_ge(self.q_staged, u + 1)
                pe.wait_ge(self.scaled, u + 1)
                for m in range(2):
                    mm = nc.tensor.matmul(ps[:, 2 * s + m, 0:n], q_stage[:, s, m], kaT[:, h, 0:n], start=True, stop=True)
                mm.then_inc(self.scored, 1)

            def turn(self, pe, i, s, u):
                pe.wait_ge(self.combined, u + 3)
                pe.wait_ge(self.aT_set, u + 1)
                for j in range(i + 1):
                    mm = nc.tensor.transpose(ps[:, 4 + s, P * j:P * j + P], a_sb[:, s, P * j:P * j + P], ident[:])
                mm.then_inc(self.turned, 1)

            def values(self, pe, i, h, s, u):
                pe.wait_ge(self.aT_set, u + 3)
                pe.wait_ge(self.o_set, u + 1)
                for j in range(i + 1):
                    mm = nc.tensor.matmul(ps[:, 6 + s, 0:DV], aT[:, s, P * j:P * j + P],
                                          v_nat[:, j, bass.ds(h * DV, DV)], start=j == 0, stop=j == i)
                mm.then_inc(self.pv, 1)

            def pe_part(self, pe):
                def head(h):
                    return bass.ds(h, 1)
                self.scores(pe, 0, head(0), 0, 0)
                self.scores(pe, 0, head(1), 1, 1)
                for i in range(NB):
                    u0 = HA * i
                    with pe.Fori(0, HA // 2 - 1) as hp:
                        for s in range(2):
                            self.scores(pe, i, head(2 * hp + s + 2), s, u0 + 2 * hp + s + 2)
                            self.turn(pe, i, s, u0 + 2 * hp + s)
                            self.values(pe, i, 2 * hp + s, s, u0 + 2 * hp + s)
                    for s in range(2):
                        if i + 1 < NB:
                            self.scores(pe, i + 1, head(s), s, u0 + HA + s)
                        self.turn(pe, i, s, u0 + HA - 2 + s)
                        self.values(pe, i, HA - 2 + s, s, u0 + HA - 2 + s)

            def scale(self, dve, i, s, u):
                n = self.keys(i)
                dve.wait_ge(self.scored, u + 3)
                dve.wait_ge(self.bias_set, u + 1)
                dve.wait_ge(self.exped, u + 1)
                nc.vector.memset(rsum[:, 2 * s:2 * s + 2], 0.0)
                for m in range(2):
                    ins = nc.vector.tensor_tensor_reduce(s_sb[:, s, m, 0:n], ps[:, 2 * s + m, 0:n], bias8[:, s, 0:n],
                                                         -DH ** -0.5, -MASKED, ALU.add, ALU.min,
                                                         nmax[:, 2 * s + m:2 * s + m + 1])
                ins.then_inc(self.scaled, 1)

            def combine(self, dve, i, s, u):
                n = self.keys(i)
                r = slice(2 * s, 2 * s + 2)
                dve.wait_ge(self.exped, u + 3)
                nc.vector.reciprocal(rr[:, r], rsum[:, r]).then_inc(self.recip, 1)
                dve.wait_ge(self.recip, u + 1)
                nc.vector.tensor_tensor(rr[:, r], rr[:, r], lamv[:], ALU.mult).then_inc(self.lammed, 1)
                dve.wait_ge(self.lammed, u + 1)
                nc.vector.tensor_scalar(p_sb[:, s, 1, 0:n], p_sb[:, s, 1, 0:n], rr[:, 2 * s + 1:2 * s + 2], None,
                                        ALU.mult).then_inc(self.second, 1)
                dve.wait_ge(self.second, u + 1)
                dve.wait_ge(self.turned, u + 1)
                nc.vector.scalar_tensor_tensor(a_sb[:, s, 0:n], p_sb[:, s, 0, 0:n], rr[:, 2 * s:2 * s + 1],
                                               p_sb[:, s, 1, 0:n], ALU.mult, ALU.subtract).then_inc(self.combined, 1)

            def dve_part(self, dve):
                self.scale(dve, 0, 0, 0)
                for i in range(NB):
                    u0 = HA * i
                    with dve.Fori(0, HA // 2 - 1) as hp:
                        for s in range(2):
                            self.scale(dve, i, 1 - s, u0 + 2 * hp + s + 1)
                            self.combine(dve, i, s, u0 + 2 * hp + s)
                    self.scale(dve, i, 1, u0 + HA - 1)
                    self.combine(dve, i, 0, u0 + HA - 2)
                    if i + 1 < NB:
                        self.scale(dve, i + 1, 0, u0 + HA)
                    self.combine(dve, i, 1, u0 + HA - 1)

            def exp(self, act, i, s, u):
                n = self.keys(i)
                act.wait_ge(self.scaled, u + 3)
                act.wait_ge(self.combined, u + 1)
                for m in range(2):
                    k = slice(2 * s + m, 2 * s + m + 1)
                    ins = nc.scalar.activation(p_sb[:, s, m, 0:n], s_sb[:, s, m, 0:n], ACT.Exp, bias=nmax[:, k],
                                               scale=-1.0, accum_out=rsum[:, k])
                ins.then_inc(self.exped, 1)

            def keep_turned(self, act, i, s, u):
                n = self.keys(i)
                act.wait_ge(self.turned, u + 3)
                act.wait_ge(self.pv, u + 1)
                nc.scalar.copy(aT[:, s, 0:n], ps[:, 4 + s, 0:n]).then_inc(self.aT_set, 1)

            def keep_output(self, act, s, u, i, h):
                act.wait_ge(self.pv, u + 3)
                nc.scalar.copy(o_nat[:, i, bass.ds(h * DV, DV)], ps[:, 6 + s, 0:DV]).then_inc(self.o_set, 1)

            def act_part(self, act):
                self.exp(act, 0, 0, 0)
                for i in range(NB):
                    u0 = HA * i
                    self.exp(act, i, 1, u0 + 1)
                    self.keep_turned(act, i, 0, u0)
                    if i:
                        self.keep_output(act, 1, u0 - 1, i - 1, HA - 1)
                    with act.Fori(0, HA // 2 - 1) as hp:
                        for s in range(2):
                            h = 2 * hp + 1 + s
                            self.exp(act, i, s, u0 + h + 1)
                            self.keep_turned(act, i, 1 - s, u0 + h)
                            self.keep_output(act, s, u0 + h - 1, i, h - 1)
                    if i + 1 < NB:
                        self.exp(act, i + 1, 0, u0 + HA)
                    self.keep_turned(act, i, 1, u0 + HA - 1)
                    self.keep_output(act, 0, u0 + HA - 2, i, HA - 2)
                self.keep_output(act, 1, HA * NB - 1, NB - 1, HA - 1)

            def credits_pe(self, pe):
                pe.sem_inc(self.scored, 2)
                pe.sem_inc(self.turned, 2)
                pe.sem_inc(self.pv, 2)

            def credits_dve(self, dve):
                dve.sem_inc(self.scaled, 2)
                dve.sem_inc(self.combined, 2)

            def credits_act(self, act):
                act.sem_inc(self.exped, 2)
                act.sem_inc(self.aT_set, 2)
                act.sem_inc(self.o_set, 2)

        ROWS = HA * 2 * TDEC
        NKEYS = PAST + NS

        class DecodeAttention:
            def __init__(self):
                self.k_landed = [sem(f"da_k_landed{r}") for r in range(4)]
                self.v_landed = [sem(f"da_v_landed{r}") for r in range(4)]
                self.qk_hi, self.qk_lo = sem("da_qk_hi"), sem("da_qk_lo")
                self.setup = sem("da_setup")
                self.vn_hi, self.vn_lo = sem("da_vn_hi"), sem("da_vn_lo")
                self.k_half = sem("da_k_half")
                self.kT_hi = sem("da_kT_hi")
                self.kT_lo = sem("da_kT_lo")
                self.q_built = sem("da_q_built")
                self.scored = sem("da_scored")
                self.s_low = sem("da_s_low")
                self.s_min = sem("da_s_min")
                self.exped = sem("da_exped")
                self.p_turned = sem("da_p_turned")
                self.pT_hi = sem("da_pT_hi")
                self.pT_lo = sem("da_pT_lo")
                self.v_hi = sem("da_v_hi")
                self.v_lo = sem("da_v_lo")
                self.pv = sem("da_pv")
                self.o_done = sem("da_o_done")
                self.o_kept = sem("da_o_kept")
                self.coef = sem("da_coef")
                self.weighed = sem("da_weighed")
                self.merged = sem("da_merged")
                self.fin = sem("da_fin")
                self.fin_ss = sem("da_fin_ss")
                self.fin_sd = sem("da_fin_sd")
                self.oa_set = sem("da_oa_set")

            def load_page(self, sp, cache, ring, landed, free, steps, b, g):
                page = sp.value_load(pages[0:1, bass.ds(PAGES * b + g, 1)], min_val=0, max_val=cache.shape[1] - 1)
                sp.wait_ge(free, steps * PAGES * b + steps * (g + 1))
                sp.dma_start(ring[:, g % 4], cache[0, bass.ds(page, 1)].rearrange("o p h d -> p (o h d)")
                             ).then_inc(landed[g % 4], 16)

            def load_k(self, sp, b, g):
                self.load_page(sp, cache_k, k_page, self.k_landed, self.k_half, 2, b, g)

            def load_v(self, sp, b, g):
                self.load_page(sp, cache_v, v_page, self.v_landed, self.v_lo, 1, b, g)

            def sp_step(self, sp, b):
                for g in range(0, PAGES, 2):
                    for n in (g, g + 1):
                        self.load_k(sp, b, n)
                    for n in (g, g + 1):
                        self.load_v(sp, b - 1, n)

            def sp_part(self, sp):
                for g in range(4):
                    self.load_k(sp, 0, g)
                sp.wait_ge(attn.pv, HA * NB + 2)
                sp.wait_ge(v_stored, 32)
                for g in range(4, PAGES):
                    self.load_k(sp, 0, g)
                with sp.Fori(1, DEC) as b:
                    self.sp_step(sp, b)
                for g in range(PAGES):
                    self.load_v(sp, DEC - 1, g)

            def turn(self, pe, b, g):
                for half in range(2):
                    if half == 0:
                        pe.wait_ge(self.k_landed[g % 4], 32 * b + 16 * (g // 4) + 16)
                    pe.wait_ge(self.kT_lo, 16 * b + 2 * g + half + 1)
                    for h in range(4):
                        mm = nc.tensor.transpose(ps[:, half, h * P:h * P + P],
                                                 k_page[:, g % 4, (4 * half + h) * P:(4 * half + h) * P + P], ident[:])
                    mm.then_inc(self.k_half, 1)

            def score_pair(self, pe, b, q):
                pe.wait_ge(self.kT_lo, 16 * b + 4 * q + 6)
                if q == 0:
                    pe.wait_ge(self.q_built, 4 * b + 4)
                    pe.wait_ge(self.s_min, b + 1)
                dst = ps[:, 2 + q // 2, 256 * (q % 2):256 * (q % 2) + 256]
                nc.tensor.matmul(dst, ident_r[0:ROWS], bias_r[0:ROWS, 256 * q:256 * q + 256], start=True, stop=False)
                for h in range(HA):
                    for kt in (kt_hi, kt_lo):
                        mm = nc.tensor.matmul(dst, q_stat[:, P * h:P * h + P], kt[:, q % 2, h],
                                              start=False, stop=h == HA - 1 and kt is kt_lo)
                mm.then_inc(self.scored, 1)

            def score_new(self, pe, b):
                dst = ps[:, 4, 0:NS]
                nc.tensor.matmul(dst, ident_r[0:ROWS], bias_r[0:ROWS, bass.ds(NS * b + PAST, NS)], start=True, stop=False)
                for h in range(HA):
                    for kn in (kn_hi, kn_lo):
                        nc.tensor.matmul(dst, q_stat[:, P * h:P * h + P], kn[:, h],
                                         start=False, stop=h == HA - 1 and kn is kn_lo)

            def turn_p(self, pe, b):
                pe.wait_ge(self.exped, b + 1)
                pe.wait_ge(self.pT_lo, 2 * b + 2)
                nc.tensor.matmul(ps[:, 5, 0:ROWS], p_s[:, 0:P], ident[:, 0:ROWS], start=True, stop=True)
                for g in range(1, PAGES):
                    nc.tensor.transpose(ps[:, 5, ROWS * g:ROWS * g + ROWS], p_s[0:ROWS, P * g:P * g + P],
                                        ident[0:ROWS, 0:ROWS])
                nc.tensor.transpose(ps[0:NS, 4, NS:NS + ROWS], p_s[0:ROWS, PAST:NKEYS], ident[0:ROWS, 0:ROWS]
                                    ).then_inc(self.p_turned, 1)

            def values(self, pe, b, g):
                if g == 0:
                    pe.wait_ge(self.pT_lo, 2 * b + 4)
                    pe.wait_ge(self.o_kept, b + 1)
                pe.wait_ge(self.v_lo, PAGES * b + g + 5)
                for half in range(2):
                    for v in (vp_hi, vp_lo):
                        mm = nc.tensor.matmul(ps[:, 6 + half, :], pT[:, g], v[:, g % 2, 512 * half:512 * half + 512],
                                              start=g == 0 and v is vp_hi, stop=False)
                mm.then_inc(self.pv, 1)

            def values_new(self, pe, b):
                for half in range(2):
                    for v in (vn_hi, vn_lo):
                        mm = nc.tensor.matmul(ps[:, 6 + half, :], pT[0:NS, PAGES], v[0:NS, 512 * half:512 * half + 512],
                                              start=False, stop=v is vn_lo)
                mm.then_inc(self.o_done, 1)

            def merge(self, pe, b):
                pe.wait_ge(self.o_kept, b + 2)
                pe.wait_ge(self.weighed, b + 1)
                for h in range(HA):
                    mm = nc.tensor.matmul(ps[:, 4, bass.ds(32 * b + (256 + TDEC * h), TDEC)],
                                          o_rows[:, P * h:P * h + P], weights[:, TDEC * h:TDEC * h + TDEC],
                                          start=True, stop=True)
                mm.then_inc(self.merged, 1)

            def pe_step(self, pe, b, past=True, older=True):
                self.turn(pe, b, 0)
                self.turn(pe, b, 1)
                if past:
                    self.turn_p(pe, b - 1)
                for q in range(PAGES // 2):
                    last = q == PAGES // 2 - 1
                    if last:
                        self.score_new(pe, b)
                    else:
                        self.turn(pe, b, 2 * q + 2)
                    self.score_pair(pe, b, q)
                    if older and q == 0:
                        pe.wait_ge(self.pT_lo, 2 * b + 2)
                        self.merge(pe, b - 2)
                    if not last:
                        self.turn(pe, b, 2 * q + 3)
                    if past:
                        self.values(pe, b - 1, 2 * q)
                        self.values(pe, b - 1, 2 * q + 1)
                if past:
                    self.values_new(pe, b - 1)

            def pe_part(self, pe):
                pe.wait_ge(self.setup, 5)
                pe.wait_ge(self.qk_lo, 2)
                pe.wait_ge(self.vn_lo, 1)
                self.pe_step(pe, 0, past=False, older=False)
                self.pe_step(pe, 1, older=False)
                with pe.Fori(2, DEC) as b:
                    self.pe_step(pe, b)
                self.merge(pe, DEC - 2)
                self.turn_p(pe, DEC - 1)
                for g in range(PAGES):
                    self.values(pe, DEC - 1, g)
                    if g == 3:
                        split_x.ready(pe)
                        branch_a.pe_gate(pe, 0, 0)
                self.values_new(pe, DEC - 1)
                self.merge(pe, DEC - 1)

            def key_half(self, b, g, half, hi):
                src = ps[:, half, :].rearrange("p (h c) -> p h c", c=P)
                n = slice(P * (g % 2), P * (g % 2) + P)
                at_hi = kt_hi[:, (g // 2) % 2, 4 * half:4 * half + 4, n]
                at_lo = kt_lo[:, (g // 2) % 2, 4 * half:4 * half + 4, n]
                if hi:
                    return nc.scalar.copy(at_hi, src)
                return nc.vector.tensor_tensor(at_lo, src, at_hi.bitcast(F32), ALU.subtract)

            def act_key(self, act, b, g):
                for half in range(2):
                    if g % 2 == 0 and half == 0:
                        act.wait_ge(self.scored, 4 * b + g // 2 + 1)
                    act.wait_ge(self.k_half, 16 * b + 2 * g + half + 9)
                    self.key_half(b, g, half, True).then_inc(self.kT_hi, 1)

            def dve_key(self, dve, b, g):
                for half in range(2):
                    dve.wait_ge(self.kT_hi, 16 * b + 2 * g + half + 1)
                    self.key_half(b, g, half, False).then_inc(self.kT_lo, 1)

            def act_value(self, act, b, g):
                act.wait_ge(self.v_landed[g % 4], 32 * b + 16 * (g // 4) + 16)
                act.wait_ge(self.pv, PAGES * b + g + 1)
                nc.scalar.copy(vp_hi[:, g % 2], v_page[:, g % 4]).then_inc(self.v_hi, 1)

            def dve_value(self, dve, b, g):
                dve.wait_ge(self.v_hi, PAGES * b + g + 1)
                nc.vector.tensor_tensor(vp_lo[:, g % 2], v_page[:, g % 4], vp_hi[:, g % 2].bitcast(F32), ALU.subtract
                                        ).then_inc(self.v_lo, 1)

            def p_parts(self):
                return ((ps[:, 5, :].rearrange("p (g c) -> p g c", c=ROWS), pT[:, 0:PAGES, 0:ROWS],
                         pT[:, 0:PAGES, ROWS:P]),
                        (ps[0:NS, 4, NS:NS + ROWS].unsqueeze(1), pT[0:NS, PAGES:PAGES + 1, 0:ROWS],
                         pT[0:NS, PAGES:PAGES + 1, ROWS:P]))

            def act_setup_early(self, act):
                nc.scalar.copy(qs_hi[:], qaT[:, :, SEQ:T]).then_inc(self.qk_hi, 1)
                nc.scalar.copy(kn_hi[:], kaT[:, :, SEQ:T]).then_inc(self.qk_hi, 1)

            def act_setup(self, act):
                nc.scalar.copy(ident_r[0:ROWS], ident[0:ROWS]).then_inc(self.setup, 1)
                act.wait_ge(dec_const, 48)
                nc.scalar.copy(bias_r[0:ROWS], bias_stage[0:ROWS]).then_inc(self.setup, 1)
                act.wait_ge(v_stored, 32)
                nc.scalar.copy(vn_hi[0:NS], v_nat_s[0:NS]).then_inc(self.vn_hi, 1)

            def act_queries(self, act, b):
                act.wait_ge(self.scored, 4 * b + 2)
                act.wait_ge(self.setup, 5)
                for src, first in ((qs_hi, 0), (qs_lo, ROWS)):
                    cols = q_stat[:, first:first + HA * (P + 8)].rearrange("p (h c) -> p h c", c=P + 8)
                    for m in range(2):
                        r = slice(DH * m, DH * m + DH)
                        nc.scalar.copy(cols[r, :, TDEC * m:TDEC * m + TDEC], src[r, :, bass.ds(TDEC * b, TDEC)]
                                       ).then_inc(self.q_built, 1)

            def act_low_rows(self, act, b):
                act.wait_ge(self.scored, 4 * b + 6)
                act.wait_ge(self.p_turned, b + 1)
                nc.scalar.copy(p_s[0:ROWS], score_ps(ROWS)).then_inc(self.s_low, 1)

            def act_exp(self, act, b):
                act.wait_ge(self.s_min, b + 2)
                nc.scalar.activation(p_s[0:ROWS], p_s[0:ROWS], ACT.Exp, bias=nmax[0:ROWS, 0:1], scale=-1.0,
                                     accum_out=rsum[0:ROWS, 0:1]).then_inc(self.exped, 1)

            def act_p(self, act, b):
                act.wait_ge(self.p_turned, b + 2)
                act.wait_ge(self.o_done, b + 1)
                for src, hi, _ in self.p_parts():
                    nc.scalar.copy(hi, src).then_inc(self.pT_hi, 1)

            def act_keep(self, act, b):
                act.wait_ge(self.o_done, b + 2)
                act.wait_ge(self.merged, b + 1)
                nc.scalar.copy(o_rows[:], ps[:, 6:8, :].rearrange("p a b -> p (a b)")).then_inc(self.o_kept, 1)

            def act_step(self, act, b, past=True, older=True):
                self.act_key(act, b, 0)
                if past:
                    self.act_exp(act, b - 1)
                self.act_key(act, b, 1)
                if past:
                    self.act_value(act, b - 1, 0)
                    self.act_p(act, b - 1)
                self.act_queries(act, b)
                if older:
                    self.act_keep(act, b - 2)
                for g in range(2, PAGES, 2):
                    self.act_key(act, b, g)
                    if past and g == 2:
                        self.act_value(act, b - 1, 1)
                    self.act_key(act, b, g + 1)
                    if past:
                        self.act_value(act, b - 1, g)
                        self.act_value(act, b - 1, g + 1)
                self.act_low_rows(act, b)

            def act_part(self, act):
                self.act_step(act, 0, past=False, older=False)
                self.act_step(act, 1, older=False)
                with act.Fori(2, DEC) as b:
                    self.act_step(act, b)
                self.act_exp(act, DEC - 1)
                self.act_keep(act, DEC - 2)
                self.act_p(act, DEC - 1)
                for g in range(PAGES):
                    self.act_value(act, DEC - 1, g)
                    if g < 4:
                        if g == 0:
                            act.wait_ge(self.scored, 4 * DEC + 2)
                        split_x.act_pair(act, g)
                self.act_keep(act, DEC - 1)

            def dve_setup_early(self, dve):
                dve.wait_ge(self.qk_hi, 1)
                nc.vector.tensor_tensor(qs_lo[:], qaT[:, :, SEQ:T], qs_hi[:].bitcast(F32), ALU.subtract
                                        ).then_inc(self.qk_lo, 1)
                dve.wait_ge(self.qk_hi, 2)
                nc.vector.tensor_tensor(kn_lo[:], kaT[:, :, SEQ:T], kn_hi[:].bitcast(F32), ALU.subtract
                                        ).then_inc(self.qk_lo, 1)

            def dve_setup(self, dve):
                nc.vector.memset(q_stat[:].bitcast(F32), 0.0).then_inc(self.setup, 1)
                nc.vector.memset(p_s[ROWS:P, 0:P], 0.0).then_inc(self.setup, 1)
                dve.wait_ge(dec_const, 48)
                nc.vector.scalar_tensor_tensor(map_signs[:], minus_second[:], lamv[:, 1:2], minus_first[:],
                                               ALU.mult, ALU.subtract).then_inc(self.setup, 1)
                dve.wait_ge(self.vn_hi, 1)
                nc.vector.tensor_tensor(vn_lo[0:NS], v_nat_s[0:NS], vn_hi[0:NS].bitcast(F32), ALU.subtract
                                        ).then_inc(self.vn_lo, 1)

            def dve_min(self, dve, b):
                dve.wait_ge(self.s_low, b + 1)
                nc.vector.memset(rsum[0:ROWS, 0:1], 0.0)
                nc.vector.tensor_tensor_reduce(p_s[0:ROWS], score_ps(0), p_s[0:ROWS], -DH ** -0.5, -MASKED,
                                               ALU.add, ALU.min, nmax[0:ROWS, 0:1]).then_inc(self.s_min, 1)

            def dve_p(self, dve, b):
                dve.wait_ge(self.pT_hi, 2 * b + 2)
                for src, hi, lo in self.p_parts():
                    nc.vector.tensor_tensor(lo, src, hi.bitcast(F32), ALU.subtract).then_inc(self.pT_lo, 1)

            def dve_weigh(self, dve, b):
                dve.wait_ge(self.exped, b + 1)
                nc.vector.reciprocal(rr[0:ROWS, 0:1], rsum[0:ROWS, 0:1]).then_inc(self.coef, 1)
                dve.wait_ge(self.coef, 2 * b + 1)
                nc.vector.tensor_copy(rr[ROWS:P, 0:1], rr[0:ROWS, 0:1]).then_inc(self.coef, 1)
                dve.wait_ge(self.coef, 2 * b + 2)
                dve.wait_ge(self.merged, b + 1)
                nc.vector.tensor_scalar(weights[:], map_signs[:], rr[:, 0:1], None, ALU.mult
                                        ).then_inc(self.weighed, 1)

            def dve_step(self, dve, b, past=True):
                self.dve_key(dve, b, 0)
                self.dve_key(dve, b, 1)
                if past:
                    self.dve_value(dve, b - 1, 0)
                    self.dve_p(dve, b - 1)
                for g in range(2, PAGES, 2):
                    self.dve_key(dve, b, g)
                    if past and g == 2:
                        self.dve_value(dve, b - 1, 1)
                    self.dve_key(dve, b, g + 1)
                    if past and g == 2:
                        self.dve_weigh(dve, b - 1)
                    if past:
                        self.dve_value(dve, b - 1, g)
                        self.dve_value(dve, b - 1, g + 1)
                self.dve_min(dve, b)

            def dve_part(self, dve):
                self.dve_step(dve, 0, past=False)
                with dve.Fori(1, DEC) as b:
                    self.dve_step(dve, b)
                self.dve_p(dve, DEC - 1)
                self.dve_weigh(dve, DEC - 1)
                for g in range(PAGES):
                    self.dve_value(dve, DEC - 1, g)
                    if g < 4:
                        split_x.dve_pair(dve, g)

            def dve_finish(self, dve):
                dve.wait_ge(self.merged, DEC + 1)
                nc.vector.tensor_copy(dec_o[:, 0], ps[:, 4, 256:512]).then_inc(self.fin, 1)
                dve.wait_ge(self.fin, 1)
                nc.vector.tensor_tensor(dec_o[:, 1], dec_o[:, 0], dec_o[:, 0], ALU.mult).then_inc(self.fin, 1)
                dve.wait_ge(self.fin_ss, 1)
                nc.vector.tensor_scalar(dec_l[:, 0], ps[:, 7, 0:256], 1.0 / DV, EPS, ALU.mult, ALU.add
                                        ).then_inc(self.fin, 1)
                dve.wait_ge(self.fin_sd, 1)
                nc.vector.reciprocal(dec_l[:, 0], dec_l[:, 1]).then_inc(self.fin, 1)
                dve.wait_ge(self.fin, 4)
                nc.vector.tensor_tensor(dec_o[:, 1], dec_o[:, 0], dec_l[:, 0], ALU.mult).then_inc(self.fin, 1)
                dve.wait_ge(self.fin, 5)
                nc.vector.tensor_scalar(oaT[:, :, SEQ:T].rearrange("p h (b t) -> p h b t", t=TDEC),
                                        dec_o[:, 1].rearrange("p (b h t) -> p h b t", h=HA, t=TDEC),
                                        subln8[:, 0:1], None, ALU.mult).then_inc(self.oa_set, 1)

            def pe_finish(self, pe):
                pe.wait_ge(self.fin, 2)
                nc.tensor.matmul(ps[:, 7, 0:256], ones[:], dec_o[:, 1], start=True, stop=True).then_inc(self.fin_ss, 1)

            def act_finish(self, act):
                act.wait_ge(self.fin, 3)
                nc.scalar.activation(dec_l[:, 1], dec_l[:, 0], ACT.Sqrt).then_inc(self.fin_sd, 1)

            def credits_pe(self, pe):
                pe.sem_inc(self.k_half, 8)
                pe.sem_inc(self.scored, 2)
                pe.sem_inc(self.p_turned, 1)
                pe.sem_inc(self.pv, 2)
                pe.sem_inc(self.o_done, 1)
                pe.sem_inc(self.merged, 1)

            def credits_dve(self, dve):
                dve.sem_inc(self.kT_lo, 2)
                dve.sem_inc(self.s_min, 1)
                dve.sem_inc(self.pT_lo, 2)
                dve.sem_inc(self.v_lo, 4)

            def credits_act(self, act):
                act.sem_inc(self.o_kept, 1)

        class Retention:
            def __init__(self):
                self.scored = sem("rt_scored")
                self.sc_set = sem("rt_sc_set")
                self.qx_set = sem("rt_qx_set")
                self.kw_set = sem("rt_kw_set")
                self.out = sem("rt_out")
                self.o_kept = sem("rt_o_kept")
                self.kv = sem("rt_kv")
                self.st_set = sem("rt_st_set")
                self.st_stored = sem("rt_st_stored")
                self.s_scored = sem("rs_scored")
                self.s_sc_set = sem("rs_sc_set")
                self.s_in = [sem(f"rs_in{j}") for j in range(4)]
                self.s_qm_zero = sem("rs_qm_zero")
                self.s_qm = sem("rs_qm")
                self.s_kw = sem("rs_kw")
                self.s_cross = sem("rs_cross")
                self.s_kv = sem("rs_kv")
                self.s_new = sem("rs_new")
                self.s_stored = [sem(f"rs_stored{j}") for j in range(2)]
                self.s_kept = sem("rs_kept")

            def chunk(self, c):
                return slice(c * P, c * P + P)

            def pe_part(self, pe):
                def scores(c):
                    if c >= 2:
                        pe.wait_ge(self.sc_set, c - 1)
                    for h in range(HR):
                        mm = nc.tensor.matmul(ps[:, c % 2, h * P:h * P + P], krT[:, h, self.chunk(c)],
                                              qrT[:, h, self.chunk(c)], start=True, stop=True)
                    mm.then_inc(self.scored, 1)

                def keys_values(c):
                    pe.wait_ge(self.kw_set, c + 1)
                    if c:
                        pe.wait_ge(self.st_set, HR * c)
                    for h in range(HR):
                        mm = nc.tensor.matmul(ps[:, 4 + h // 2, (h % 2) * RV:(h % 2) * RV + RV],
                                              kr_nat[:, c, h * RK:h * RK + RK], vr_nat[:, c, h * RV:h * RV + RV],
                                              start=True, stop=True)
                    mm.then_inc(self.kv, 1)

                def output(c):
                    pe.wait_ge(self.sc_set, c + 1)
                    if c:
                        pe.wait_ge(self.qx_set, c)
                        pe.wait_ge(self.st_set, HR * c)
                    if c >= 2:
                        pe.wait_ge(self.o_kept, c - 1)
                    for h in range(HR):
                        dst = ps[:, (6 if c % 2 else 2) + h // 2, (h % 2) * RV:(h % 2) * RV + RV]
                        mm = nc.tensor.matmul(dst, scT[:, c % 2, h * P:h * P + P], vr_nat[:, c, h * RV:h * RV + RV],
                                              start=True, stop=c == 0)
                        if c:
                            mm = nc.tensor.matmul(dst, qx[:, c % 2, h], state[:, c % 2, h * RV:h * RV + RV],
                                                  start=False, stop=True)
                    mm.then_inc(self.out, 1)

                scores(0)
                for c in range(NB):
                    if c + 1 < NB:
                        scores(c + 1)
                    if c == 0:
                        rv.all_stored(pe)
                    keys_values(c)
                    output(c)
                pe.wait_ge(self.sc_set, NB)
                for h in range(HR):
                    mm = nc.tensor.matmul(ps[0:NS, 0, h * NS:h * NS + NS], krT[:, h, SEQ:T], qrT[:, h, SEQ:T],
                                          start=True, stop=True)
                mm.then_inc(self.s_scored, 1)
                pe.wait_ge(self.s_sc_set, 1)
                pe.wait_ge(self.o_kept, NB)
                pe.wait_ge(self.st_set, HR * NB)
                for h in range(HR):
                    nc.tensor.matmul(ps[0:NS, 2 + h // 2, (h % 2) * RV:(h % 2) * RV + RV],
                                     scT[0:NS, 0, h * NS:h * NS + NS], vr_nat_s[0:NS, h * RV:h * RV + RV],
                                     start=h % 2 == 0, stop=False, skip_group_check=True)
                pe.wait_ge(self.s_qm, DEC)
                for b in range(DEC):
                    pe.wait_ge(self.s_in[b % 4], 16 * (b // 4) + 16)
                    for h in range(HR):
                        mm = nc.tensor.matmul(ps[0:NS, 2 + h // 2, (h % 2) * RV:(h % 2) * RV + RV], qm[:, b, h],
                                              st_in[:, b % 4, h * RV:h * RV + RV], start=False,
                                              stop=b == DEC - 1, skip_group_check=True)
                    mm.then_inc(self.s_cross, 1)
                    pe.wait_ge(self.s_kw, b + 1)
                    if b >= 2:
                        pe.wait_ge(self.s_new, HR * (b - 1))
                    for h in range(HR):
                        mm = nc.tensor.matmul(ps[:, (6 if b % 2 else 4) + h // 2, (h % 2) * RV:(h % 2) * RV + RV],
                                              kw_s[0:NS, b % 2, h * RK:h * RK + RK],
                                              vr_nat_s[0:NS, h * RV:h * RV + RV], start=True, stop=True)
                    mm.then_inc(self.s_kv, 1)

            def dve_part(self, dve):
                def weigh(c):
                    dve.wait_ge(self.scored, c + 1)
                    if c >= 2:
                        dve.wait_ge(self.out, c - 1)
                    nc.vector.tensor_tensor(scT[:, c % 2], ps[:, c % 2, :], decay[:].rearrange("p h i -> p (h i)"),
                                            ALU.mult).then_inc(self.sc_set, 1)

                def advance(c):
                    dve.wait_ge(self.kv, c + 1)
                    if c >= 1:
                        dve.wait_ge(self.st_set, HR * c)
                        dve.wait_ge(self.out, c)
                    for h in range(HR):
                        e = slice(h * RV, h * RV + RV)
                        src = ps[:, 4 + h // 2, (h % 2) * RV:(h % 2) * RV + RV]
                        if c == 0:
                            ins = nc.vector.tensor_copy(state[:, 1, e], src)
                        else:
                            ins = nc.vector.scalar_tensor_tensor(state[:, (c + 1) % 2, e], state[:, c % 2, e],
                                                                 gamma[h] ** P, src, ALU.mult, ALU.add)
                        ins.then_inc(self.st_set, 1)

                weigh(0)
                for c in range(NB):
                    if c + 1 < NB:
                        weigh(c + 1)
                    advance(c)
                dve.wait_ge(self.s_scored, 1)
                dve.wait_ge(self.out, NB)
                nc.vector.tensor_tensor(scT[0:NS, 0, 0:HR * NS], ps[0:NS, 0, 0:HR * NS],
                                        decay_s[0:NS].rearrange("p h i -> p (h i)"), ALU.mult).then_inc(self.s_sc_set, 1)
                for b in range(DEC):
                    dve.wait_ge(self.s_kv, b + 1)
                    dve.wait_ge(self.s_in[b % 4], 16 * (b // 4) + 16)
                    if b >= 2:
                        dve.wait_ge(self.s_stored[b % 2], 16 * (b // 2))
                    for h in range(HR):
                        e = slice(h * RV, h * RV + RV)
                        nc.vector.scalar_tensor_tensor(st_out[:, b % 2, e], st_in[:, b % 4, e], gamma[h] ** TDEC,
                                                       ps[:, (6 if b % 2 else 4) + h // 2,
                                                          (h % 2) * RV:(h % 2) * RV + RV],
                                                       ALU.mult, ALU.add).then_inc(self.s_new, 1)

            def act_part(self, act):
                for c in range(NB):
                    act.wait_ge(self.out, c + 1)
                    b = 6 if c % 2 else 2
                    nc.scalar.copy(or_nat[:, c], ps[:, b:b + 2, :].rearrange("p a b -> p (a b)")
                                   ).then_inc(self.o_kept, 1)
                act.wait_ge(self.s_cross, DEC)
                act.wait_ge(self.s_kv, DEC)
                nc.scalar.copy(or_s[0:NS], ps[0:NS, 2:4, :].rearrange("p a b -> p (a b)")).then_inc(self.s_kept, 1)

            def pool_part(self, pool):
                for c in range(NB):
                    rows = kr_nat[:, c].rearrange("p (h d) -> p h d", d=RK)
                    nc.gpsimd.tensor_tensor(rows, rows, kdec[:].unsqueeze(2).broadcast_to([P, HR, RK]), ALU.mult
                                            ).then_inc(self.kw_set, 1)
                    if c:
                        if c >= 2:
                            pool.wait_ge(self.out, c - 1)
                        nc.gpsimd.tensor_tensor(qx[:, c % 2], qrT[:, :, self.chunk(c)], cross[:], ALU.mult
                                                ).then_inc(self.qx_set, 1)
                pool.wait_ge(self.out, NB)
                nc.gpsimd.memset(qm[:], 0.0).then_inc(self.s_qm_zero, 1)
                pool.wait_ge(self.s_qm_zero, 1)
                for b in range(DEC):
                    a = TDEC * b
                    nc.gpsimd.tensor_tensor(qm[:, b, :, a:a + TDEC], qrT[:, :, SEQ + a:SEQ + a + TDEC],
                                            cross[:, :, 0:TDEC], ALU.mult).then_inc(self.s_qm, 1)
                for b in range(DEC):
                    if b >= 2:
                        pool.wait_ge(self.s_kv, b - 1)
                    nc.gpsimd.tensor_tensor(kw_s[0:NS, b % 2].rearrange("p (h d) -> p h d", d=RK),
                                            kr_nat_s[0:NS].rearrange("p (h d) -> p h d", d=RK),
                                            kdec_s[0:NS, HR * b:HR * b + HR].unsqueeze(2).broadcast_to([NS, HR, RK]),
                                            ALU.mult).then_inc(self.s_kw, 1)

            def sp_part(self, sp):
                sp.wait_ge(self.st_set, HR * NB)
                sp.dma_start(ret_state_prompt[0, 0].rearrange("h d e -> d h e"),
                             state[:, 0].rearrange("p (h e) -> p h e", e=RV)).then_inc(out_stored, 16)
                sp.wait_ge(self.out, NB)

                def load(b):
                    sp.dma_start(st_in[:, b % 4].rearrange("p (h e) -> p h e", e=RV),
                                 state_ret[0, b].rearrange("h d e -> d h e")).then_inc(self.s_in[b % 4], 16)
                for b in range(4):
                    load(b)
                for b in range(DEC):
                    sp.wait_ge(self.s_new, HR * (b + 1))
                    sp.dma_start(ret_state_sample[0, b].rearrange("h d e -> d h e"),
                                 st_out[:, b % 2].rearrange("p (h e) -> p h e", e=RV)).then_inc(self.s_stored[b % 2], 16)
                    if b + 4 < DEC:
                        sp.wait_ge(self.s_cross, b + 1)
                        load(b + 4)

        class RetGate:
            def __init__(self, c):
                self.c = c
                self.silu_done = sem("rg_silu_done")
                self.prod_done = sem("rg_prod_done")
                self.o_hi, self.o_lo = sem("rg_o_hi"), sem("rg_o_lo")

            def loads(self, sp, first, last):
                for i in range(first, last):
                    for j in range(2):
                        load_chunk(sp, self.c + 2 * i + j, self.c // 2 + i, j,
                                   w_in, W_IN_COLS["gr"] + 512 * i + 256 * j)

            def pe_tiles(self, pe, first, last):
                for u in range(first, last):
                    if u % 2 == 0:
                        chunk_ready(pe, self.c + u // 2)
                    pe.wait_ge(self.silu_done, u + 1)
                    gemm(4 + 2 * (u % 2), (u // 2) % 2, u % 2, KD, xh, xl)

            def act_silu(self, act, u):
                tile_done(act, self.c + u // 2, u % 2)
                act.wait_ge(self.prod_done, u + 1)
                nc.scalar.activation(halves(gated[:, u % 2]), banks(4 + 2 * (u % 2)), ACT.Silu
                                     ).then_inc(self.silu_done, 1)

            def act_part(self, act):
                for u in range(KD):
                    act.wait_ge(self.prod_done, u + 3)
                    nc.scalar.copy(obh[:, u], prod[:, u % 2]).then_inc(self.o_hi, 1)
                    if u % 2:
                        c = self.c + u // 2 + 2
                        split_hi(act, c, c // 2, c % 2)
                    if u + 2 < KD:
                        self.act_silu(act, u + 2)

            def dve_part(self, dve):
                with dve.Fori(0, 2) as i:
                    for t in range(4):
                        u, c = 4 * i + t, self.c + 2 * i + t // 2
                        k, s = bass.ds(u, 1), slice(t % 2, t % 2 + 1)
                        dve.wait_ge(self.silu_done, u + 3)
                        nc.vector.tensor_tensor(prod[:, s], gated[:, s], onT[:, k], ALU.mult).then_inc(self.prod_done, 1)
                        dve.wait_ge(self.o_hi, u + 1)
                        nc.vector.tensor_tensor(obl[:, k], prod[:, s], obh[:, k].bitcast(F32), ALU.subtract
                                                ).then_inc(self.o_lo, 1)
                        if t % 2 == 1:
                            split_lo(dve, c + 2, t // 2)

        class OutProject:
            def __init__(self, c):
                self.c = c
                self.resid = sem("op_resid")

            def loads(self, sp):
                for i in range(2):
                    for j in range(2):
                        load_chunk(sp, self.c + 2 * i + j, self.c // 2 + i, j,
                                   w_out, 512 * i + 256 * j)

            def pe_part(self, pe):
                with pe.Fori(0, 2) as i:
                    for t in range(4):
                        if t % 2 == 0:
                            chunk_ready(pe, self.c + 2 * i + t // 2)
                        pe.wait_ge(self.resid, 4 * i + t + 1)
                        gemm(2 * t, t // 2, t % 2, KD, mh, ml,
                             tile_ready=None if t else lambda k: pe.wait_ge(branch_b.m_lo, k + 1))

            def act_part(self, act):
                with act.Fori(0, 2) as i:
                    for j in range(2):
                        split_hi(act, self.c + 2 * i + j + 2, self.c // 2 + i + 1, j)

            def dve_part(self, dve):
                dve.wait_ge(branch_b.m_lo, KD)
                ln2.dve_clear(dve)
                with dve.Fori(0, 2) as i:
                    for t in range(4):
                        c = self.c + 2 * i + t // 2
                        k = bass.ds(4 * i + t, 1)
                        tile_done(dve, c, t % 2)
                        xk = xT[:, k].rearrange("p o (a b) -> p (o a) b", b=HALF)
                        nc.vector.scalar_tensor_tensor(xk, banks(2 * t), 1.0 / ALPHA, xk, ALU.mult, ALU.add
                                                       ).then_inc(self.resid, 1)
                        dve.wait_ge(self.resid, 4 * i + t + 5)
                        ln2.dve_add(dve, 4 * i + t, xT[:, k].rearrange("p o t -> p (o t)"))
                        if t % 2 == 1:
                            split_lo(dve, c + 2, t // 2)

        x_landed = [sem(f"x_landed{t}") for t in range(5)]
        turn_in = Norm(0, 0, 0, stats=False)
        turn_in.row_ready = lambda pe, t: pe.wait_ge(x_landed[t], 16)
        ffn1 = FFN(0, C_FFN1_UP, ffn1_w_gu, ffn1_w_down)
        ln1 = ChannelNorm(0)
        pk = Project(C_KA, 4, stage=turned, nat=k_nat, nat_s=k_nat_s, keep=kaT)
        pv = Project(C_VA, 4, stage=turned, nat=v_nat, nat_s=v_nat_s)
        pq = Project(C_QA, 4, direct=qaT)
        attn = PromptAttention()
        attn_norm = HeadNorm(0, 0, [(o_nat[:, b], P * b, P) for b in range(NB)], sq, DV)
        dec = DecodeAttention()
        split_oa = Split(1, oaT, oah, oal)
        split_x = Split(0, xT, xh, xl)
        branch_a = Branch(C_BRANCH_A, W_IN_COLS["ga"], w_branch_a, oah, oal, add=False)
        rq = Project(C_QR, 2, direct=qrT)
        rk = Project(C_KR, 2, stage=rturned, nat=kr_nat, nat_s=kr_nat_s, keep=krT, scale=RK ** -0.5)
        rv = Project(C_VR, 4, stage=rturned, nat=vr_nat, nat_s=vr_nat_s)
        ret = Retention()
        ret_norm = HeadNorm(NB, 1, [(or_nat[:, b], P * b, P) for b in range(NB)] + [(or_s[0:NS], SEQ, NS)], rsq, RV)
        ret_gate = RetGate(C_GR)
        branch_b = Branch(C_BRANCH_B, W_IN_COLS["gb"], w_branch_b, obh, obl, add=True)
        out_proj = OutProject(C_OUT)
        ln2 = ChannelNorm(1)
        ffn2 = FFN(1, C_FFN2_UP, ffn2_w_gu, ffn2_w_down, last=True)
        ln3 = Norm(2, 0, 1, back=False)

        att_const = sem("att_const")
        dec_const = sem("dec_const")
        ret_const = sem("ret_const")
        lam_sums, lam_exp, lam_set, subln_set = sem("lam_sums"), sem("lam_exp"), sem("lam_set"), sem("subln_set")
        guard_set = sem("guard_set")
        cols_turned, cols_set = sem("cols_turned"), sem("cols_set")
        k_stored, v_stored = sem("k_stored"), sem("v_stored")
        START_LOADS = 11

        block = ctx.enter_context(nc.Block())

        def const_load(eng, dst, name, signal, rows=P):
            a, n = const_at[name]
            eng.dma_start(dst, const[0:rows, a:a + n]).then_inc(signal, 16)

        def flat(t):
            return t.rearrange("p a b -> p (a b)")

        @block.sync
        def _(sp):
            for t, (t0, n) in enumerate(TOKENS):
                src = x_prompt[0, t0:t0 + n, :] if t < NB else x_sample.rearrange("b t d -> (b t) d")
                sp.dma_start(xn[0:n, t], src).then_inc(x_landed[t], 16)
                if t == 0:
                    const_load(sp, ident[:], "ident", const_landed)
            const_load(sp, ones[:], "ones", const_landed)
            const_load(sp, slope8[:], "slope8", const_landed)
            const_load(sp, map_rows[:], "map_rows", const_landed)
            const_load(sp, kdec[:], "kdec", const_landed)
            const_load(sp, kdec_s[:], "kdec_s", const_landed)
            sp.dma_start(lam_in[:], da_lambda[0:1].broadcast_to([P, 4, DH])).then_inc(const_landed, 16)
            sp.dma_start(subln[:], da_subln_g.rearrange("o d -> d o")).then_inc(const_landed, 16)
            sp.dma_start(pages[0:1], page_table.rearrange("b g -> (b g)").unsqueeze(0)).then_inc(const_landed, 16)
            for j, src in ((0, ln_g), (1, ln_b)):
                sp.dma_start(ln_rows[2 * KD * j:2 * KD * j + 2 * KD],
                             src[0, 0:2, :].rearrange("i (k p) -> (i k) p", p=P)).then_inc(const_landed, 16)
            ffn1.loads(sp)
            const_load(sp, dist[:], "dist", att_const)
            pk.loads(sp, W_IN_COLS["ka"])
            pv.loads(sp, W_IN_COLS["va"])
            pq.loads(sp, W_IN_COLS["qa"])
            branch_a.loads(sp, 0, 1)
            sp.wait_ge(gemm_done, 2 * C_BRANCH_A + 4)
            const_load(sp, minus_first[:], "minus_first", dec_const)
            const_load(sp, minus_second[:], "minus_second", dec_const)
            sp.wait_ge(attn.combined, HA * NB + 2)
            const_load(sp, bias_stage[0:ROWS], "bias_dec", dec_const, ROWS)
            sp.wait_ge(attn.scored, HA * NB + 2)
            dec.sp_part(sp)
            branch_a.loads(sp, 1, KD // 2)
            rq.loads(sp, W_IN_COLS["qr"])
            sp.wait_ge(branch_a.prod_done, KD + 2)
            const_load(sp, flat(decay[:]), "decay", ret_const)
            const_load(sp, flat(cross[:]), "cross", ret_const)
            const_load(sp, flat(decay_s[0:NS]), "decay_s", ret_const, NS)
            rk.loads(sp, W_IN_COLS["kr"])
            rv.loads(sp, W_IN_COLS["vr"])
            ret_gate.loads(sp, 0, 1)
            ret.sp_part(sp)
            ret_gate.loads(sp, 1, 2)
            branch_b.loads(sp, 0, KD // 2)
            out_proj.loads(sp)
            ffn2.loads(sp)
            ffn2.hidden(sp)
            ln3.load_params(sp)
            for t, (t0, n) in enumerate(TOKENS):
                sp.wait_ge(ln3.biased, ln3.s + t + 1)
                dst = y_prompt[0, t0:t0 + n, :] if t < NB else y_sample.rearrange("b t d -> (b t) d")
                sp.dma_start(dst, xn[0:n, t]).then_inc(out_stored, 16)
            sp.wait_ge(out_stored, 16 * 6)
            sp.wait_ge(k_stored, 32)
            sp.wait_ge(v_stored, 32)
            for stored in ret.s_stored:
                sp.wait_ge(stored, 8 * DEC)

        @block.scalar
        def _(act):
            act.sem_inc(FFN.silu_done, 2)
            act.sem_inc(Project.taken, 2)
            act.sem_inc(Branch.sig_done, 2)
            act.sem_inc(ret_gate.silu_done, 2)
            act.wait_ge(guard_set, 1)
            turn_in.act_part(act)
            split_hi(act, 1, 0, 1)
            act.wait_ge(lam_sums, 2)
            nc.scalar.activation(lam_t[:, 2:4], lam_t[:, 0:2], ACT.Exp).then_inc(lam_exp, 1)
            ffn1.act_part(act)
            ln1.act_part(act)
            pk.act_part(act)
            pk.all_kept(act)
            pv.act_part(act)
            pq.act_part(act)
            attn.credits_act(act)
            dec.credits_act(act)
            pq.all_taken(act)
            dec.act_setup_early(act)
            act.wait_ge(k_stored, 32)
            attn.act_part(act)
            act.wait_ge(attn.combined, HA * NB + 2)
            act.wait_ge(attn.o_set, HA * NB + 2)
            attn_norm.act_squares(act)
            act.wait_ge(subln_set, 1)
            dec.act_setup(act)
            attn_norm.act_evict(act, oaT, subln8[:, 0:1])
            dec.act_part(act)
            dec.act_finish(act)
            act.wait_ge(v_stored, 32)
            act.wait_ge(dec.oa_set, 1)
            split_oa.act_part(act)
            branch_a.act_part(act)
            rq.act_part(act)
            rk.act_part(act)
            rk.all_kept(act)
            rv.act_part(act)
            ret.act_part(act)
            act.wait_ge(ret.s_kept, 1)
            ret_norm.act_squares(act)
            ret_gate.act_silu(act, 0)
            ret_gate.act_silu(act, 1)
            ret_norm.act_evict(act, onT)
            for stored in ret.s_stored:
                act.wait_ge(stored, 8 * DEC)
            ret_gate.act_part(act)
            branch_b.act_part(act)
            out_proj.act_part(act)
            ln2.act_part(act)
            ffn2.act_part(act)
            ln3.act_part(act)

        @block.vector
        def _(dve):
            dve.sem_inc(lo_split, 2)
            dve.sem_inc(HeadNorm.summed, 2)
            dve.sem_inc(FFN.prod_done, 2)
            dve.sem_inc(FFN.resid, 4)
            dve.sem_inc(Project.stored, 2)
            dve.sem_inc(Branch.prod_done, 2)
            dve.sem_inc(ret_gate.prod_done, 2)
            dve.sem_inc(out_proj.resid, 4)
            nc.vector.memset(guard[:], EPS / ALPHA ** 2).then_inc(guard_set, 1)
            dve.wait_ge(cols_turned, 1)
            nc.vector.tensor_copy(flat(ln_cols[:]), ps[:, 0, 0:4 * KD]).then_inc(cols_set, 1)
            turn_in.dve_part(dve)
            split_lo(dve, 1, 1)
            dve.wait_ge(const_landed, 16 * START_LOADS)
            nc.vector.memset(lamv[:, 0:1], 1.0)
            for j in range(2):
                nc.vector.tensor_tensor_reduce(lam_in[:, 2 * j], lam_in[:, 2 * j], lam_in[:, 2 * j + 1], 1.0, 0.0,
                                               ALU.mult, ALU.add, lam_t[:, j:j + 1]).then_inc(lam_sums, 1)
            nc.vector.tensor_scalar(subln8[:], subln[:], 1.0 - LAM_INIT, None, ALU.mult).then_inc(subln_set, 1)
            dve.wait_ge(lam_exp, 1)
            nc.vector.scalar_tensor_tensor(lamv[:, 1:2], lam_t[:, 2:3], LAM_INIT, lam_t[:, 3:4], ALU.add, ALU.subtract
                                           ).then_inc(lam_set, 1)
            ffn1.dve_part(dve, ln1)
            ln1.dve_part(dve)
            pk.dve_part(dve)
            pv.dve_part(dve)
            pq.dve_part(dve)
            attn.credits_dve(dve)
            dec.credits_dve(dve)
            dec.dve_setup_early(dve)
            dve.wait_ge(k_stored, 32)
            dve.wait_ge(lam_set, 1)
            attn.dve_part(dve)
            attn_norm.dve_scale(dve)
            dec.dve_setup(dve)
            dec.dve_part(dve)
            dec.dve_finish(dve)
            split_oa.dve_part(dve)
            branch_a.dve_part(dve)
            rq.dve_part(dve)
            rk.dve_part(dve)
            rv.dve_part(dve)
            dve.wait_ge(ret_const, 48)
            ret.dve_part(dve)
            ret_norm.dve_scale(dve)
            ret_norm.all_evicted(dve)
            ret_gate.dve_part(dve)
            branch_b.dve_part(dve)
            out_proj.dve_part(dve)
            ln2.dve_part(dve)
            ffn2.dve_part(dve)
            ln3.dve_part(dve)

        @block.tensor
        def _(pe):
            pe.sem_inc(gemm_done, 4)
            pe.sem_inc(ChannelNorm.sq_used, 2)
            attn.credits_pe(pe)
            dec.credits_pe(pe)
            pe.sem_inc(Project.rows, 2)
            pe.wait_ge(const_landed, 16 * START_LOADS)
            nc.tensor.transpose(ps[:, 0, 0:4 * KD], ln_rows[0:4 * KD], ident[0:4 * KD, 0:4 * KD]
                                ).then_inc(cols_turned, 1)
            turn_in.pe_part(pe)
            turn_in.ready(pe)
            pe.wait_ge(cols_set, 1)
            ffn1.pe_part(pe)
            ln1.pe_part(pe)
            pk.pe_part(pe, lambda k: ln1.ready(pe, k))
            pv.pe_part(pe, before=pk)
            pq.pe_part(pe, before=pv)
            pq.all_taken(pe)
            pv.all_stored(pe)
            attn.pe_part(pe)
            attn_norm.pe_part(pe)
            attn_norm.all_evicted(pe)
            pe.wait_ge(attn.aT_set, HA * NB + 2)
            pe.wait_ge(attn.o_set, HA * NB + 2)
            dec.pe_part(pe)
            dec.pe_finish(pe)
            pe.wait_ge(dec.fin, 3)
            branch_a.pe_gate(pe, 0, 1)
            branch_a.pe_part(pe, lambda k: split_oa.ready(pe, k))
            pe.wait_ge(branch_a.sig_done, KD + 2)
            rq.pe_part(pe)
            pe.wait_ge(branch_a.prod_done, KD + 2)
            rk.pe_part(pe)
            rv.pe_part(pe, before=rk)
            rv.turn(pe, rv.tiles - 1)
            rk.all_kept(pe)
            rv.all_taken(pe)
            ret.pe_part(pe)
            pe.wait_ge(ret.s_kept, 1)
            pe.wait_ge(ret.s_new, HR * DEC)
            ret_gate.pe_tiles(pe, 0, 2)
            ret_norm.pe_part(pe)
            ret_gate.pe_tiles(pe, 2, KD)
            ret_norm.all_evicted(pe)
            for n in range(2):
                branch_b.pe_gate(pe, 0, n)
            branch_b.pe_part(pe, lambda k: pe.wait_ge(ret_gate.o_lo, k + 1))
            pe.wait_ge(branch_b.sig_done, 2 * KD + 2)
            out_proj.pe_part(pe)
            ln2.pe_part(pe)
            ffn2.pe_part(pe, lambda k: ln2.ready(pe, k))
            pe.wait_ge(ffn2.resid, 2 * KD + 4)
            ln3.pe_part(pe)

        @block.gpsimd
        def _(pool):
            pool.sem_inc(Project.kept, 2)
            pk.pool_part(pool)
            pk.all_stored(pool)
            pool.dma_start(k_prompt[0, 0].rearrange("(b p) h d -> p b (h d)", p=P), k_nat[:]).then_inc(k_stored, 16)
            pool.dma_start(k_sample[0].rearrange("b t h d -> (b t) (h d)"), k_nat_s[0:NS]).then_inc(k_stored, 16)
            pv.all_stored(pool)
            pool.dma_start(v_prompt[0, 0].rearrange("(b p) h d -> p b (h d)", p=P), v_nat[:]).then_inc(v_stored, 16)
            pool.dma_start(v_sample[0].rearrange("b t h d -> (b t) (h d)"), v_nat_s[0:NS]).then_inc(v_stored, 16)
            pq.all_taken(pool)
            pool.wait_ge(att_const, 16)
            attn.pool_part(pool)
            rk.pool_part(pool)
            rk.all_stored(pool)
            rv.all_stored(pool)
            pool.wait_ge(ret_const, 48)
            ret.pool_part(pool)
            ln3.pool_part(pool)


_INS = ["x_prompt", "x_sample", "cache_k", "cache_v", "state_ret", "page_table", "ln_g", "ln_b", "ffn1_w_gu",
        "ffn1_w_down", "w_in", "da_lambda", "da_subln_g", "w_branch_a", "w_branch_b", "w_out", "ffn2_w_gu",
        "ffn2_w_down"]
_OUTS = [(1, SEQ, D), (DEC, TDEC, D), (1, 1, SEQ, HA, 2 * DH), (1, 1, SEQ, HA, DV), (1, 1, HR, RK, RV),
         (1, DEC, TDEC, HA, 2 * DH), (1, DEC, TDEC, HA, DV), (1, DEC, HR, RK, RV)]


def kernel(**inputs):
    import numpy as _np
    import concourse.bacc as _bacc
    from concourse import mybir as _mybir
    from concourse.bass_utils import run_bass_kernel_spmd as _run

    nc = _bacc.Bacc("TRN2", target_bir_lowering=False, num_devices=1)
    arrays, args = {}, []
    for name in _INS:
        arrays[f"in_{name}_dram"] = _np.ascontiguousarray(inputs[name])
    arrays["in_const_dram"] = constants()[1]
    for name, a in arrays.items():
        args.append(nc.dram_tensor(name, a.shape, _mybir.dt.from_np(a.dtype), kind="ExternalInput").ap())
    for i, shape in enumerate(_OUTS):
        args.append(nc.dram_tensor(f"out_{i}_dram", shape, _mybir.dt.float32, kind="ExternalOutput").ap())
    build(nc, *args)
    r = _run(nc, [arrays], core_ids=[0])
    return tuple(r.results[0][f"out_{i}_dram"] for i in range(len(_OUTS)))
```
